# Optimizing a Trainium2 kernel written in Bass

```python
import jax, jax.numpy as jnp
from jax import lax
import numpy as np

D_MODEL = 1024
BATCH = 1
SEQ = 256
DEPTH = 2
DEC_BATCH = 8
DEC_SEQ = 16
PAST_LEN = 256

CHUNK = 64
N_HEADS = 16
HEAD_DIM = D_MODEL // N_HEADS
D_FF = 2816
CONV_K = 31
N_A = DEPTH // 2
N_B = DEPTH - N_A
N_SUB = 3
ALPHA = float((2 * DEPTH) ** 0.25)
BETA = float((8 * DEPTH) ** -0.25)
Q_BLOCK = 128
LN_EPS = 1e-5

kernel_name = 'yoco_conformer_fox_stream_step'

def _layer_norm(x, g, b):
    xf = x.astype(jnp.float32)
    mu = jnp.mean(xf, axis=-1, keepdims=True)
    var = jnp.mean(jnp.square(xf - mu), axis=-1, keepdims=True)
    y = (xf - mu) * lax.rsqrt(var + LN_EPS) * g.astype(jnp.float32) + b.astype(jnp.float32)
    return y.astype(x.dtype)

def _modulate(x, shift, scale):
    return x * (1 + scale[:, None, :]) + shift[:, None, :]

def _swiglu(h, w_gate, w_up, w_down):
    return (jax.nn.silu(h @ w_gate) * (h @ w_up)) @ w_down

def _conv_module(h, prev, pw1_w, pw1_b, dw_w, dw_b, cln_g, cln_b, pw2_w, pw2_b):
    u = h @ pw1_w + pw1_b
    u = u[..., :D_MODEL] * jax.nn.sigmoid(u[..., D_MODEL:])
    u_full = jnp.concatenate([prev.astype(u.dtype), u], axis=1)
    z = lax.conv_general_dilated(
        u_full, dw_w.astype(u.dtype)[:, None, :], window_strides=(1,), padding='VALID',
        dimension_numbers=('NWC', 'WIO', 'NWC'), feature_group_count=D_MODEL) + dw_b
    z = jax.nn.silu(_layer_norm(z, cln_g, cln_b))
    return z @ pw2_w + pw2_b, u_full[:, -(CONV_K - 1):]

def _fox_attention(q, k, v, logf):
    tq, tk = q.shape[1], k.shape[1]
    off = tk - tq
    cum = jnp.cumsum(logf.astype(jnp.float32), axis=1).transpose(0, 2, 1)
    qb = min(Q_BLOCK, tq)
    scale = HEAD_DIM ** -0.5
    outs = []
    for start in range(0, tq, qb):
        stop = min(start + qb, tq)
        kend = off + stop
        s = jnp.einsum('bqhd,bkhd->bhqk', q[:, start:stop], k[:, :kend]).astype(jnp.float32) * scale
        bias = cum[:, :, off + start:off + stop, None] - cum[:, :, None, :kend]
        qpos = off + start + jnp.arange(stop - start)
        kpos = jnp.arange(kend)
        mask = kpos[None, :] <= qpos[:, None]
        p = jax.nn.softmax(jnp.where(mask, s + bias, -jnp.inf), axis=-1)
        outs.append(jnp.einsum('bhqk,bkhd->bqhd', p.astype(v.dtype), v[:, :kend]))
    return jnp.concatenate(outs, axis=1)

def _trunk(x, c, conv_prev, kv_cache, w_ada, b_ada, ln_g, ln_b, ffn_w_gate, ffn_w_up, ffn_w_down,
           pw1_w, pw1_b, dw_w, dw_b, conv_ln_g, conv_ln_b, pw2_w, pw2_b,
           w_ada_kv, b_ada_kv, w_k, w_v, w_f, b_f, w_q, w_o):
    bsz, t, _ = x.shape
    c_act = jax.nn.silu(c)
    new_conv = []
    for l in range(DEPTH):
        if l == N_A:
            shift_kv, scale_kv = jnp.split(c_act @ w_ada_kv + b_ada_kv, 2, axis=-1)
            h_kv = _modulate(x, shift_kv, scale_kv)
            k_new = (h_kv @ w_k).reshape(bsz, t, N_HEADS, HEAD_DIM)
            v_new = (h_kv @ w_v).reshape(bsz, t, N_HEADS, HEAD_DIM)
            logf_new = jax.nn.log_sigmoid((h_kv @ w_f + b_f).astype(jnp.float32))
            if kv_cache is None:
                k_all, v_all, logf_all = k_new, v_new, logf_new
            else:
                ck, cv, clf = kv_cache
                k_all = jnp.concatenate([ck.astype(k_new.dtype), k_new], axis=1)
                v_all = jnp.concatenate([cv.astype(v_new.dtype), v_new], axis=1)
                logf_all = jnp.concatenate([clf.astype(jnp.float32), logf_new], axis=1)
        mods = (c_act @ w_ada[l] + b_ada[l]).reshape(bsz, N_SUB, 3, D_MODEL)
        shift, scale, gate = mods[:, :, 0], mods[:, :, 1], 1 + mods[:, :, 2]
        h = _modulate(x, shift[:, 0], scale[:, 0])
        f1 = _swiglu(h, ffn_w_gate[l, 0], ffn_w_up[l, 0], ffn_w_down[l, 0])
        x = _layer_norm(ALPHA * x + 0.5 * gate[:, 0, None, :] * f1, ln_g[l, 0], ln_b[l, 0])
        h = _modulate(x, shift[:, 1], scale[:, 1])
        if l < N_A:
            mix, st = _conv_module(h, conv_prev[l], pw1_w[l], pw1_b[l], dw_w[l], dw_b[l],
                                   conv_ln_g[l], conv_ln_b[l], pw2_w[l], pw2_b[l])
            new_conv.append(st)
        else:
            j = l - N_A
            q = (h @ w_q[j]).reshape(bsz, t, N_HEADS, HEAD_DIM)
            mix = _fox_attention(q, k_all, v_all, logf_all).reshape(bsz, t, D_MODEL) @ w_o[j]
        x = _layer_norm(ALPHA * x + gate[:, 1, None, :] * mix, ln_g[l, 1], ln_b[l, 1])
        h = _modulate(x, shift[:, 2], scale[:, 2])
        f2 = _swiglu(h, ffn_w_gate[l, 1], ffn_w_up[l, 1], ffn_w_down[l, 1])
        x = _layer_norm(ALPHA * x + 0.5 * gate[:, 2, None, :] * f2, ln_g[l, 2], ln_b[l, 2])
    return x, jnp.stack(new_conv), k_new, v_new, logf_new

def setup_inputs(seed: int = 0) -> dict:
    key = jax.random.key(seed)
    ks = jax.random.split(key, 40)
    n = lambda i, shape, s: jax.random.normal(ks[i], shape, jnp.float32) * s
    D = D_MODEL
    return {
        'x_prompt': n(0, (BATCH, SEQ, D), 1.0),
        'x_sample': n(1, (DEC_BATCH, DEC_SEQ, D), 1.0),
        'cache_conv': n(2, (N_A, DEC_BATCH, CONV_K - 1, D), 0.5),
        'cache_k': n(3, (DEC_BATCH, PAST_LEN, N_HEADS, HEAD_DIM), 1.0),
        'cache_v': n(4, (DEC_BATCH, PAST_LEN, N_HEADS, HEAD_DIM), BETA),
        'cache_logf': jax.nn.log_sigmoid(3.0 + n(5, (DEC_BATCH, PAST_LEN, N_HEADS), 1.0)),
        'c_prompt': n(6, (BATCH, D), 1.0),
        'c_sample': n(7, (DEC_BATCH, D), 1.0),
        'w_ada': n(8, (DEPTH, D, N_SUB * 3 * D), 0.1 * D ** -0.5),
        'b_ada': n(9, (DEPTH, N_SUB * 3 * D), 0.01),
        'ln_g': 1.0 + n(10, (DEPTH, N_SUB, D), 0.01),
        'ln_b': n(11, (DEPTH, N_SUB, D), 0.01),
        'ffn_w_gate': n(12, (DEPTH, 2, D, D_FF), D ** -0.5),
        'ffn_w_up': n(13, (DEPTH, 2, D, D_FF), D ** -0.5),
        'ffn_w_down': n(14, (DEPTH, 2, D_FF, D), BETA * D_FF ** -0.5),
        'pw1_w': n(15, (N_A, D, 2 * D), D ** -0.5),
        'pw1_b': n(16, (N_A, 2 * D), 0.01),
        'dw_w': n(17, (N_A, CONV_K, D), CONV_K ** -0.5),
        'dw_b': n(18, (N_A, D), 0.01),
        'conv_ln_g': 1.0 + n(19, (N_A, D), 0.01),
        'conv_ln_b': n(20, (N_A, D), 0.01),
        'pw2_w': n(21, (N_A, D, D), BETA * D ** -0.5),
        'pw2_b': n(22, (N_A, D), 0.01),
        'w_ada_kv': n(23, (D, 2 * D), 0.1 * D ** -0.5),
        'b_ada_kv': n(24, (2 * D,), 0.01),
        'w_k': n(25, (D, D), D ** -0.5),
        'w_v': n(26, (D, D), BETA * D ** -0.5),
        'w_f': n(27, (D, N_HEADS), D ** -0.5),
        'b_f': jnp.linspace(1.0, 6.0, N_HEADS, dtype=jnp.float32) + n(28, (N_HEADS,), 0.01),
        'w_q': n(29, (N_B, D, D), D ** -0.5),
        'w_o': n(30, (N_B, D, D), BETA * D ** -0.5),
    }

def reference(x_prompt, x_sample, cache_conv, cache_k, cache_v, cache_logf, c_prompt, c_sample,
              w_ada, b_ada, ln_g, ln_b, ffn_w_gate, ffn_w_up, ffn_w_down,
              pw1_w, pw1_b, dw_w, dw_b, conv_ln_g, conv_ln_b, pw2_w, pw2_b,
              w_ada_kv, b_ada_kv, w_k, w_v, w_f, b_f, w_q, w_o):
    weights = (w_ada, b_ada, ln_g, ln_b, ffn_w_gate, ffn_w_up, ffn_w_down,
               pw1_w, pw1_b, dw_w, dw_b, conv_ln_g, conv_ln_b, pw2_w, pw2_b,
               w_ada_kv, b_ada_kv, w_k, w_v, w_f, b_f, w_q, w_o)
    zero_conv = jnp.zeros((N_A, x_prompt.shape[0], CONV_K - 1, D_MODEL), x_prompt.dtype)
    y_prompt, conv_p, k_p, v_p, logf_p = _trunk(x_prompt, c_prompt, zero_conv, None, *weights)
    y_sample, conv_s, k_s, v_s, logf_s = _trunk(
        x_sample, c_sample, cache_conv, (cache_k, cache_v, cache_logf), *weights)
    return (y_prompt, y_sample, conv_p, k_p, v_p, logf_p, conv_s, k_s, v_s, logf_s)


_drawn_inputs = setup_inputs


def setup_inputs(seed=0):
    import zlib

    import numpy as np

    out = dict(_drawn_inputs(seed))
    spreads = {}
    factors = {'cache_logf': 8.0,
     'b_ada': 3.721,
     'pw1_b': 5.351,
     'dw_b': 8.0,
     'conv_ln_g': 8.0,
     'conv_ln_b': 8.0,
     'pw2_b': 7.823,
     'b_ada_kv': 3.964}
    for name, (base, spread) in spreads.items():
        noise = np.random.default_rng([zlib.crc32(name.encode()), seed]).standard_normal(out[name].shape)
        drawn = base * np.exp(spread * noise) if base else spread * noise
        out[name] = __import__('jax').numpy.asarray(drawn.astype(out[name].dtype))
    for name, factor in factors.items():
        out[name] = (out[name] * factor).astype(out[name].dtype)
    return out
```

```python
from contextlib import ExitStack

import numpy as np
import concourse.bass as bass
from concourse import mybir

F32 = mybir.dt.float32
F32R = mybir.dt.float32r
ALU = mybir.AluOpType
ACT = mybir.ActivationFunctionType
AX = mybir.AxisListType

P = 128
D = 1024
KT = D // P
SEQ = 256
DB, DS = 8, 16
T = SEQ + DB * DS
FF = 2816
FT = FF // P
PAST = 256
H, HD = 16, 64
CK = 31
HIST = CK - 1
NG = 1 + DB
ALPHA = float(4 ** 0.25)
EPS = 1e-5
UNIT = 1024
RING = 4
DOWN_K = ((0, 8), (8, 7), (15, 7))
FFN_UNITS = 2 * FT + 3 * KT
NK = PAST + DS
NEG = -1e30

U_FFN0 = 0
U_PW1 = U_FFN0 + FFN_UNITS
U_PW2 = U_PW1 + 2 * KT
U_FFN1 = U_PW2 + KT
U_K = U_FFN1 + FFN_UNITS
U_V = U_K + KT
U_FFN2 = U_V + KT
U_Q = U_FFN2 + FFN_UNITS
U_O = U_Q + KT
U_FFN3 = U_O + KT
N_UNITS = U_FFN3 + FFN_UNITS

V_L0, V_KV, V_L1, N_VEC = 0, 9, 11, 20
CHUNKS = 4 * N_VEC
FIRST_CHUNKS = 8

PAR = {}


def _par(name, n):
    PAR[name] = (PAR["_end"][1], n)
    PAR["_end"] = (0, PAR["_end"][1] + n)


PAR["_end"] = (0, 0)
_par("ln_g", 7 * KT)
_par("ln_b", 7 * KT)
_par("cln_g", KT)
_par("cln_b", KT)
_par("b_ada", 2 * CHUNKS)
_par("pw1_b", 2 * KT)
_par("pw2_b", KT)
_par("dw_b", KT)
_par("dw_w", KT * CK)
_par("b_f", 1)
N_PAR = PAR["_end"][1]

C_ID, C_ONES, C_SEL9, C_SELH, C_MP, C_MS, C_ONE = 0, 128, 256, 265, 521, 649, 665
N_CONST = 793


def build_program(nc, W, ADA, par_d, con_d, x_d, c_d, conv_d, kt_d, v_d, lf_d, wf_d,
                  y_o, kT_o, v_o, lf_o, conv_o, ncp_d, ncs_d):
    with ExitStack() as ctx:
        place = [(nc.sbuf_base + 31) // 32 * 32]

        def at(name, shape, offset, dt=F32):
            return nc.alloc_sbuf_tensor_at(name, shape, dt, offset=offset)

        def sb(name, shape, dt=F32):
            n = int(np.prod(shape[1:])) * 4
            o = place[0]
            place[0] += (n + 31) // 32 * 32
            return at(name, shape, o, dt)

        def sem(name):
            return ctx.enter_context(nc.semaphore(name))

        xa = sb("xa", [P, KT, T])
        z = sb("z", [P, KT, T])
        hH = sb("hH", [P, KT, T], F32R)
        hL = sb("hL", [P, KT, T], F32R)
        raw = sb("raw", [P, RING, UNIT])
        wH = sb("wH", [P, RING, UNIT], F32R)
        wL = sb("wL", [P, RING, UNIT], F32R)
        araw = sb("araw", [P, 2, 4, 256])
        hid = place[0]
        hidH = sb("hidH", [P, FT, T], F32R)
        hidL = sb("hidL", [P, FT, T], F32R)
        BLK = KT * T * 4
        land = at("land", [P, FIRST_CHUNKS, 2, 4, 256], hid)
        sq = at("sq", [P, KT, T], hid + 3 * BLK)
        h32 = at("h32", [P, KT, T], hid + 3 * BLK)
        uP = at("uP", [P, KT, HIST + SEQ], hid)
        uS = at("uS", [P, KT, DB, HIST + DS], hid + KT * (HIST + SEQ) * 4)
        conv_st = at("conv_st", [P, KT, HIST * NG], hid + 2 * BLK)
        conv_in = at("conv_in", [P, KT, DB, HIST], hid + 4 * BLK)
        kvH = at("kvH", [P, KT, T], hid, F32R)
        kvL = at("kvL", [P, KT, T], hid + BLK, F32R)
        kv32 = at("kv32", [P, KT, T], hid + 2 * BLK)
        kF = at("kF", [P, KT, T], hid + 3 * BLK)
        vS = at("vS", [P, 3, D], hid + 4 * BLK)
        hH_off = hH.manual_sbuf_range[0]
        lfS = at("lfS", [H, DB, NK], hH_off)
        lfP = at("lfP", [H, SEQ], hH_off + DB * NK * 4)
        hL_off = hL.manual_sbuf_range[0]
        lf_l = at("lf_l", [H, T], hL_off)
        lf_m = at("lf_m", [H, T], hL_off + 4 * T)
        lf_e = at("lf_e", [H, T], hL_off + 8 * T)
        lf_g = at("lf_g", [H, T], hL_off + 12 * T)
        lf_n = at("lf_n", [H, T], hL_off + 16 * T)
        q32 = at("q32", [P, KT, T], hid)
        o = hid + BLK
        KP = at("KP", [P, 2, SEQ], o)
        VP = at("VP", [P, 2, 2, P], o + 2048)
        qP = at("qP", [P, 2, SEQ], o + 4096)
        ncP = at("ncP", [1, 2, 2, SEQ], o + 6144)
        ncS = at("ncS", [H, 2, NK], o + 10240)
        o += 10240 + 2 * NK * 4
        KTb = at("KTb", [P, 2, KT, NK], o)
        o += 2 * KT * NK * 4
        Vb = at("Vb", [P, 2, 2, D], o)
        o += 2 * 2 * D * 4
        Vn = at("Vn", [DS, 2, D], o)
        assert o + 2 * D * 4 <= hid + 2 * FT * T * 4
        par = sb("par", [P, N_PAR])
        con = sb("con", [P, N_CONST])
        mods = sb("mods", [P, KT * N_VEC, NG])
        craw = sb("craw", [P, KT, 32])
        cact = sb("cact", [P, KT, 32])
        wf = sb("wf", [P, KT, H])
        Am = sb("Am", [P, 2, KT, NG])
        Bm = sb("Bm", [P, 2, KT, NG])
        Gm = sb("Gm", [P, 2, KT, NG])
        gA = sb("gA", [P, 7 * KT])
        bA = sb("bA", [P, 7 * KT])
        sg = sb("sg", [P, 2, T])
        tmp = sb("tmp", [P, 2, T])
        epS = sb("epS", [P, 2, DB * DS])
        zs = sb("zs", [P, T])
        ve = sb("ve", [P, T])
        rstd = sb("rstd", [P, T])
        sd = sb("sd", [P, T])
        adaS = sb("adaS", [P, 256])
        qbd = sb("qbd", [P, 2, KT, 2 * DS])
        nmx = sb("nmx", [P, 4])
        rsm = sb("rsm", [P, 4])
        rin = sb("rin", [P, 4])
        assert place[0] <= nc.sbuf_usable_end, place[0] - nc.sbuf_usable_end
        ident = con[:, C_ID:C_ID + P]
        ones = con[:, C_ONES:C_ONES + P]

        bank = [ctx.enter_context(nc.psum_tensor(f"bank{i}", [P, 512], F32)) for i in range(8)]
        MEAN, VAR, ADB = bank[6], bank[5], bank[7]

        def pcol(name, c=0, n=1):
            a = PAR[name][0]
            return par[:, bass.ds(a + c, n)]

        par_in, wf_in, con_in, x_in, c_in, convc_in, lf_in, conv_out = (sem(n) for n in (
            "par_in", "wf_in", "con_in", "x_in", "c_in", "convc_in", "lf_in", "conv_out"))
        land_in = [sem(f"land_in{i}") for i in range(FIRST_CHUNKS)]
        w_in = [sem(f"w_in{i}") for i in range(RING)]
        w_hi = sem("w_hi")
        w_lo = sem("w_lo")
        w_used = sem("w_used")
        a_in = [sem(f"a_in{i}") for i in range(2)]
        a_mm, a_ev, a_tr, a_mod = (sem(n) for n in ("a_mm", "a_ev", "a_tr", "a_mod"))
        cact_ok, init_dve, init_pool = sem("cact_ok"), sem("init_dve"), sem("init_pool")
        z_ready = sem("z_ready")
        zs_done, mean_ok, zc_done, sq_done, var_ok, ve_done, sd_done, rs_done, zn_done = (sem(n) for n in (
            "zs_done", "mean_ok", "zc_done", "sq_done", "var_ok", "ve_done", "sd_done", "rs_done", "zn_done"))
        ab_done, hp_done, hs1_done, hs_done, hh_done, hl_done, xa_done = (sem(n) for n in (
            "ab_done", "hp_done", "hs1_done", "hs_done", "hh_done", "hl_done", "xa_done"))
        sm_done = sem("sm_done")
        gm_done = sem("gm_done")
        ep1_done = sem("ep1_done")
        sg_done = [sem(f"sg_done{i}") for i in range(4)]
        prod = [sem(f"prod{i}") for i in range(4)]
        hidh = [sem(f"hidh{i}") for i in range(4)]
        hidl = [sem(f"hidl{i}") for i in range(4)]
        hist_ok, sig_done, u_done, tapP, tapS, convst_ok = (sem(n) for n in (
            "hist_ok", "sig_done", "u_done", "tapP", "tapS", "convst_ok"))
        silu_done = sem("silu_done")
        kf_done, vs_done, f_mm, lf_chain, lfe_done, lfg_done, ncum_done, lfo_done = (sem(n) for n in (
            "kf_done", "vs_done", "f_mm", "lf_chain", "lfe_done", "lfg_done", "ncum_done", "lfo_done"))
        kv_out, nc_out, fin_out = sem("kv_out"), sem("nc_out"), sem("fin_out")
        q_done, qp_done, qbd_done = sem("q_done"), sem("qp_done"), sem("qbd_done")
        pr_in = [sem(f"pr_in{i}") for i in range(2)]
        st_in = [sem(f"st_in{i}") for i in range(2)]
        s_mm, nm_done, p_done, ri_done, pn_done, t_mm, pt_done, pv_mm, o_done = (sem(n) for n in (
            "s_mm", "nm_done", "p_done", "ri_done", "pn_done", "t_mm", "pt_done", "pv_mm", "o_done"))
        y_done = sem("y_done")

        GATE_VEC = [V_L0 + 2, V_L0 + 5, V_L0 + 8, V_L1 + 2, V_L1 + 5, V_L1 + 8]
        MODS = [(-1, 0, V_L0, False), (0, 1, V_L0 + 3, False), (2, 2, V_L0 + 6, False),
                (3, 3, V_KV, True), (3, 3, V_L1, False), (4, 4, V_L1 + 3, False), (5, 5, V_L1 + 6, False)]
        M_S0, M_S1, M_PW2, M_S2, M_KV, M_S3, M_S4, M_O, M_S5 = range(9)
        FFN_M = [M_S0, M_S2, M_S3, M_S5]
        FFN_U = [U_FFN0, U_FFN1, U_FFN2, U_FFN3]
        FFN_LN = [0, 3, 4, 6]
        FFN_SUB = [0, 2, 3, 5]
        FFN_ADA = [(8, 11, 1, 0), (32, 11, 1, 8), (52, 11, 1, 0), (76, 4, 0, 0)]
        CH_S1, CH_S4 = 20, 64

        def streams(ap):
            return ap.rearrange("p k (b t) -> p k b t", b=DB)

        def over_tokens(ap, k):
            return ap.unsqueeze(3).to_broadcast([P, k, DB, DS])

        block = ctx.enter_context(nc.Block())

        @block.sync
        def _(sp):
            def w_unit(n, slot, wait=True):
                if wait:
                    sp.wait_ge(w_lo, n - (RING - 1))
                sp.dma_start(raw[:, slot, :], W[n]).then_inc(w_in[slot], 16)

            def w_units(n, count, wait=True):
                for j in range(count):
                    w_unit(n + j, j % RING, wait)

            def ada_chunk(c):
                sp.wait_ge(a_mm, c)
                for j in range(2):
                    sp.dma_start(araw[:, j], ADA[2 * c + j]).then_inc(a_in[j], 16)

            def ffn(fi):
                u, (c, na, before, after) = FFN_U[fi], FFN_ADA[fi]
                if fi != 2:
                    w_units(u, RING, wait=fi > 0)
                with sp.Fori(0, na) as i:
                    ada_chunk(c + i)
                    w_units(u + RING + RING * i, RING)
                if na < 11:
                    with sp.Fori(na, 11) as i:
                        w_units(u + RING + RING * i, RING)
                for j in range(before):
                    ada_chunk(c + na + j)
                with sp.Fori(0, 5 if fi == 3 else 6) as i:
                    w_units(u + 48 + RING * i, RING)
                if after:
                    with sp.Fori(0, after) as i:
                        ada_chunk(c + na + before + i)

            sp.dma_start(craw[:], c_d).then_inc(c_in, 16)
            sp.dma_start(par[:], par_d).then_inc(par_in, 16)
            sp.dma_start(con[:], con_d).then_inc(con_in, 16)
            sp.dma_start(z[:], x_d).then_inc(x_in, 16)
            for c in range(FIRST_CHUNKS):
                sp.dma_start(land[:, c, 0], ADA[2 * c]).then_inc(land_in[c], 16)
                sp.dma_start(land[:, c, 1], ADA[2 * c + 1]).then_inc(land_in[c], 16)
            sp.dma_start(wf[:], wf_d).then_inc(wf_in, 16)
            ffn(0)
            sp.wait_ge(xa_done, 2 * KT)
            sp.dma_start(conv_in[:], conv_d).then_inc(convc_in, 16)
            with sp.Fori(0, 4) as i:
                ada_chunk(CH_S1 + 2 * i)
                ada_chunk(CH_S1 + 2 * i + 1)
                w_units(U_PW1 + RING + RING * i, RING)
            with sp.Fori(0, 4) as i:
                ada_chunk(CH_S1 + 8 + i)
            w_units(U_PW2 + RING, RING)
            sp.wait_ge(convst_ok, 1)
            sp.dma_start(conv_o, conv_st[:]).then_inc(conv_out, 16)
            ffn(1)
            sp.dma_start(lfS[:, :, 0:PAST], lf_d).then_inc(lf_in, 16)
            w_units(U_K + RING, RING)
            sp.wait_ge(ncum_done, NG)
            sp.dma_start(ncs_d, lfS[:]).then_inc(nc_out, 16)
            sp.dma_start(ncp_d, lfP[:]).then_inc(nc_out, 16)
            sp.dma_start(lf_o, lf_n[:]).then_inc(nc_out, 16)
            w_units(U_V, 3 * RING)
            sp.wait_ge(kf_done, KT)
            sp.dma_start(kT_o, kF[:]).then_inc(kv_out, 16)
            sp.wait_ge(vs_done, 6)
            sp.dma_start(v_o.rearrange("(t p) n -> p t n", p=P), vS[:]).then_inc(kv_out, 16)
            ffn(2)
            w_units(U_Q + RING, RING)
            w_units(U_O, RING)
            sp.wait_ge(kv_out, 32)
            sp.wait_ge(nc_out, 48)
            sp.wait_ge(xa_done, 5 * KT)

            def prompt_pair(pr, s):
                sp.dma_start(KP[:, s], kT_o[:, pr, 0:SEQ]).then_inc(pr_in[s], 16)
                sp.dma_start(VP[:, s], v_o[0:SEQ, bass.ds(P * pr, P)].rearrange("(t p) n -> p t n", p=P))\
                    .then_inc(pr_in[s], 16)
                sp.dma_start(ncP[:, s], ncp_d[bass.ds(2 * pr, 2), :].rearrange("(a h) s -> a h s", a=1))\
                    .then_inc(pr_in[s], 16)

            def stream(b, s):
                sp.dma_start(KTb[:, s, :, 0:PAST], kt_d[b]).then_inc(st_in[s], 16)
                sp.dma_start(KTb[:, s, :, PAST:NK], kT_o[:, :, bass.ds(SEQ + DS * b, DS)]).then_inc(st_in[s], 16)
                sp.dma_start(Vb[:, s], v_d[b].rearrange("(t p) n -> p t n", p=P)).then_inc(st_in[s], 16)
                sp.dma_start(Vn[:, s], v_o[bass.ds(SEQ + DS * b, DS), :]).then_inc(st_in[s], 16)
                sp.dma_start(ncS[:, s], ncs_d[:, b, :]).then_inc(st_in[s], 16)

            for s in range(2):
                prompt_pair(s, s)
            with sp.Fori(0, 3) as i:
                ada_chunk(CH_S4 + i)
                for s in range(2):
                    sp.wait_ge(pv_mm, 8 * i + 4 * (s + 1))
                    prompt_pair(2 * (i + 1) + s, s)
            ada_chunk(CH_S4 + 3)
            for s in range(2):
                stream(s, s)
            with sp.Fori(0, 3) as i:
                ada_chunk(CH_S4 + 4 + 2 * i)
                for s in range(2):
                    sp.wait_ge(pv_mm, 32 + 4 * i + 2 * (s + 1))
                    stream(2 * (i + 1) + s, s)
                ada_chunk(CH_S4 + 5 + 2 * i)
            ada_chunk(CH_S4 + 10)
            ada_chunk(CH_S4 + 11)
            w_units(U_O + RING, RING)
            ffn(3)
            for g in range(4):
                sp.wait_ge(y_done, g + 1)
                sp.dma_start(y_o[:, 2 * g:2 * g + 2], z[:, 2 * g:2 * g + 2]).then_inc(fin_out, 16)
            sp.wait_ge(fin_out, 64)
            sp.wait_ge(conv_out, 16)

        @block.gpsimd
        def _(pool):
            g = nc.gpsimd
            g.memset(qbd[:], 0.0).then_inc(init_pool, 1)

            def sums(n):
                for k in range(KT):
                    pool.wait_ge(z_ready, 2 + KT * n + k + 1)
                    if k == 0:
                        op = g.tensor_copy(zs[:], z[:, 0, :])
                    else:
                        pool.wait_ge(zs_done, KT * n + k)
                        op = g.tensor_tensor(zs[:], zs[:], z[:, k, :], ALU.add)
                    op.then_inc(zs_done, 1)

            def modulate(mi):
                n, _, _, kv = MODS[mi]
                dst = kv32 if mi in (3, 4) else h32
                pool.wait_ge(ab_done, mi + 1)
                for q in range(4):
                    ks = slice(2 * q, 2 * q + 2)
                    if n >= 0:
                        pool.wait_ge(zn_done, 4 * n + q + 1)
                    else:
                        pool.wait_ge(x_in, 16)
                    dd = streams(dst[:, ks, SEQ:T])
                    g.tensor_tensor(dd, streams(z[:, ks, SEQ:T]),
                                    over_tokens(Am[:, mi % 2, ks, 1:NG], 2), ALU.mult).then_inc(hs1_done, 1)
                    pool.wait_ge(hs1_done, 4 * mi + q + 1)
                    g.tensor_tensor(dd, dd, over_tokens(Bm[:, mi % 2, ks, 1:NG], 2), ALU.add)\
                        .then_inc(hs_done, 1)

            def residual(e):
                for k in range(KT):
                    c = e * KT + k
                    g.tensor_scalar(xa[:, k, :], z[:, k, :], gA[:, c:c + 1], bA[:, c:c + 1],
                                    ALU.mult, ALU.add).then_inc(xa_done, 1)

            modulate(0)
            pool.wait_ge(init_dve, 1)
            residual(0)
            sums(0)
            modulate(1)
            residual(1)
            g.memset(uP[:, :, 0:HIST], 0.0).then_inc(hist_ok, 1)
            pool.wait_ge(convc_in, 16)
            for k in range(KT):
                op = g.tensor_copy(uS[:, k, :, 0:HIST], conv_in[:, k])
            op.then_inc(hist_ok, 1)
            sums(1)
            for k in range(KT):
                g.tensor_copy(conv_st[:, k, 0:HIST], uP[:, k, SEQ:SEQ + HIST])
                op = g.tensor_copy(conv_st[:, k, HIST:].rearrange("p (b t) -> p b t", b=DB),
                                   uS[:, k, :, DS:DS + HIST])
            op.then_inc(convst_ok, 1)
            sums(2)
            modulate(2)
            residual(2)
            sums(3)
            modulate(3)
            pool.wait_ge(f_mm, 1)
            pool.wait_ge(hl_done, 4 * M_KV + 4)
            modulate(4)
            residual(3)
            sums(4)
            modulate(5)
            residual(4)
            sums(5)
            modulate(6)
            residual(5)
            sums(6)

        @block.scalar
        def _(act):
            a = nc.scalar

            def refill(n, slot, wait_used=True):
                if wait_used:
                    act.wait_ge(w_used, n - (RING - 1))
                act.wait_ge(w_in[slot], landed(n, slot))
                a.activation(wH[:, slot, :], raw[:, slot, :], ACT.Copy).then_inc(w_hi, 1)

            def landed(n, slot):
                return 4 * n - 4 * slot + 16

            def ada_evac(c):
                act.wait_ge(a_mm, c + 1)
                a.activation(adaS[:], ADB[:, 0:256], ACT.Copy).then_inc(a_ev, 1)

            def ada_mods(c):
                act.wait_ge(a_tr, c + 1)
                for j in range(2):
                    op = a.activation(mods[:, 2 * c + j, :], ADB[:, 256 + 16 * j:256 + 16 * j + NG], ACT.Identity,
                                      bias=pcol("b_ada", 2 * c + j))
                op.then_inc(a_mod, 1)

            def squares(n):
                a.preload_act_table(ACT.Sqrt)
                for q in range(4):
                    act.wait_ge(zc_done, 4 * n + q + 1)
                    a.activation(sq[:, 2 * q:2 * q + 2, :], z[:, 2 * q:2 * q + 2, :], ACT.Square)\
                        .then_inc(sq_done, 1)
                act.wait_ge(ve_done, n + 1)
                a.activation(sd[:], ve[:], ACT.Sqrt).then_inc(sd_done, 1)

            def split_h(m, mi, src, dst):
                for q in range(4):
                    if mi is not None:
                        act.wait_ge(hp_done, 4 * mi + q + 1)
                        act.wait_ge(hs_done, 4 * mi + q + 1)
                    a.activation(dst[:, 2 * q:2 * q + 2, :], src[:, 2 * q:2 * q + 2, :], ACT.Copy)\
                        .then_inc(hh_done, 1)

            def ffn(fi):
                u, (c, na, before, after) = FFN_U[fi], FFN_ADA[fi]

                def gate_up(i, with_ada):
                    for j in range(2):
                        f, n = 2 * i + j, u + 4 * i + 2 * j
                        act.wait_ge(w_used, n + 1)
                        act.wait_ge(prod[fi], f + 1)
                        a.activation(sg[:, j, :], bank[2 * j][:, 0:T], ACT.Silu).then_inc(sg_done[fi], 1)
                        refill(n + RING, 2 * j)
                        refill(n + RING + 1, 2 * j + 1)
                        act.wait_ge(prod[fi], f + 3)
                        a.activation(hidH[:, f, :], tmp[:, j, :], ACT.Copy).then_inc(hidh[fi], 1)
                        if with_ada:
                            if j == 0:
                                ada_evac(c + i)
                            else:
                                ada_mods(c + i)

                with act.Fori(0, na) as i:
                    gate_up(i, True)
                if na < 11:
                    with act.Fori(na, 11) as i:
                        gate_up(i, False)
                for j in range(before):
                    ada_evac(c + na + j)
                    ada_mods(c + na + j)
                last = fi == 3
                with act.Fori(0, 5 if last else 6) as i:
                    for j in range(RING):
                        refill(u + 48 + RING * i + j, j)
                if after:
                    with act.Fori(0, after) as i:
                        ada_evac(c + na + before + i)
                        ada_mods(c + na + before + i)
                squares(FFN_LN[fi])

            act.wait_ge(c_in, 16)
            a.activation(cact[:], craw[:], ACT.Silu).then_inc(cact_ok, 1)
            act.wait_ge(par_in, 16)
            act.wait_ge(con_in, 16)
            for c in range(FIRST_CHUNKS):
                ada_evac(c)
                ada_mods(c)
                if c < RING:
                    refill(c, c, wait_used=False)
            split_h(M_S0, 0, h32, hH)
            ffn(0)
            split_h(M_S1, 1, h32, hH)
            with act.Fori(0, 4) as i:
                for j in range(2):
                    n = U_PW1 + 4 * i + 2 * j
                    act.wait_ge(w_used, n + 2)
                    act.wait_ge(u_done, 2 * i + j + 1)
                    a.activation(sg[:, j, :], bank[2 * j + 1][:, 0:T], ACT.Sigmoid,
                                 bias=pcol("pw1_b", KT + 2 * i + j)).then_inc(sig_done, 1)
                    refill(n + RING, 2 * j)
                    refill(n + RING + 1, 2 * j + 1)
                    ada_evac(CH_S1 + 2 * i + j)
                    ada_mods(CH_S1 + 2 * i + j)
            with act.Fori(0, 4) as i:
                ada_evac(CH_S1 + 8 + i)
                ada_mods(CH_S1 + 8 + i)
            squares(1)
            for k in range(KT):
                act.wait_ge(zn_done, 4 * 1 + k // 2 + 1)
                a.activation(h32[:, k, :], z[:, k, :], ACT.Silu, bias=pcol("cln_b", k),
                             scale=pcol("cln_g", k)).then_inc(silu_done, 1)
            act.wait_ge(silu_done, KT)
            split_h(M_PW2, None, h32, hH)
            with act.Fori(0, 2) as i:
                for j in range(RING):
                    refill(U_PW2 + RING + RING * i + j, j)
            squares(2)
            split_h(M_S2, 2, h32, hH)
            act.wait_ge(conv_out, 16)
            ffn(1)
            split_h(M_KV, 3, kv32, kvH)
            act.wait_ge(lf_chain, 1)
            a.activation(lf_e[:], lf_e[:], ACT.Exp, scale=-1.0).then_inc(lfe_done, 1)
            act.wait_ge(lfe_done, 1)
            a.activation(lf_g[:], lf_e[:], ACT.Ln, bias=1.0).then_inc(lfg_done, 1)
            with act.Fori(0, 2) as i:
                for j in range(RING):
                    n = U_K + RING * i + j
                    act.wait_ge(w_used, n + 1)
                    a.activation(kF[:, RING * i + j, :], bank[j][:, 0:T], ACT.Copy).then_inc(kf_done, 1)
                    refill(n + RING, j)
            for half in range(2):
                for j in range(RING):
                    n = U_V + RING * half + j
                    refill(n + RING, j)
                for t in range(3):
                    a.activation(vS[:, t, half * 512:(half + 1) * 512], bank[3 * half + t][:, :], ACT.Copy)\
                        .then_inc(vs_done, 1)
            act.wait_ge(nc_out, 48)
            split_h(M_S3, 4, kv32, hH)
            act.wait_ge(kv_out, 32)
            ffn(2)
            split_h(M_S4, 5, h32, hH)
            act.wait_ge(xa_done, 5 * KT)
            with act.Fori(0, 2) as i:
                for j in range(RING):
                    n = U_Q + RING * i + j
                    act.wait_ge(w_used, n + 1)
                    a.activation(q32[:, RING * i + j, :], bank[j][:, 0:T], ACT.Copy, scale=HD ** -0.5)\
                        .then_inc(q_done, 1)
                    refill(n + RING, j)

            def soft(J, w, par2):
                act.wait_ge(nm_done, J + 1)
                act.wait_ge(t_mm, J + 1)
                a.activation(sg[:, par2, 0:w], bank[par2][:, 0:w], ACT.Exp, bias=nmx[:, par2:par2 + 1],
                             accum_out=rsm[:, par2:par2 + 1]).then_inc(p_done, 1)

            def evac_t(J, nt, par2):
                act.wait_ge(t_mm, J + 3)
                a.activation(tmp[:, par2, 0:nt * P], bank[2 + par2][:, 0:nt * P], ACT.Copy).then_inc(pt_done, 1)

            act.wait_ge(q_done, KT)
            with act.Fori(0, 4) as i:
                for s in range(2):
                    act.wait_ge(t_mm, 8 * i + 2)
                    a.activation(qP[:, s, :], q32[:, 2 * i + s, 0:SEQ], ACT.Copy).then_inc(qp_done, 1)
                for j in range(8 + 1):
                    if j < 8:
                        soft(8 * i + j, P * (1 + j % 2), j % 2)
                    if j >= 1:
                        evac_t(8 * i + j - 1, 1 + (j - 1) % 2, (j - 1) % 2)
                ada_evac(CH_S4 + i)
                ada_mods(CH_S4 + i)
            with act.Fori(0, 4) as i:
                for j in range(4 + 1):
                    if j < 4:
                        soft(32 + 4 * i + j, NK, j % 2)
                    if j >= 1:
                        evac_t(32 + 4 * i + j - 1, 3, (j - 1) % 2)
                for j in range(2):
                    ada_evac(CH_S4 + 4 + 2 * i + j)
                    ada_mods(CH_S4 + 4 + 2 * i + j)
            act.wait_ge(o_done, 2 + 48)
            split_h(M_O, None, z, hH)
            with act.Fori(0, 2) as i:
                for j in range(RING):
                    refill(U_O + RING + RING * i + j, j)
            squares(5)
            split_h(M_S5, 6, h32, hH)
            ffn(3)

        @block.vector
        def _(dve):
            v = nc.vector
            small = [0]

            def step(op):
                small[0] += 1
                op.then_inc(sm_done, 1)
                dve.wait_ge(sm_done, small[0])

            def refill(n, slot):
                dve.wait_ge(w_hi, n + 1)
                v.tensor_tensor(wL[:, slot, :], raw[:, slot, :], wH[:, slot, :].bitcast(F32), ALU.subtract)\
                    .then_inc(w_lo, 1)

            def normalise(n, meanwhile=()):
                dve.wait_ge(mean_ok, n + 1)
                for q in range(4):
                    ks = slice(2 * q, 2 * q + 2)
                    v.tensor_tensor(z[:, ks, :], z[:, ks, :],
                                    MEAN[:, 0:T].unsqueeze(1).to_broadcast([P, 2, T]), ALU.subtract)\
                        .then_inc(zc_done, 1)
                for mi in meanwhile:
                    prepare(mi)
                dve.wait_ge(var_ok, n + 1)
                v.tensor_scalar(ve[:], VAR[:, 0:T], EPS, None, ALU.add).then_inc(ve_done, 1)
                dve.wait_ge(sd_done, n + 1)
                v.reciprocal(rstd[:], sd[:]).then_inc(rs_done, 1)
                dve.wait_ge(rs_done, n + 1)
                for q in range(4):
                    ks = slice(2 * q, 2 * q + 2)
                    v.tensor_tensor(z[:, ks, :], z[:, ks, :],
                                    rstd[:].unsqueeze(1).to_broadcast([P, 2, T]), ALU.mult).then_inc(zn_done, 1)

            def prepare(mi):
                _, e, vec, _ = MODS[mi]
                dve.wait_ge(a_mod, 4 * (vec + 2))
                shift, scale = mods[:, KT * vec:KT * vec + KT, :], mods[:, KT * vec + KT:KT * vec + 2 * KT, :]
                gg = pcol("ln_g", e * KT, KT).unsqueeze(2).to_broadcast([P, KT, NG])
                bb = pcol("ln_b", e * KT, KT).unsqueeze(2).to_broadcast([P, KT, NG])
                step(v.scalar_tensor_tensor(Am[:, mi % 2], scale, 1.0, gg, ALU.add, ALU.mult))
                step(v.scalar_tensor_tensor(Bm[:, mi % 2], scale, 1.0, bb, ALU.add, ALU.mult))
                v.tensor_tensor(Bm[:, mi % 2], Bm[:, mi % 2], shift, ALU.add).then_inc(ab_done, 1)

            def modulate(mi):
                n, _, _, kv = MODS[mi]
                dst = kv32 if mi in (3, 4) else h32
                dve.wait_ge(ab_done, mi + 1)
                if n >= 0:
                    dve.wait_ge(zn_done, 4 * n + 4)
                else:
                    dve.wait_ge(x_in, 16)
                for k in range(KT):
                    op = v.tensor_scalar(dst[:, k, 0:SEQ], z[:, k, 0:SEQ], Am[:, mi % 2, k, 0:1],
                                         Bm[:, mi % 2, k, 0:1], ALU.mult, ALU.add)
                    if k % 2:
                        op.then_inc(hp_done, 1)

            def rest_h(m, src, hi, lo):
                for q in range(4):
                    ks = slice(2 * q, 2 * q + 2)
                    dve.wait_ge(hh_done, 4 * m + q + 1)
                    v.tensor_tensor(lo[:, ks, :], src[:, ks, :], hi[:, ks, :].bitcast(F32), ALU.subtract)\
                        .then_inc(hl_done, 1)

            def gate(r):
                vec = GATE_VEC[r]
                dve.wait_ge(a_mod, 4 * (vec + 1))
                v.tensor_scalar(Gm[:, r % 2], mods[:, KT * vec:KT * vec + KT, :], 1.0,
                                1.0 if r in (1, 4) else 0.5, ALU.add, ALU.mult).then_inc(gm_done, 1)
                dve.wait_ge(gm_done, r + 1)

            def add_residual(r, d, src, par2, bias=None):
                G = Gm[:, r % 2]
                if bias is None:
                    v.scalar_tensor_tensor(z[:, d, 0:SEQ], src[:, 0:SEQ], G[:, d, 0:1], xa[:, d, 0:SEQ],
                                           ALU.mult, ALU.add)
                    v.tensor_tensor(epS[:, par2].rearrange("p (b t) -> p b t", b=DB),
                                    src[:, SEQ:T].rearrange("p (b t) -> p b t", b=DB),
                                    G[:, d, 1:NG].unsqueeze(2).to_broadcast([P, DB, DS]), ALU.mult)\
                        .then_inc(ep1_done, 1)
                else:
                    v.tensor_scalar(z[:, d, 0:SEQ], src[:, 0:SEQ], bias, G[:, d, 0:1], ALU.add, ALU.mult)
                    v.scalar_tensor_tensor(epS[:, par2].rearrange("p (b t) -> p b t", b=DB),
                                           src[:, SEQ:T].rearrange("p (b t) -> p b t", b=DB), bias,
                                           G[:, d, 1:NG].unsqueeze(2).to_broadcast([P, DB, DS]),
                                           ALU.add, ALU.mult).then_inc(ep1_done, 1)
                dve.wait_ge(ep1_done, KT * r + d + 1)
                if bias is not None:
                    v.tensor_tensor(z[:, d, 0:SEQ], z[:, d, 0:SEQ], xa[:, d, 0:SEQ], ALU.add)
                v.tensor_tensor(z[:, d, SEQ:T], epS[:, par2], xa[:, d, SEQ:T], ALU.add).then_inc(z_ready, 1)

            def ffn(fi):
                u, (c, na, before, after) = FFN_U[fi], FFN_ADA[fi]
                r, n_ln = FFN_SUB[fi], FFN_LN[fi]
                dve.sem_inc(prod[fi], 2)
                with dve.Fori(0, 11) as i:
                    for j in range(2):
                        f, n = 2 * i + j, u + 4 * i + 2 * j
                        dve.wait_ge(w_used, n + 2)
                        dve.wait_ge(sg_done[fi], f + 1)
                        v.tensor_tensor(tmp[:, j, :], sg[:, j, :], bank[2 * j + 1][:, 0:T], ALU.mult)\
                            .then_inc(prod[fi], 1)
                        refill(n + RING, 2 * j)
                        refill(n + RING + 1, 2 * j + 1)
                        dve.wait_ge(hidh[fi], f + 1)
                        v.tensor_tensor(hidL[:, f, :], tmp[:, j, :], hidH[:, f, :].bitcast(F32), ALU.subtract)\
                            .then_inc(hidl[fi], 1)
                gate(r)
                dve.wait_ge(xa_done, KT * (r + 1))

                def down(i, dd, n_refill):
                    n = u + 2 * FT + 12 * i + 3 * dd
                    dve.wait_ge(w_used, n + 3)
                    add_residual(r, 4 * i + dd, bank[4 + dd % 2], dd % 2)

                last = fi == 3
                if not last:
                    with dve.Fori(0, 2) as i:
                        for dd in range(4):
                            for j in range(3):
                                refill(u + 48 + 12 * i + 3 * dd + j, (3 * dd + j) % RING)
                            down(i, dd, 3)
                else:
                    for i in range(2):
                        for dd in range(4):
                            for j in range(3):
                                if 12 * i + 3 * dd + j < 20:
                                    refill(u + 48 + 12 * i + 3 * dd + j, (3 * dd + j) % RING)
                            down(i, dd, 3)
                normalise(n_ln, PREP[r])

            PREP = {0: [1], 2: [3, 4], 3: [5], 5: []}

            dve.sem_inc(z_ready, 2)
            dve.sem_inc(u_done, 2)
            dve.sem_inc(o_done, 2)
            dve.wait_ge(par_in, 16)
            g0, b0 = PAR["ln_g"][0], PAR["ln_b"][0]
            v.tensor_scalar(gA[:], par[:, g0:g0 + 7 * KT], ALPHA, None, ALU.mult)
            v.tensor_scalar(bA[:], par[:, b0:b0 + 7 * KT], ALPHA, None, ALU.mult).then_inc(init_dve, 1)
            for n in range(RING):
                refill(n, n)
            prepare(0)
            modulate(0)
            rest_h(M_S0, h32, hH, hL)
            ffn(0)
            modulate(1)
            rest_h(M_S1, h32, hH, hL)
            dve.wait_ge(hist_ok, 2)
            with dve.Fori(0, 4) as i:
                for j in range(2):
                    d, n = 2 * i + j, U_PW1 + 4 * i + 2 * j
                    dve.wait_ge(sig_done, d + 1)
                    A = bank[2 * j]
                    v.scalar_tensor_tensor(uP[:, d, HIST:], A[:, 0:SEQ], pcol("pw1_b", d), sg[:, j, 0:SEQ],
                                           ALU.add, ALU.mult)
                    v.scalar_tensor_tensor(uS[:, d, :, HIST:], A[:, SEQ:T].rearrange("p (b t) -> p b t", b=DB),
                                           pcol("pw1_b", d), sg[:, j, SEQ:T].rearrange("p (b t) -> p b t", b=DB),
                                           ALU.add, ALU.mult).then_inc(u_done, 1)
                    refill(n + RING, 2 * j)
                    refill(n + RING + 1, 2 * j + 1)
                    dve.wait_ge(u_done, 2 + d + 1)
                    zP = z[:, d, 0:SEQ]
                    zS = z[:, d, SEQ:T].rearrange("p (b t) -> p b t", b=DB)
                    for k in range(CK):
                        w = pcol("dw_w", CK * d + k)
                        sP, sS = uP[:, d, k:k + SEQ], uS[:, d, :, k:k + DS]
                        if k == 0:
                            v.tensor_scalar(zP, sP, w, pcol("dw_b", d), ALU.mult, ALU.add).then_inc(tapP, 1)
                            v.tensor_scalar(zS, sS, w, pcol("dw_b", d), ALU.mult, ALU.add).then_inc(tapS, 1)
                        else:
                            dve.wait_ge(tapP, CK * d + k)
                            v.scalar_tensor_tensor(zP, sP, w, zP, ALU.mult, ALU.add).then_inc(tapP, 1)
                            dve.wait_ge(tapS, (CK - 1) * d + k)
                            op = v.scalar_tensor_tensor(zS, sS, w, zS, ALU.mult, ALU.add)
                            op.then_inc(tapS if k < CK - 1 else z_ready, 1)
            normalise(1)
            rest_h(M_PW2, h32, hH, hL)
            gate(1)
            dve.wait_ge(xa_done, 2 * KT)
            with dve.Fori(0, 2) as i:
                for j in range(RING):
                    n = U_PW2 + RING * i + j
                    refill(n + RING, j)
                    dve.wait_ge(w_used, n + 1)
                    add_residual(1, RING * i + j, bank[j], j % 2, bias=pcol("pw2_b", RING * i + j))
            normalise(2, [2])
            modulate(2)
            rest_h(M_S2, h32, hH, hL)
            ffn(1)
            modulate(3)
            rest_h(M_KV, kv32, kvH, kvL)
            dve.wait_ge(f_mm, 1)
            step(v.tensor_scalar(lf_l[:], bank[6][0:H, 0:T], par[0:H, PAR["b_f"][0]:PAR["b_f"][0] + 1], None,
                                 ALU.add))
            step(v.tensor_scalar(lf_m[:], lf_l[:], 0.0, None, ALU.min))
            v.scalar_tensor_tensor(lf_e[:], lf_m[:], -2.0, lf_l[:], ALU.mult, ALU.add).then_inc(lf_chain, 1)
            dve.wait_ge(lfg_done, 1)
            step(v.tensor_tensor(lf_n[:], lf_m[:], lf_g[:], ALU.subtract))
            dve.wait_ge(lf_in, 16)
            step(v.tensor_copy(lfS[:, :, PAST:NK], lf_n[:, SEQ:T].rearrange("h (b t) -> h b t", b=DB)))
            one_row = pcol("ln_g", 0)[0:H, :]
            for b in range(DB):
                v.tensor_tensor_scan(lfS[:, b, :], one_row.to_broadcast([H, NK]), lfS[:, b, :], 0.0,
                                     ALU.mult, ALU.subtract).then_inc(ncum_done, 1)
            v.tensor_tensor_scan(lfP[:], one_row.to_broadcast([H, SEQ]), lf_n[:, 0:SEQ], 0.0,
                                 ALU.mult, ALU.subtract).then_inc(ncum_done, 1)
            modulate(4)
            for n in range(U_K + RING, U_FFN2 + RING):
                refill(n, n % RING)
            rest_h(M_S3, kv32, hH, hL)
            ffn(2)
            modulate(5)
            rest_h(M_S4, h32, hH, hL)
            for n in range(U_Q + RING, U_O + RING):
                refill(n, n % RING)

            def row_max(J, w, par2):
                dve.wait_ge(s_mm, J + 1)
                v.tensor_reduce(nmx[:, par2:par2 + 1], bank[par2][:, 0:w], AX.X, ALU.max, negate=True)\
                    .then_inc(nm_done, 1)

            def norm(J, w, par2):
                dve.wait_ge(p_done, J + 1)
                v.reciprocal(rin[:, par2:par2 + 1], rsm[:, par2:par2 + 1]).then_inc(ri_done, 1)
                dve.wait_ge(ri_done, J + 1)
                v.tensor_scalar(sg[:, par2, 0:w], sg[:, par2, 0:w], rin[:, par2:par2 + 1], None, ALU.mult)\
                    .then_inc(pn_done, 1)

            dve.wait_ge(init_pool, 1)
            dve.wait_ge(xa_done, 5 * KT)
            with dve.Fori(0, 4) as i:
                for j in range(8 + 2):
                    if j < 8:
                        row_max(8 * i + j, P * (1 + j % 2), j % 2)
                    if 1 <= j <= 8:
                        norm(8 * i + j - 1, P * (1 + (j - 1) % 2), (j - 1) % 2)
                    if j >= 2:
                        jj = j - 2
                        qt, hh, s = jj % 2, jj // 2 % 2, jj // 4
                        rows = slice(HD * hh, HD * hh + HD)
                        dve.wait_ge(pv_mm, 8 * i + jj + 1)
                        v.tensor_copy(z[rows, 2 * i + s, P * qt:P * qt + P], bank[4 + jj % 2][rows, 0:P])\
                            .then_inc(o_done, 1)
            dve.wait_ge(t_mm, 2 + 32)
            step(v.memset(sg[:, :, NK:T], 0.0))

            def block_q(b, s):
                for hh in range(2):
                    rows = slice(HD * hh, HD * hh + HD)
                    op = v.tensor_copy(qbd[rows, s, :, DS * hh:DS * hh + DS], q32[rows, :, bass.ds(SEQ + DS * b, DS)])
                op.then_inc(qbd_done, 1)

            with dve.Fori(0, 4) as i:
                for s in range(2):
                    dve.wait_ge(s_mm, 32 + 4 * i)
                    block_q(2 * i + s, s)
                for j in range(4 + 2):
                    if j < 4:
                        row_max(32 + 4 * i + j, NK, j % 2)
                    if 1 <= j <= 4:
                        norm(32 + 4 * i + j - 1, NK, (j - 1) % 2)
                    if j >= 2:
                        jj = j - 2
                        b, hf = 2 * i + jj // 2, jj % 2
                        dve.wait_ge(pv_mm, 32 + 4 * i + jj + 1)
                        for hh in range(2):
                            rows = slice(HD * hh, HD * hh + HD)
                            src = bank[4 + jj % 2][rows, 0:P].rearrange("p (k c) -> p k c", k=4)
                            op = v.tensor_copy(z[rows, 4 * hf:4 * hf + 4, bass.ds(SEQ + DS * b, DS)],
                                               src[:, :, DS * hh:DS * hh + DS])
                        op.then_inc(o_done, 1)
            rest_h(M_O, z, hH, hL)
            gate(4)
            with dve.Fori(0, 2) as i:
                for j in range(RING):
                    n = U_O + RING * i + j
                    refill(n + RING, j)
                    dve.wait_ge(w_used, n + 1)
                    add_residual(4, RING * i + j, bank[j], j % 2)
            normalise(5, [6])
            modulate(6)
            rest_h(M_S5, h32, hH, hL)
            ffn(3)
            for k in range(KT):
                c = 6 * KT + k
                dve.wait_ge(zn_done, 4 * 6 + k // 2 + 1)
                op = v.tensor_scalar(z[:, k, :], z[:, k, :], pcol("ln_g", c), pcol("ln_b", c), ALU.mult, ALU.add)
                if k % 2:
                    op.then_inc(y_done, 1)

        @block.tensor
        def _(pe):
            mm = nc.tensor.matmul

            def tile_w(ring, slot, k):
                return ring[:, slot, k * P:(k + 1) * P]

            def unit(n, slot, out, movH, movL, k0=0, nk=8, start=True, stop=True, ready=None):
                pe.wait_ge(w_lo, n + 1)
                for k in range(nk):
                    if ready is not None and k % 2 == 0:
                        pe.wait_ge(hl_done, 4 * ready + k // 2 + 1)
                    for q, (w, m) in enumerate(((wH, movH), (wH, movL), (wL, movH))):
                        op = mm(out, tile_w(w, slot, k), m[:, k0 + k, :],
                                start=start and k == 0 and q == 0, stop=stop and k == nk - 1 and q == 2)
                op.then_inc(w_used, 1)

            def ada_mm(c, tile, waits):
                if not isinstance(c, int) or c > 0:
                    pe.wait_ge(a_mod, c)
                for half in range(2):
                    waits(half)
                    for j in range(4):
                        op = mm(ADB[32 * j:32 * j + 32, 0:256], cact[:, 4 * half + j, :], tile[:, half, j, :],
                                start=half == 0, stop=half == 1)
                op.then_inc(a_mm, 1)

            def ada_tr(c):
                pe.wait_ge(a_ev, c + 1)
                for j in range(2):
                    op = mm(ADB[:, 256 + 16 * j:256 + 16 * j + NG], adaS[:, P * j:P * j + P],
                            con[:, C_SEL9:C_SEL9 + NG], start=True, stop=True)
                op.then_inc(a_tr, 1)

            def ring_waits(c):
                return lambda half: pe.wait_ge(a_in[half], 16 * (c - FIRST_CHUNKS) + 16)

            def ada(c):
                ada_mm(c, araw, ring_waits(c))
                ada_tr(c)

            def stats(n):
                pe.wait_ge(zs_done, KT * (n + 1))
                mm(MEAN[:, 0:T], ones, zs[:], start=True, stop=True).then_inc(mean_ok, 1)
                for q in range(4):
                    pe.wait_ge(sq_done, 4 * n + q + 1)
                    for k in (2 * q, 2 * q + 1):
                        op = mm(VAR[:, 0:T], ones, sq[:, k, :], start=k == 0, stop=k == KT - 1)
                op.then_inc(var_ok, 1)

            def ffn(fi):
                u, (c, na, before, after) = FFN_U[fi], FFN_ADA[fi]
                m = FFN_M[fi]

                def gate_up(i, with_ada):
                    for j in range(2):
                        f, n = 2 * i + j, u + 4 * i + 2 * j
                        pe.wait_ge(prod[fi], f + 1)
                        unit(n, 2 * j, bank[2 * j][:, 0:T], hH, hL, ready=m)
                        unit(n + 1, 2 * j + 1, bank[2 * j + 1][:, 0:T], hH, hL)
                        if with_ada:
                            if j == 0:
                                ada_mm(c + i, araw, ring_waits(c + i))
                            else:
                                ada_tr(c + i)

                with pe.Fori(0, na) as i:
                    gate_up(i, True)
                if na < 11:
                    with pe.Fori(na, 11) as i:
                        gate_up(i, False)
                for j in range(before):
                    ada(c + na + j)
                with pe.Fori(0, 2) as i:
                    for dd in range(4):
                        pe.wait_ge(z_ready, KT * FFN_LN[fi] + 4 * i + dd + 1)
                        for j, (k0, nk) in enumerate(DOWN_K):
                            n = u + 2 * FT + 12 * i + 3 * dd + j
                            pe.wait_ge(hidl[fi], k0 + nk)
                            unit(n, (3 * dd + j) % RING, bank[4 + dd % 2][:, 0:T], hidH, hidL, k0, nk,
                                 start=j == 0, stop=j == 2)
                if after:
                    with pe.Fori(0, after) as i:
                        ada(c + na + before + i)
                stats(FFN_LN[fi])

            pe.wait_ge(con_in, 16)
            pe.wait_ge(cact_ok, 1)
            pe.sem_inc(t_mm, 2)
            for c in range(FIRST_CHUNKS):
                ada_mm(c, land[:, c], lambda half, c=c: pe.wait_ge(land_in[c], 32))
                ada_tr(c)
            ffn(0)
            with pe.Fori(0, 4) as i:
                for j in range(2):
                    n = U_PW1 + 4 * i + 2 * j
                    pe.wait_ge(u_done, 2 * i + j + 1)
                    unit(n, 2 * j, bank[2 * j][:, 0:T], hH, hL, ready=M_S1)
                    unit(n + 1, 2 * j + 1, bank[2 * j + 1][:, 0:T], hH, hL)
                    ada(CH_S1 + 2 * i + j)
            with pe.Fori(0, 4) as i:
                ada(CH_S1 + 8 + i)
            stats(1)
            pe.wait_ge(u_done, 2 + KT)
            with pe.Fori(0, 2) as i:
                for j in range(RING):
                    pe.wait_ge(z_ready, 2 + KT * 2 - 4 + 4 * i + j + 1)
                    unit(U_PW2 + RING * i + j, j, bank[j][:, 0:T], hH, hL, ready=M_PW2)
            stats(2)
            ffn(1)
            pe.wait_ge(wf_in, 16)
            for k in range(KT):
                if k % 2 == 0:
                    pe.wait_ge(hl_done, 4 * M_KV + k // 2 + 1)
                op = mm(bank[6][0:H, 0:T], wf[:, k, :], kv32[:, k, :], start=k == 0, stop=k == KT - 1)
            op.then_inc(f_mm, 1)
            for i in range(2):
                for j in range(RING):
                    if i:
                        pe.wait_ge(kf_done, j + 1)
                    unit(U_K + RING * i + j, j, bank[j][:, 0:T], kvH, kvL, ready=M_KV)
            for half in range(2):
                if half == 0:
                    pe.wait_ge(kf_done, KT)
                for j in range(RING):
                    n = U_V + RING * half + j
                    pe.wait_ge(w_lo, n + 1)
                    for t in range(3):
                        tok = slice(P * t, P * t + P)
                        for kk in range(2):
                            k = 2 * j + kk
                            for q, (h, w) in enumerate(((kvH, wH), (kvH, wL), (kvL, wH))):
                                op = mm(bank[3 * half + t][:, :], h[:, k, tok],
                                        w[:, j, 512 * kk:512 * kk + 512],
                                        start=k == 0 and q == 0, stop=k == KT - 1 and q == 2)
                    op.then_inc(w_used, 1)
            pe.wait_ge(vs_done, 6)
            ffn(2)
            for i in range(2):
                for j in range(RING):
                    if i:
                        pe.wait_ge(q_done, j + 1)
                    unit(U_Q + RING * i + j, j, bank[j][:, 0:T], hH, hL, ready=M_S4)
            pe.wait_ge(q_done, KT)

            def transposes(J, nt, par2):
                pe.wait_ge(pn_done, J + 1)
                for t in range(nt):
                    op = nc.tensor.transpose(bank[2 + par2][:, t * P:t * P + P], sg[:, par2, t * P:t * P + P], ident)
                op.then_inc(t_mm, 1)

            with pe.Fori(0, 4) as i:
                for j in range(8 + 2):
                    if j < 8:
                        J, qt, hh, s = 8 * i + j, j % 2, j // 2 % 2, j // 4
                        rows, w = slice(HD * hh, HD * hh + HD), P * (1 + qt)
                        if j % 4 == 0:
                            pe.wait_ge(pr_in[s], 48 * i + 48)
                            pe.wait_ge(qp_done, 2 * i + s + 1)
                        if j >= 2:
                            pe.wait_ge(p_done, J - 1)
                        mm(bank[qt][:, 0:w], qP[rows, s, P * qt:P * qt + P], KP[rows, s, 0:w],
                           start=True, stop=False)
                        mm(bank[qt][:, 0:w], con[0:1, C_ONE:C_ONE + P], ncP[0:1, s, hh, 0:w],
                           start=False, stop=False)
                        mm(bank[qt][:, w - P:w], ident, con[:, C_MP:C_MP + P], start=False, stop=True)\
                            .then_inc(s_mm, 1)
                    if 1 <= j <= 8:
                        transposes(8 * i + j - 1, 1 + (j - 1) % 2, (j - 1) % 2)
                    if j >= 2:
                        jj = j - 2
                        J, qt, hh, s = 8 * i + jj, jj % 2, jj // 2 % 2, jj // 4
                        rows = slice(HD * hh, HD * hh + HD)
                        pe.wait_ge(pt_done, J + 1)
                        pe.wait_ge(o_done, J + 1)
                        for t in range(1 + qt):
                            op = mm(bank[4 + qt][rows, 0:P], VP[:, s, t, rows], tmp[:, qt, t * P:t * P + P],
                                    start=t == 0, stop=t == qt)
                        op.then_inc(pv_mm, 1)
                ada(CH_S4 + i)
            with pe.Fori(0, 4) as i:
                for j in range(4 + 2):
                    if j < 4:
                        J, hf, s = 32 + 4 * i + j, j % 2, j // 2
                        if hf == 0:
                            pe.wait_ge(st_in[s], 80 * i + 80)
                            pe.wait_ge(qbd_done, 2 * i + s + 1)
                        pe.wait_ge(p_done, J - 1)
                        S = bank[hf]
                        mm(S[:, 0:NK], con[0:H, C_SELH + P * hf:C_SELH + P * hf + P], ncS[:, s, :],
                           start=True, stop=False)
                        for kk in range(4):
                            mm(S[32 * kk:32 * kk + 32, 0:NK], qbd[:, s, 4 * hf + kk, :], KTb[:, s, 4 * hf + kk, :],
                               start=False, stop=False)
                        mm(S[:, PAST:NK], ident, con[:, C_MS:C_MS + DS], start=False, stop=True).then_inc(s_mm, 1)
                    if 1 <= j <= 4:
                        transposes(32 + 4 * i + j - 1, 3, (j - 1) % 2)
                    if j >= 2:
                        jj = j - 2
                        J, hf, s = 32 + 4 * i + jj, jj % 2, jj // 2
                        pe.wait_ge(pt_done, J + 1)
                        pe.wait_ge(o_done, J + 1)
                        for kk in range(4):
                            pair = slice(P * (4 * hf + kk), P * (4 * hf + kk) + P)
                            for t in range(3):
                                rr = P if t < 2 else DS
                                lhs = Vb[:, s, t, pair] if t < 2 else Vn[:, s, pair]
                                c0 = t * P + 32 * kk
                                op = mm(bank[4 + hf][:, 32 * kk:32 * kk + 32], lhs, tmp[0:rr, hf, c0:c0 + 32],
                                        start=t == 0, stop=t == 2)
                        op.then_inc(pv_mm, 1)
                for j in range(2):
                    ada(CH_S4 + 4 + 2 * i + j)
            for i in range(2):
                for j in range(RING):
                    if i:
                        pe.wait_ge(z_ready, 2 + KT * 5 + j + 1)
                    unit(U_O + RING * i + j, j, bank[j][:, 0:T], hH, hL, ready=M_O)
            stats(5)
            ffn(3)


def _tiles(w):
    k, n = w.shape[0] // P, w.shape[1] // P
    return w.reshape(k, P, n, P).transpose(2, 1, 0, 3)


def _cols(a):
    return np.ascontiguousarray(a.reshape(-1, P).T)


def _weight_stream(i):
    W = np.zeros((N_UNITS, P, UNIT), np.float32)

    def ffn(u, l, j):
        gu = W[u:u + 2 * FT].reshape(FT, 2, P, KT, P)
        gu[:, 0] = _tiles(i["ffn_w_gate"][l, j])
        gu[:, 1] = _tiles(i["ffn_w_up"][l, j])
        down = _tiles(i["ffn_w_down"][l, j])
        for q, (k0, nk) in enumerate(DOWN_K):
            W[u + 2 * FT + q:u + FFN_UNITS:3, :, 0:nk * P] = down[:, :, k0:k0 + nk].reshape(KT, P, nk * P)

    def square(u, w):
        W[u:u + KT] = _tiles(w).reshape(KT, P, UNIT)

    ffn(U_FFN0, 0, 0)
    pw1 = _tiles(i["pw1_w"][0]).reshape(2, KT, P, UNIT)
    W[U_PW1:U_PW2:2], W[U_PW1 + 1:U_PW2:2] = pw1[0], pw1[1]
    square(U_PW2, i["pw2_w"][0])
    ffn(U_FFN1, 0, 1)
    square(U_K, i["w_k"])
    W[U_V:U_V + KT] = i["w_v"].reshape(4, 2, P, 2, 512).transpose(3, 0, 2, 1, 4).reshape(KT, P, UNIT)
    ffn(U_FFN2, 1, 0)
    square(U_Q, i["w_q"][0])
    square(U_O, i["w_o"][0])
    ffn(U_FFN3, 1, 1)
    return W


def _constants():
    con = np.zeros((P, N_CONST), np.float32)
    r = np.arange(P)
    con[:, C_ID:C_ID + P] = np.eye(P)
    con[:, C_ONES:C_ONES + P] = 1.0 / D
    for g in range(NG):
        con[32 * np.arange(4) + g, C_SEL9 + g] = 1.0
    con[:, C_ONE:C_ONE + P] = 1.0
    for hf in range(2):
        con[8 * hf + r // DS, C_SELH + P * hf + r] = 1.0
    con[:, C_MP:C_MP + P] = np.where(r[None, :] <= r[:, None], 0.0, NEG)
    con[:, C_MS:C_MS + DS] = np.where(np.arange(DS)[None, :] <= (r % DS)[:, None], 0.0, NEG)
    return con


def kernel(**inputs):
    import concourse.bacc as bacc
    from concourse.bass_utils import run_bass_kernel_spmd as run

    i = {k: np.asarray(v) for k, v in inputs.items()}
    par = np.zeros((P, N_PAR), np.float32)

    def put(name, a):
        a0, n = PAR[name]
        par[:, a0:a0 + n] = a

    one = np.ones((P, KT), np.float32)
    put("ln_g", np.concatenate([one, _cols(i["ln_g"])], 1))
    put("ln_b", np.concatenate([0 * one, _cols(i["ln_b"])], 1))
    put("cln_g", _cols(i["conv_ln_g"]))
    put("cln_b", _cols(i["conv_ln_b"]))
    put("b_ada", np.concatenate([_cols(i["b_ada"][0]), _cols(i["b_ada_kv"]), _cols(i["b_ada"][1])], 1))
    put("pw1_b", _cols(i["pw1_b"]))
    put("pw2_b", _cols(i["pw2_b"]))
    put("dw_b", _cols(i["dw_b"]))
    put("dw_w", i["dw_w"][0].reshape(CK, KT, P).transpose(2, 1, 0).reshape(P, KT * CK))
    par[0:H, PAR["b_f"][0]] = i["b_f"]

    ada = np.concatenate([i["w_ada"][0], i["w_ada_kv"], i["w_ada"][1]], 1)
    ada = ada.reshape(2, 4, P, CHUNKS, 256).transpose(3, 0, 2, 1, 4).reshape(2 * CHUNKS, P, 4, 256)
    x = np.concatenate([i["x_prompt"].reshape(SEQ, D), i["x_sample"].reshape(DB * DS, D)], 0)
    c = np.zeros((32, D), np.float32)
    c[0:1], c[1:NG] = i["c_prompt"], i["c_sample"]

    def fm(a):
        return np.ascontiguousarray(a.reshape(-1, KT, P).transpose(2, 1, 0))

    arrays = {
        "W": _weight_stream(i), "ADA": np.ascontiguousarray(ada), "par_d": par, "con_d": _constants(),
        "x_d": fm(x), "c_d": fm(c),
        "conv_d": fm(i["cache_conv"][0].reshape(DB * HIST, D)).reshape(P, KT, DB, HIST),
        "kt_d": np.ascontiguousarray(
            i["cache_k"].reshape(DB, PAST, KT, P).transpose(0, 3, 2, 1)),
        "v_d": i["cache_v"].reshape(DB, PAST, D),
        "lf_d": np.ascontiguousarray(i["cache_logf"].transpose(2, 0, 1)),
        "wf_d": np.ascontiguousarray(i["w_f"].reshape(KT, P, H).transpose(1, 0, 2)),
    }
    outs = {"y_o": (P, KT, T), "kT_o": (P, KT, T), "v_o": (T, D), "lf_o": (H, T), "conv_o": (P, KT, HIST * NG)}
    nc = bacc.Bacc("TRN2", target_bir_lowering=False, num_devices=1)
    args = [nc.dram_tensor(n, a.shape, F32, kind="ExternalInput").ap() for n, a in arrays.items()]
    args += [nc.dram_tensor(n, s, F32, kind="ExternalOutput").ap() for n, s in outs.items()]
    args.append(nc.dram_tensor("ncp_d", (H, SEQ), F32, kind="Internal").ap())
    args.append(nc.dram_tensor("ncs_d", (H, DB, NK), F32, kind="Internal").ap())
    build_program(nc, *args)
    r = run(nc, [arrays], core_ids=[0]).results[0]

    def rows(a):
        return np.asarray(a).transpose(2, 1, 0).reshape(-1, D)

    y, k, v, lf, cv = rows(r["y_o"]), rows(r["kT_o"]), r["v_o"], r["lf_o"].T, rows(r["conv_o"])
    return (y[:SEQ].reshape(1, SEQ, D), y[SEQ:].reshape(DB, DS, D),
            cv[:HIST].reshape(1, 1, HIST, D),
            k[:SEQ].reshape(1, SEQ, H, HD), v[:SEQ].reshape(1, SEQ, H, HD), lf[:SEQ].reshape(1, SEQ, H),
            cv[HIST:].reshape(1, DB, HIST, D),
            k[SEQ:].reshape(DB, DS, H, HD), v[SEQ:].reshape(DB, DS, H, HD), lf[SEQ:].reshape(DB, DS, H))
```

```python
from contextlib import ExitStack

import numpy as np
import concourse.bass as bass
from concourse import mybir

F32 = mybir.dt.float32
F32R = mybir.dt.float32r
ALU = mybir.AluOpType
ACT = mybir.ActivationFunctionType
AX = mybir.AxisListType

P = 128
D = 1024
KT = D // P
SEQ = 256
DB, DS = 8, 16
T = SEQ + DB * DS
FF = 2816
FT = FF // P
PAST = 256
H, HD = 16, 64
CK = 31
HIST = CK - 1
NG = 1 + DB
ALPHA = float(4 ** 0.25)
EPS = 1e-5
UNIT = 1024
RING = 4
DOWN_K = ((0, 8), (8, 7), (15, 7))
FFN_UNITS = 2 * FT + 3 * KT
NK = PAST + DS
NEG = -1e30

U_FFN0 = 0
U_PW1 = U_FFN0 + FFN_UNITS
U_PW2 = U_PW1 + 2 * KT
U_FFN1 = U_PW2 + KT
U_K = U_FFN1 + FFN_UNITS
U_V = U_K + KT
U_FFN2 = U_V + KT
U_Q = U_FFN2 + FFN_UNITS
U_O = U_Q + KT
U_FFN3 = U_O + KT
N_UNITS = U_FFN3 + FFN_UNITS

V_L0, V_KV, V_L1, N_VEC = 0, 9, 11, 20
CHUNKS = 4 * N_VEC
FIRST_CHUNKS = 8

PAR = {}


def _par(name, n):
    PAR[name] = (PAR["_end"][1], n)
    PAR["_end"] = (0, PAR["_end"][1] + n)


PAR["_end"] = (0, 0)
_par("ln_g", 7 * KT)
_par("ln_b", 7 * KT)
_par("cln_g", KT)
_par("cln_b", KT)
_par("b_ada", 2 * CHUNKS)
_par("pw1_b", 2 * KT)
_par("pw2_b", KT)
_par("dw_b", KT)
_par("dw_w", KT * CK)
_par("b_f", 1)
N_PAR = PAR["_end"][1]

C_ID, C_ONES, C_SEL9, C_SELH, C_MP, C_MS, C_ONE = 0, 128, 256, 265, 521, 649, 665
N_CONST = 793


def build_program(nc, W, ADA, par_d, con_d, x_d, c_d, conv_d, kt_d, v_d, lf_d, wf_d,
                  y_o, kT_o, v_o, lf_o, conv_o, ncp_d, ncs_d):
    with ExitStack() as ctx:
        place = [(nc.sbuf_base + 31) // 32 * 32]

        def at(name, shape, offset, dt=F32):
            return nc.alloc_sbuf_tensor_at(name, shape, dt, offset=offset)

        def sb(name, shape, dt=F32):
            n = int(np.prod(shape[1:])) * 4
            o = place[0]
            place[0] += (n + 31) // 32 * 32
            return at(name, shape, o, dt)

        def sem(name):
            return ctx.enter_context(nc.semaphore(name))

        xa = sb("xa", [P, KT, T])
        z = sb("z", [P, KT, T])
        hH = sb("hH", [P, KT, T], F32R)
        hL = sb("hL", [P, KT, T], F32R)
        raw = sb("raw", [P, RING, UNIT])
        wH = sb("wH", [P, RING, UNIT], F32R)
        wL = sb("wL", [P, RING, UNIT], F32R)
        araw = sb("araw", [P, 2, 4, 256])
        hid = place[0]
        hidH = sb("hidH", [P, FT, T], F32R)
        hidL = sb("hidL", [P, FT, T], F32R)
        BLK = KT * T * 4
        land = at("land", [P, FIRST_CHUNKS, 2, 4, 256], hid)
        sq = at("sq", [P, KT, T], hid + 3 * BLK)
        h32 = at("h32", [P, KT, T], hid + 3 * BLK)
        uP = at("uP", [P, KT, HIST + SEQ], hid)
        uS = at("uS", [P, KT, DB, HIST + DS], hid + KT * (HIST + SEQ) * 4)
        conv_st = at("conv_st", [P, KT, HIST * NG], hid + 2 * BLK)
        conv_in = at("conv_in", [P, KT, DB, HIST], hid + 4 * BLK)
        kvH = at("kvH", [P, KT, T], hid, F32R)
        kvL = at("kvL", [P, KT, T], hid + BLK, F32R)
        kv32 = at("kv32", [P, KT, T], hid + 2 * BLK)
        kF = at("kF", [P, KT, T], hid + 3 * BLK)
        vS = at("vS", [P, 3, D], hid + 4 * BLK)
        hH_off = hH.manual_sbuf_range[0]
        lfS = at("lfS", [H, DB, NK], hH_off)
        lfP = at("lfP", [H, SEQ], hH_off + DB * NK * 4)
        hL_off = hL.manual_sbuf_range[0]
        lf_l = at("lf_l", [H, T], hL_off)
        lf_m = at("lf_m", [H, T], hL_off + 4 * T)
        lf_e = at("lf_e", [H, T], hL_off + 8 * T)
        lf_g = at("lf_g", [H, T], hL_off + 12 * T)
        lf_n = at("lf_n", [H, T], hL_off + 16 * T)
        q32 = at("q32", [P, KT, T], hid)
        o = hid + BLK
        qP = at("qP", [P, 2, 2, SEQ], o)
        VP = at("VP", [P, 2, 2, P], o + 4096)
        KP = at("KP", [P, 2, SEQ], o + 6144)
        knS = at("knS", [P, 2, KT, DS], o + 8192)
        Kn = at("Kn", [P, KT, DB * DS], o + 12288)
        KTb = at("KTb", [P, 2, KT, PAST], o + 16384)
        Vb = at("Vb", [P, 2, 2, D], o + 32768)
        o += 49152
        prS = at("prS", [P, 4, 512], hH_off)
        PT = at("PT", [P, 2, 512], hH_off + 8192)
        Vn = at("Vn", [DS, 2, D], hL_off)
        assert o <= hid + 2 * FT * T * 4
        par = sb("par", [P, N_PAR])
        con = sb("con", [P, N_CONST])
        mods = sb("mods", [P, KT * N_VEC, NG])
        craw = sb("craw", [P, KT, 32])
        cact = sb("cact", [P, KT, 32])
        wf = sb("wf", [P, KT, H])
        Am = sb("Am", [P, 2, KT, NG])
        Bm = sb("Bm", [P, 2, KT, NG])
        Gm = sb("Gm", [P, 2, KT, NG])
        gA = sb("gA", [P, 7 * KT])
        bA = sb("bA", [P, 7 * KT])
        sg = sb("sg", [P, 2, T])
        tmp = sb("tmp", [P, 2, T])
        epS = sb("epS", [P, 2, DB * DS])
        zs = sb("zs", [P, T])
        ve = sb("ve", [P, T])
        rstd = sb("rstd", [P, T])
        sd = sb("sd", [P, T])
        adaS = sb("adaS", [P, 256])
        qbd = sb("qbd", [P, 2, KT, 2 * DS])
        nmx = sb("nmx", [P, 4, 2])
        rsm = sb("rsm", [P, 4, 2])
        rin = sb("rin", [P, 4, 2])
        ncS = at("ncS", [H, 2, NK], sg.manual_sbuf_range[0])
        om = at("om", [P, 2, P], tmp.manual_sbuf_range[0])
        ncP = at("ncP", [1, 2, 2, SEQ], zs.manual_sbuf_range[0])
        assert place[0] <= nc.sbuf_usable_end, place[0] - nc.sbuf_usable_end
        ident = con[:, C_ID:C_ID + P]
        ones = con[:, C_ONES:C_ONES + P]

        bank = [ctx.enter_context(nc.psum_tensor(f"bank{i}", [P, 512], F32)) for i in range(8)]
        MEAN, VAR, ADB = bank[6], bank[5], bank[7]

        def pcol(name, c=0, n=1):
            a = PAR[name][0]
            return par[:, bass.ds(a + c, n)]

        par_in, wf_in, con_in, x_in, c_in, convc_in, lf_in, conv_out = (sem(n) for n in (
            "par_in", "wf_in", "con_in", "x_in", "c_in", "convc_in", "lf_in", "conv_out"))
        land_in = [sem(f"land_in{i}") for i in range(FIRST_CHUNKS)]
        w_in = [sem(f"w_in{i}") for i in range(RING)]
        w_hi = sem("w_hi")
        w_lo = sem("w_lo")
        w_used = sem("w_used")
        a_in = [sem(f"a_in{i}") for i in range(2)]
        a_mm, a_ev, a_tr, a_mod = (sem(n) for n in ("a_mm", "a_ev", "a_tr", "a_mod"))
        cact_ok, init_dve, init_pool = sem("cact_ok"), sem("init_dve"), sem("init_pool")
        z_ready = sem("z_ready")
        zs_done, mean_ok, zc_done, sq_done, var_ok, ve_done, sd_done, rs_done, zn_done = (sem(n) for n in (
            "zs_done", "mean_ok", "zc_done", "sq_done", "var_ok", "ve_done", "sd_done", "rs_done", "zn_done"))
        ab_done, hp_done, hs1_done, hs_done, hh_done, hl_done, xa_done = (sem(n) for n in (
            "ab_done", "hp_done", "hs1_done", "hs_done", "hh_done", "hl_done", "xa_done"))
        sm_done = sem("sm_done")
        gm_done = sem("gm_done")
        ep1_done = sem("ep1_done")
        sg_done = [sem(f"sg_done{i}") for i in range(4)]
        prod = [sem(f"prod{i}") for i in range(4)]
        hidh = [sem(f"hidh{i}") for i in range(4)]
        hidl = [sem(f"hidl{i}") for i in range(4)]
        hist_ok, sig_done, u_done, tapP, tapS, convst_ok = (sem(n) for n in (
            "hist_ok", "sig_done", "u_done", "tapP", "tapS", "convst_ok"))
        silu_done = sem("silu_done")
        kf_done, vs_done, f_mm, lf_chain, lfe_done, lfg_done, ncum_done, lfo_done = (sem(n) for n in (
            "kf_done", "vs_done", "f_mm", "lf_chain", "lfe_done", "lfg_done", "ncum_done", "lfo_done"))
        kv_out, nc_out, fin_out = sem("kv_out"), sem("nc_out"), sem("fin_out")
        q_done, qp_done, qbd_done = sem("q_done"), sem("qp_done"), sem("qbd_done")
        kn_in = sem("kn_in")
        kp_in, vp_in, sk_in, sv_in = ([sem(f"{n}{i}") for i in range(2)] for n in ("kp_in", "vp_in", "sk_in", "sv_in"))
        om_done, o_mm = sem("om_done"), sem("o_mm")
        s_mm, nm_done, p_done, ri_done, pn_done, t_mm, pt_done, pv_mm, o_done = (sem(n) for n in (
            "s_mm", "nm_done", "p_done", "ri_done", "pn_done", "t_mm", "pt_done", "pv_mm", "o_done"))
        y_done = sem("y_done")

        GATE_VEC = [V_L0 + 2, V_L0 + 5, V_L0 + 8, V_L1 + 2, V_L1 + 5, V_L1 + 8]
        MODS = [(-1, 0, V_L0, False), (0, 1, V_L0 + 3, False), (2, 2, V_L0 + 6, False),
                (3, 3, V_KV, True), (3, 3, V_L1, False), (4, 4, V_L1 + 3, False), (5, 5, V_L1 + 6, False)]
        M_S0, M_S1, M_PW2, M_S2, M_KV, M_S3, M_S4, M_O, M_S5 = range(9)
        FFN_M = [M_S0, M_S2, M_S3, M_S5]
        FFN_U = [U_FFN0, U_FFN1, U_FFN2, U_FFN3]
        FFN_LN = [0, 3, 4, 6]
        FFN_SUB = [0, 2, 3, 5]
        FFN_ADA = [(8, 11, 8), (35, 11, 8), (54, 11, 8), (77, 3, 0)]
        CH_S1, CH_S4 = 27, 73
        JP, JS = 16, 16

        def streams(ap):
            return ap.rearrange("p k (b t) -> p k b t", b=DB)

        def job(kind, i, j):
            return 4 * i + j + (JP if kind == "s" else 0)

        def earlier(kind, i, j):
            if j >= 0:
                return kind, i, j
            if isinstance(i, int) and i == 0:
                return None if kind == "p" else ("p", JP // 4 - 1, j + 4)
            return kind, i - 1, j + 4

        def width(kind, j):
            return P * (1 + j % 2) if kind == "p" else NK

        def over_tokens(ap, k):
            return ap.unsqueeze(3).to_broadcast([P, k, DB, DS])

        block = ctx.enter_context(nc.Block())

        @block.sync
        def _(sp):
            def w_unit(n, slot, wait=True):
                if wait:
                    sp.wait_ge(w_lo, n - (RING - 1))
                sp.dma_start(raw[:, slot, :], W[n]).then_inc(w_in[slot], 16)

            def w_units(n, count, wait=True):
                for j in range(count):
                    w_unit(n + j, j % RING, wait)

            def ada_chunk(c):
                sp.wait_ge(a_mm, c)
                for j in range(2):
                    sp.dma_start(araw[:, j], ADA[2 * c + j]).then_inc(a_in[j], 16)

            def ffn(fi):
                u, (c, na, nd) = FFN_U[fi], FFN_ADA[fi]
                if fi != 2:
                    w_units(u, RING, wait=fi > 0)
                with sp.Fori(0, na) as i:
                    ada_chunk(c + i)
                    w_units(u + RING + RING * i, RING)
                if na < 11:
                    with sp.Fori(na, 11) as i:
                        w_units(u + RING + RING * i, RING)
                if nd:
                    with sp.Fori(0, 2) as i:
                        for dd in range(4):
                            ada_chunk(c + na + 4 * i + dd)
                            for j in range(3):
                                w_unit(u + 48 + 12 * i + 3 * dd + j, (3 * dd + j) % RING)
                else:
                    with sp.Fori(0, 5) as i:
                        w_units(u + 48 + RING * i, RING)

            sp.dma_start(craw[:], c_d).then_inc(c_in, 16)
            sp.dma_start(par[:], par_d).then_inc(par_in, 16)
            sp.dma_start(con[:], con_d).then_inc(con_in, 16)
            sp.dma_start(z[:], x_d).then_inc(x_in, 16)
            for c in range(FIRST_CHUNKS):
                sp.dma_start(land[:, c, 0], ADA[2 * c]).then_inc(land_in[c], 16)
                sp.dma_start(land[:, c, 1], ADA[2 * c + 1]).then_inc(land_in[c], 16)
            sp.dma_start(wf[:], wf_d).then_inc(wf_in, 16)
            ffn(0)
            sp.wait_ge(xa_done, 2 * KT)
            sp.dma_start(conv_in[:], conv_d).then_inc(convc_in, 16)
            with sp.Fori(0, 4) as i:
                ada_chunk(CH_S1 + 2 * i)
                ada_chunk(CH_S1 + 2 * i + 1)
                w_units(U_PW1 + RING + RING * i, RING)
            w_units(U_PW2 + RING, RING)
            sp.wait_ge(convst_ok, 1)
            sp.dma_start(conv_o, conv_st[:]).then_inc(conv_out, 16)
            ffn(1)
            sp.dma_start(lfS[:, :, 0:PAST], lf_d).then_inc(lf_in, 16)
            w_units(U_K + RING, RING)
            sp.wait_ge(ncum_done, NG)
            sp.dma_start(ncs_d, lfS[:]).then_inc(nc_out, 16)
            sp.dma_start(ncp_d, lfP[:]).then_inc(nc_out, 16)
            sp.dma_start(lf_o, lf_n[:]).then_inc(nc_out, 16)
            w_units(U_V, 3 * RING)
            sp.wait_ge(kf_done, KT)
            sp.dma_start(kT_o, kF[:]).then_inc(kv_out, 16)
            sp.wait_ge(vs_done, 6)
            sp.dma_start(v_o.rearrange("(t p) n -> p t n", p=P), vS[:]).then_inc(kv_out, 16)
            ffn(2)
            w_units(U_Q + RING, RING)
            sp.wait_ge(kv_out, 32)
            sp.wait_ge(nc_out, 48)
            sp.wait_ge(hl_done, 4 * M_S4 + 4)
            sp.wait_ge(xa_done, 5 * KT)

            def prompt_k(pr, s):
                sp.dma_start(KP[:, s], kT_o[:, pr, 0:SEQ]).then_inc(kp_in[s], 16)
                sp.dma_start(ncP[:, s], ncp_d[bass.ds(2 * pr, 2), :].rearrange("(a h) s -> a h s", a=1))\
                    .then_inc(kp_in[s], 16)

            def prompt_v(pr, s):
                sp.dma_start(VP[:, s], v_o[0:SEQ, bass.ds(P * pr, P)].rearrange("(t p) n -> p t n", p=P))\
                    .then_inc(vp_in[s], 16)

            def stream_k(b, s):
                sp.dma_start(KTb[:, s], kt_d[b]).then_inc(sk_in[s], 16)
                sp.dma_start(ncS[:, s], ncs_d[:, b, :]).then_inc(sk_in[s], 16)

            def stream_v(b, s):
                sp.dma_start(Vb[:, s], v_d[b].rearrange("(t p) n -> p t n", p=P)).then_inc(sv_in[s], 16)
                sp.dma_start(Vn[:, s], v_o[bass.ds(SEQ + DS * b, DS), :]).then_inc(sv_in[s], 16)

            def next_k(b, s):
                sp.wait_ge(s_mm, JP + 2 * b - 2)
                stream_k(b, s)

            def next_v(b, s):
                sp.wait_ge(pv_mm, JP + 2 * b - 2)
                stream_v(b, s)

            for s in range(2):
                prompt_k(s, s)
                prompt_v(s, s)
            sp.dma_start(Kn[:], kT_o[:, :, SEQ:T]).then_inc(kn_in, 16)
            w_units(U_O, RING)
            stream_k(0, 0)
            stream_k(1, 1)
            sp.wait_ge(q_done, KT)
            stream_v(0, 0)
            stream_v(1, 1)
            ada_chunk(CH_S4)
            with sp.Fori(0, 3) as i:
                for s in range(2):
                    sp.wait_ge(s_mm, 4 * i + 2 * s + 2)
                    prompt_k(2 * i + 2 + s, s)
                ada_chunk(CH_S4 + 1 + i)
                for s in range(2):
                    sp.wait_ge(pv_mm, 4 * i + 2 * s + 2)
                    prompt_v(2 * i + 2 + s, s)
            next_k(2, 0)
            next_k(3, 1)
            next_v(2, 0)
            with sp.Fori(1, 3) as i:
                next_k(2 * i + 2, 0)
                next_v(2 * i + 1, 1)
                next_k(2 * i + 3, 1)
                next_v(2 * i + 2, 0)
            next_v(7, 1)
            w_units(U_O + RING, RING)
            ffn(3)
            for g in range(4):
                sp.wait_ge(y_done, g + 1)
                sp.dma_start(y_o[:, 2 * g:2 * g + 2], z[:, 2 * g:2 * g + 2]).then_inc(fin_out, 16)
            sp.wait_ge(fin_out, 64)
            sp.wait_ge(conv_out, 16)

        @block.gpsimd
        def _(pool):
            g = nc.gpsimd
            g.memset(qbd[:], 0.0).then_inc(init_pool, 1)

            def sums(n):
                for k in range(KT):
                    pool.wait_ge(z_ready, 2 + KT * n + k + 1)
                    if k == 0:
                        op = g.tensor_copy(zs[:], z[:, 0, :])
                    else:
                        pool.wait_ge(zs_done, KT * n + k)
                        op = g.tensor_tensor(zs[:], zs[:], z[:, k, :], ALU.add)
                    op.then_inc(zs_done, 1)

            def modulate(mi):
                n, _, _, kv = MODS[mi]
                dst = kv32 if mi in (3, 4) else h32
                pool.wait_ge(ab_done, mi + 1)
                for q in range(4):
                    ks = slice(2 * q, 2 * q + 2)
                    if n >= 0:
                        pool.wait_ge(zn_done, 4 * n + q + 1)
                    else:
                        pool.wait_ge(x_in, 16)
                    dd = streams(dst[:, ks, SEQ:T])
                    g.tensor_tensor(dd, streams(z[:, ks, SEQ:T]),
                                    over_tokens(Am[:, mi % 2, ks, 1:NG], 2), ALU.mult).then_inc(hs1_done, 1)
                    pool.wait_ge(hs1_done, 4 * mi + q + 1)
                    g.tensor_tensor(dd, dd, over_tokens(Bm[:, mi % 2, ks, 1:NG], 2), ALU.add)\
                        .then_inc(hs_done, 1)

            def residual(e):
                for k in range(KT):
                    c = e * KT + k
                    g.tensor_scalar(xa[:, k, :], z[:, k, :], gA[:, c:c + 1], bA[:, c:c + 1],
                                    ALU.mult, ALU.add).then_inc(xa_done, 1)

            modulate(0)
            pool.wait_ge(init_dve, 1)
            residual(0)
            sums(0)
            modulate(1)
            residual(1)
            g.memset(uP[:, :, 0:HIST], 0.0).then_inc(hist_ok, 1)
            pool.wait_ge(convc_in, 16)
            for k in range(KT):
                op = g.tensor_copy(uS[:, k, :, 0:HIST], conv_in[:, k])
            op.then_inc(hist_ok, 1)
            sums(1)
            for k in range(KT):
                g.tensor_copy(conv_st[:, k, 0:HIST], uP[:, k, SEQ:SEQ + HIST])
                op = g.tensor_copy(conv_st[:, k, HIST:].rearrange("p (b t) -> p b t", b=DB),
                                   uS[:, k, :, DS:DS + HIST])
            op.then_inc(convst_ok, 1)
            sums(2)
            modulate(2)
            residual(2)
            sums(3)
            modulate(3)
            pool.wait_ge(f_mm, 1)
            pool.wait_ge(hl_done, 4 * M_KV + 4)
            modulate(4)
            residual(3)
            sums(4)
            modulate(5)
            residual(4)

            def pair_q(pr, s):
                for hh in range(2):
                    rows = slice(HD * hh, HD * hh + HD)
                    g.tensor_copy(qP[rows, s, hh, :], q32[rows, pr, 0:SEQ]).then_inc(qp_done, 1)
                    pool.wait_ge(qp_done, 2 * pr + hh + 1)

            def block_q(b, s):
                g.tensor_copy(knS[:, s], Kn[:, :, bass.ds(DS * b, DS)]).then_inc(qbd_done, 1)
                pool.wait_ge(qbd_done, 3 * b + 1)
                for hh in range(2):
                    rows = slice(HD * hh, HD * hh + HD)
                    g.tensor_copy(qbd[rows, s, :, DS * hh:DS * hh + DS], q32[rows, :, bass.ds(SEQ + DS * b, DS)])\
                        .then_inc(qbd_done, 1)
                    pool.wait_ge(qbd_done, 3 * b + hh + 2)

            g.memset(qP[:], 0.0).then_inc(init_pool, 1)
            pool.wait_ge(init_pool, 2)
            for s in range(2):
                pool.wait_ge(q_done, s + 1)
                pair_q(s, s)
            pool.wait_ge(q_done, KT)
            pool.wait_ge(kn_in, 16)
            for s in range(2):
                block_q(s, s)
            with pool.Fori(0, 3) as i:
                for s in range(2):
                    pool.wait_ge(s_mm, 4 * i + 2 * s + 2)
                    pair_q(2 * i + 2 + s, s)
            with pool.Fori(0, 3) as i:
                for s in range(2):
                    pool.wait_ge(s_mm, JP + 4 * i + 2 * s + 2)
                    block_q(2 * i + 2 + s, s)
            sums(5)
            modulate(6)
            residual(5)
            sums(6)

        @block.scalar
        def _(act):
            a = nc.scalar

            def refill(n, slot, wait_used=True):
                if wait_used:
                    act.wait_ge(w_used, n - (RING - 1))
                act.wait_ge(w_in[slot], landed(n, slot))
                a.activation(wH[:, slot, :], raw[:, slot, :], ACT.Copy).then_inc(w_hi, 1)

            def landed(n, slot):
                return 4 * n - 4 * slot + 16

            def ada_evac(c):
                act.wait_ge(a_mm, c + 1)
                a.activation(adaS[:], ADB[:, 0:256], ACT.Copy).then_inc(a_ev, 1)

            def ada_mods(c):
                act.wait_ge(a_tr, c + 1)
                for j in range(2):
                    op = a.activation(mods[:, 2 * c + j, :], ADB[:, 256 + 16 * j:256 + 16 * j + NG], ACT.Identity,
                                      bias=pcol("b_ada", 2 * c + j))
                op.then_inc(a_mod, 1)

            def squares(n):
                a.preload_act_table(ACT.Sqrt)
                for q in range(4):
                    act.wait_ge(zc_done, 4 * n + q + 1)
                    a.activation(sq[:, 2 * q:2 * q + 2, :], z[:, 2 * q:2 * q + 2, :], ACT.Square)\
                        .then_inc(sq_done, 1)
                act.wait_ge(ve_done, n + 1)
                a.activation(sd[:], ve[:], ACT.Sqrt).then_inc(sd_done, 1)

            def split_h(m, mi, src, dst):
                for q in range(4):
                    if mi is not None:
                        act.wait_ge(hp_done, 4 * mi + q + 1)
                        act.wait_ge(hs_done, 4 * mi + q + 1)
                    a.activation(dst[:, 2 * q:2 * q + 2, :], src[:, 2 * q:2 * q + 2, :], ACT.Copy)\
                        .then_inc(hh_done, 1)

            def ffn(fi):
                u, (c, na, nd) = FFN_U[fi], FFN_ADA[fi]

                def gate_up(i, with_ada):
                    for j in range(2):
                        f, n = 2 * i + j, u + 4 * i + 2 * j
                        act.wait_ge(w_used, n + 1)
                        act.wait_ge(prod[fi], f + 1)
                        a.activation(sg[:, j, :], bank[2 * j][:, 0:T], ACT.Silu).then_inc(sg_done[fi], 1)
                        refill(n + RING, 2 * j)
                        refill(n + RING + 1, 2 * j + 1)
                        act.wait_ge(prod[fi], f + 3)
                        a.activation(hidH[:, f, :], tmp[:, j, :], ACT.Copy).then_inc(hidh[fi], 1)
                        if with_ada:
                            if j == 0:
                                ada_evac(c + i)
                            else:
                                ada_mods(c + i)

                with act.Fori(0, na) as i:
                    gate_up(i, True)
                if na < 11:
                    with act.Fori(na, 11) as i:
                        gate_up(i, False)
                if nd:
                    with act.Fori(0, 2) as i:
                        for dd in range(4):
                            for j in range(3):
                                refill(u + 48 + 12 * i + 3 * dd + j, (3 * dd + j) % RING)
                                if j == 0:
                                    ada_evac(c + na + 4 * i + dd)
                            ada_mods(c + na + 4 * i + dd)
                else:
                    with act.Fori(0, 5) as i:
                        for j in range(RING):
                            refill(u + 48 + RING * i + j, j)
                squares(FFN_LN[fi])

            act.wait_ge(c_in, 16)
            a.activation(cact[:], craw[:], ACT.Silu).then_inc(cact_ok, 1)
            act.wait_ge(par_in, 16)
            act.wait_ge(con_in, 16)
            for c in range(FIRST_CHUNKS):
                ada_evac(c)
                ada_mods(c)
                if c < RING:
                    refill(c, c, wait_used=False)
            split_h(M_S0, 0, h32, hH)
            ffn(0)
            split_h(M_S1, 1, h32, hH)
            with act.Fori(0, 4) as i:
                for j in range(2):
                    n = U_PW1 + 4 * i + 2 * j
                    act.wait_ge(w_used, n + 2)
                    act.wait_ge(u_done, 2 * i + j + 1)
                    a.activation(sg[:, j, :], bank[2 * j + 1][:, 0:T], ACT.Sigmoid,
                                 bias=pcol("pw1_b", KT + 2 * i + j)).then_inc(sig_done, 1)
                    refill(n + RING, 2 * j)
                    refill(n + RING + 1, 2 * j + 1)
                    ada_evac(CH_S1 + 2 * i + j)
                    ada_mods(CH_S1 + 2 * i + j)
            squares(1)
            for k in range(KT):
                act.wait_ge(zn_done, 4 * 1 + k // 2 + 1)
                a.activation(h32[:, k, :], z[:, k, :], ACT.Silu, bias=pcol("cln_b", k),
                             scale=pcol("cln_g", k)).then_inc(silu_done, 1)
            act.wait_ge(silu_done, KT)
            split_h(M_PW2, None, h32, hH)
            with act.Fori(0, 2) as i:
                for j in range(RING):
                    refill(U_PW2 + RING + RING * i + j, j)
            squares(2)
            split_h(M_S2, 2, h32, hH)
            act.wait_ge(conv_out, 16)
            ffn(1)
            split_h(M_KV, 3, kv32, kvH)
            act.wait_ge(lf_chain, 1)
            a.activation(lf_e[:], lf_e[:], ACT.Exp, scale=-1.0).then_inc(lfe_done, 1)
            act.wait_ge(lfe_done, 1)
            a.activation(lf_g[:], lf_e[:], ACT.Ln, bias=1.0).then_inc(lfg_done, 1)
            with act.Fori(0, 2) as i:
                for j in range(RING):
                    n = U_K + RING * i + j
                    act.wait_ge(w_used, n + 1)
                    a.activation(kF[:, RING * i + j, :], bank[j][:, 0:T], ACT.Copy).then_inc(kf_done, 1)
                    refill(n + RING, j)
            for half in range(2):
                for j in range(RING):
                    n = U_V + RING * half + j
                    refill(n + RING, j)
                for t in range(3):
                    a.activation(vS[:, t, half * 512:(half + 1) * 512], bank[3 * half + t][:, :], ACT.Copy)\
                        .then_inc(vs_done, 1)
            act.wait_ge(nc_out, 48)
            split_h(M_S3, 4, kv32, hH)
            act.wait_ge(kv_out, 32)
            ffn(2)
            split_h(M_S4, 5, h32, hH)
            act.wait_ge(xa_done, 5 * KT)
            with act.Fori(0, 2) as i:
                for j in range(RING):
                    n = U_Q + RING * i + j
                    act.wait_ge(w_used, n + 1)
                    a.activation(q32[:, RING * i + j, :], bank[j][:, 0:T], ACT.Copy, scale=HD ** -0.5)\
                        .then_inc(q_done, 1)
                    refill(n + RING, j)

            def soft(kind, i, j):
                J, slot = job(kind, i, j), j % 4
                act.wait_ge(nm_done, J + 1)
                if not isinstance(J, int) or J >= 4:
                    act.wait_ge(t_mm, J - 3)
                parts = 2 if kind == "p" else 1
                w = width(kind, j)
                for hh in range(parts):
                    op = a.activation(prS[:, slot, hh * w:hh * w + w], bank[slot][:, hh * w:hh * w + w], ACT.Exp,
                                      bias=nmx[:, slot, hh:hh + 1], accum_out=rsm[:, slot, hh:hh + 1])
                op.then_inc(p_done, 1)

            def evac_t(kind, i, j):
                J, w = job(kind, i, j), 2 * width("p", j) if kind == "p" else 3 * P
                act.wait_ge(t_mm, J + 1)
                a.activation(PT[:, j % 2, 0:w], bank[4 + j % 2][:, 0:w], ACT.Copy).then_inc(pt_done, 1)

            def body(kind, i, with_ada=False, scores=True):
                for j in range(4):
                    if scores:
                        soft(kind, i, j)
                    before = earlier(kind, i, j - 2)
                    if before and (scores or j < 2):
                        evac_t(*before)
                    if with_ada and j == 2:
                        ada_evac(CH_S4 + i)
                    if with_ada and j == 3:
                        ada_mods(CH_S4 + i)

            act.wait_ge(q_done, KT)
            body("p", 0, True)
            with act.Fori(1, 4) as i:
                body("p", i, True)
            body("s", 0)
            with act.Fori(1, 4) as i:
                body("s", i)
            body("s", 4, scores=False)
            act.wait_ge(o_done, JP + JS)
            split_h(M_O, None, z, hH)
            with act.Fori(0, 2) as i:
                for j in range(RING):
                    refill(U_O + RING + RING * i + j, j)
            squares(5)
            split_h(M_S5, 6, h32, hH)
            ffn(3)

        @block.vector
        def _(dve):
            v = nc.vector
            small = [0]

            def step(op):
                small[0] += 1
                op.then_inc(sm_done, 1)
                dve.wait_ge(sm_done, small[0])

            def refill(n, slot):
                dve.wait_ge(w_hi, n + 1)
                v.tensor_tensor(wL[:, slot, :], raw[:, slot, :], wH[:, slot, :].bitcast(F32), ALU.subtract)\
                    .then_inc(w_lo, 1)

            def normalise(n, meanwhile=()):
                dve.wait_ge(mean_ok, n + 1)
                for q in range(4):
                    ks = slice(2 * q, 2 * q + 2)
                    v.tensor_tensor(z[:, ks, :], z[:, ks, :],
                                    MEAN[:, 0:T].unsqueeze(1).to_broadcast([P, 2, T]), ALU.subtract)\
                        .then_inc(zc_done, 1)
                for mi in meanwhile:
                    prepare(mi)
                dve.wait_ge(var_ok, n + 1)
                v.tensor_scalar(ve[:], VAR[:, 0:T], EPS, None, ALU.add).then_inc(ve_done, 1)
                dve.wait_ge(sd_done, n + 1)
                v.reciprocal(rstd[:], sd[:]).then_inc(rs_done, 1)
                dve.wait_ge(rs_done, n + 1)
                for q in range(4):
                    ks = slice(2 * q, 2 * q + 2)
                    v.tensor_tensor(z[:, ks, :], z[:, ks, :],
                                    rstd[:].unsqueeze(1).to_broadcast([P, 2, T]), ALU.mult).then_inc(zn_done, 1)

            def prepare(mi):
                _, e, vec, _ = MODS[mi]
                dve.wait_ge(a_mod, 4 * (vec + 2))
                shift, scale = mods[:, KT * vec:KT * vec + KT, :], mods[:, KT * vec + KT:KT * vec + 2 * KT, :]
                gg = pcol("ln_g", e * KT, KT).unsqueeze(2).to_broadcast([P, KT, NG])
                bb = pcol("ln_b", e * KT, KT).unsqueeze(2).to_broadcast([P, KT, NG])
                step(v.scalar_tensor_tensor(Am[:, mi % 2], scale, 1.0, gg, ALU.add, ALU.mult))
                step(v.scalar_tensor_tensor(Bm[:, mi % 2], scale, 1.0, bb, ALU.add, ALU.mult))
                v.tensor_tensor(Bm[:, mi % 2], Bm[:, mi % 2], shift, ALU.add).then_inc(ab_done, 1)

            def modulate(mi):
                n, _, _, kv = MODS[mi]
                dst = kv32 if mi in (3, 4) else h32
                dve.wait_ge(ab_done, mi + 1)
                if n >= 0:
                    dve.wait_ge(zn_done, 4 * n + 4)
                else:
                    dve.wait_ge(x_in, 16)
                for k in range(KT):
                    op = v.tensor_scalar(dst[:, k, 0:SEQ], z[:, k, 0:SEQ], Am[:, mi % 2, k, 0:1],
                                         Bm[:, mi % 2, k, 0:1], ALU.mult, ALU.add)
                    if k % 2:
                        op.then_inc(hp_done, 1)

            def rest_h(m, src, hi, lo):
                for q in range(4):
                    ks = slice(2 * q, 2 * q + 2)
                    dve.wait_ge(hh_done, 4 * m + q + 1)
                    v.tensor_tensor(lo[:, ks, :], src[:, ks, :], hi[:, ks, :].bitcast(F32), ALU.subtract)\
                        .then_inc(hl_done, 1)

            def gate(r):
                vec = GATE_VEC[r]
                dve.wait_ge(a_mod, 4 * (vec + 1))
                v.tensor_scalar(Gm[:, r % 2], mods[:, KT * vec:KT * vec + KT, :], 1.0,
                                1.0 if r in (1, 4) else 0.5, ALU.add, ALU.mult).then_inc(gm_done, 1)
                dve.wait_ge(gm_done, r + 1)

            def add_residual(r, d, src, par2, bias=None):
                G = Gm[:, r % 2]
                if bias is None:
                    v.scalar_tensor_tensor(z[:, d, 0:SEQ], src[:, 0:SEQ], G[:, d, 0:1], xa[:, d, 0:SEQ],
                                           ALU.mult, ALU.add)
                    v.tensor_tensor(epS[:, par2].rearrange("p (b t) -> p b t", b=DB),
                                    src[:, SEQ:T].rearrange("p (b t) -> p b t", b=DB),
                                    G[:, d, 1:NG].unsqueeze(2).to_broadcast([P, DB, DS]), ALU.mult)\
                        .then_inc(ep1_done, 1)
                else:
                    v.tensor_scalar(z[:, d, 0:SEQ], src[:, 0:SEQ], bias, G[:, d, 0:1], ALU.add, ALU.mult)
                    v.scalar_tensor_tensor(epS[:, par2].rearrange("p (b t) -> p b t", b=DB),
                                           src[:, SEQ:T].rearrange("p (b t) -> p b t", b=DB), bias,
                                           G[:, d, 1:NG].unsqueeze(2).to_broadcast([P, DB, DS]),
                                           ALU.add, ALU.mult).then_inc(ep1_done, 1)
                dve.wait_ge(ep1_done, KT * r + d + 1)
                if bias is not None:
                    v.tensor_tensor(z[:, d, 0:SEQ], z[:, d, 0:SEQ], xa[:, d, 0:SEQ], ALU.add)
                v.tensor_tensor(z[:, d, SEQ:T], epS[:, par2], xa[:, d, SEQ:T], ALU.add).then_inc(z_ready, 1)

            def ffn(fi):
                u, (c, na, nd) = FFN_U[fi], FFN_ADA[fi]
                r, n_ln = FFN_SUB[fi], FFN_LN[fi]
                dve.sem_inc(prod[fi], 2)
                with dve.Fori(0, 11) as i:
                    for j in range(2):
                        f, n = 2 * i + j, u + 4 * i + 2 * j
                        dve.wait_ge(w_used, n + 2)
                        dve.wait_ge(sg_done[fi], f + 1)
                        v.tensor_tensor(tmp[:, j, :], sg[:, j, :], bank[2 * j + 1][:, 0:T], ALU.mult)\
                            .then_inc(prod[fi], 1)
                        refill(n + RING, 2 * j)
                        refill(n + RING + 1, 2 * j + 1)
                        dve.wait_ge(hidh[fi], f + 1)
                        v.tensor_tensor(hidL[:, f, :], tmp[:, j, :], hidH[:, f, :].bitcast(F32), ALU.subtract)\
                            .then_inc(hidl[fi], 1)
                gate(r)
                dve.wait_ge(xa_done, KT * (r + 1))

                def down(i, dd, n_refill):
                    n = u + 2 * FT + 12 * i + 3 * dd
                    dve.wait_ge(w_used, n + 3)
                    add_residual(r, 4 * i + dd, bank[4 + dd % 2], dd % 2)

                last = fi == 3
                if not last:
                    with dve.Fori(0, 2) as i:
                        for dd in range(4):
                            for j in range(3):
                                refill(u + 48 + 12 * i + 3 * dd + j, (3 * dd + j) % RING)
                            down(i, dd, 3)
                else:
                    for i in range(2):
                        for dd in range(4):
                            for j in range(3):
                                if 12 * i + 3 * dd + j < 20:
                                    refill(u + 48 + 12 * i + 3 * dd + j, (3 * dd + j) % RING)
                            down(i, dd, 3)
                normalise(n_ln, PREP[r])

            PREP = {0: [1], 2: [3, 4], 3: [5], 5: []}

            dve.sem_inc(z_ready, 2)
            dve.sem_inc(u_done, 2)
            dve.wait_ge(par_in, 16)
            g0, b0 = PAR["ln_g"][0], PAR["ln_b"][0]
            v.tensor_scalar(gA[:], par[:, g0:g0 + 7 * KT], ALPHA, None, ALU.mult)
            v.tensor_scalar(bA[:], par[:, b0:b0 + 7 * KT], ALPHA, None, ALU.mult).then_inc(init_dve, 1)
            for n in range(RING):
                refill(n, n)
            prepare(0)
            modulate(0)
            rest_h(M_S0, h32, hH, hL)
            ffn(0)
            modulate(1)
            rest_h(M_S1, h32, hH, hL)
            dve.wait_ge(hist_ok, 2)
            with dve.Fori(0, 4) as i:
                for j in range(2):
                    d, n = 2 * i + j, U_PW1 + 4 * i + 2 * j
                    dve.wait_ge(sig_done, d + 1)
                    A = bank[2 * j]
                    v.scalar_tensor_tensor(uP[:, d, HIST:], A[:, 0:SEQ], pcol("pw1_b", d), sg[:, j, 0:SEQ],
                                           ALU.add, ALU.mult)
                    v.scalar_tensor_tensor(uS[:, d, :, HIST:], A[:, SEQ:T].rearrange("p (b t) -> p b t", b=DB),
                                           pcol("pw1_b", d), sg[:, j, SEQ:T].rearrange("p (b t) -> p b t", b=DB),
                                           ALU.add, ALU.mult).then_inc(u_done, 1)
                    refill(n + RING, 2 * j)
                    refill(n + RING + 1, 2 * j + 1)
                    dve.wait_ge(u_done, 2 + d + 1)
                    zP = z[:, d, 0:SEQ]
                    zS = z[:, d, SEQ:T].rearrange("p (b t) -> p b t", b=DB)
                    for k in range(CK):
                        w = pcol("dw_w", CK * d + k)
                        sP, sS = uP[:, d, k:k + SEQ], uS[:, d, :, k:k + DS]
                        if k == 0:
                            v.tensor_scalar(zP, sP, w, pcol("dw_b", d), ALU.mult, ALU.add).then_inc(tapP, 1)
                            v.tensor_scalar(zS, sS, w, pcol("dw_b", d), ALU.mult, ALU.add).then_inc(tapS, 1)
                        else:
                            dve.wait_ge(tapP, CK * d + k)
                            v.scalar_tensor_tensor(zP, sP, w, zP, ALU.mult, ALU.add).then_inc(tapP, 1)
                            dve.wait_ge(tapS, (CK - 1) * d + k)
                            op = v.scalar_tensor_tensor(zS, sS, w, zS, ALU.mult, ALU.add)
                            op.then_inc(tapS if k < CK - 1 else z_ready, 1)
            normalise(1)
            rest_h(M_PW2, h32, hH, hL)
            gate(1)
            dve.wait_ge(xa_done, 2 * KT)
            with dve.Fori(0, 2) as i:
                for j in range(RING):
                    n = U_PW2 + RING * i + j
                    refill(n + RING, j)
                    dve.wait_ge(w_used, n + 1)
                    add_residual(1, RING * i + j, bank[j], j % 2, bias=pcol("pw2_b", RING * i + j))
            normalise(2, [2])
            modulate(2)
            rest_h(M_S2, h32, hH, hL)
            ffn(1)
            modulate(3)
            rest_h(M_KV, kv32, kvH, kvL)
            dve.wait_ge(f_mm, 1)
            step(v.tensor_scalar(lf_l[:], bank[6][0:H, 0:T], par[0:H, PAR["b_f"][0]:PAR["b_f"][0] + 1], None,
                                 ALU.add))
            step(v.tensor_scalar(lf_m[:], lf_l[:], 0.0, None, ALU.min))
            v.scalar_tensor_tensor(lf_e[:], lf_m[:], -2.0, lf_l[:], ALU.mult, ALU.add).then_inc(lf_chain, 1)
            dve.wait_ge(lfg_done, 1)
            step(v.tensor_tensor(lf_n[:], lf_m[:], lf_g[:], ALU.subtract))
            dve.wait_ge(lf_in, 16)
            step(v.tensor_copy(lfS[:, :, PAST:NK], lf_n[:, SEQ:T].rearrange("h (b t) -> h b t", b=DB)))
            one_row = pcol("ln_g", 0)[0:H, :]
            for b in range(DB):
                v.tensor_tensor_scan(lfS[:, b, :], one_row.to_broadcast([H, NK]), lfS[:, b, :], 0.0,
                                     ALU.mult, ALU.subtract).then_inc(ncum_done, 1)
            v.tensor_tensor_scan(lfP[:], one_row.to_broadcast([H, SEQ]), lf_n[:, 0:SEQ], 0.0,
                                 ALU.mult, ALU.subtract).then_inc(ncum_done, 1)
            modulate(4)
            for n in range(U_K + RING, U_FFN2 + RING):
                refill(n, n % RING)
            rest_h(M_S3, kv32, hH, hL)
            ffn(2)
            modulate(5)
            rest_h(M_S4, h32, hH, hL)
            for n in range(U_Q + RING, U_O + RING):
                refill(n, n % RING)

            def row_max(kind, i, j):
                slot, w = j % 4, width(kind, j)
                dve.wait_ge(s_mm, job(kind, i, j) + 1)
                if kind == "p":
                    v.tensor_reduce(nmx[:, slot, :], bank[slot][:, 0:2 * w].rearrange("p (h w) -> p h w", h=2),
                                    AX.X, ALU.max, negate=True).then_inc(nm_done, 1)
                else:
                    v.tensor_reduce(nmx[:, slot, 0:1], bank[slot][:, 0:w], AX.X, ALU.max, negate=True)\
                        .then_inc(nm_done, 1)

            def norm(kind, i, j):
                J, slot, w = job(kind, i, j), j % 4, width(kind, j)
                n = 2 if kind == "p" else 1
                dve.wait_ge(p_done, J + 1)
                v.reciprocal(rin[:, slot, 0:n], rsm[:, slot, 0:n]).then_inc(ri_done, 1)
                dve.wait_ge(ri_done, J + 1)
                if kind == "p":
                    pr = prS[:, slot, 0:2 * w].rearrange("p (h w) -> p h w", h=2)
                    v.tensor_tensor(pr, pr, rin[:, slot, :].unsqueeze(2).to_broadcast([P, 2, w]), ALU.mult)\
                        .then_inc(pn_done, 1)
                else:
                    v.tensor_scalar(prS[:, slot, 0:w], prS[:, slot, 0:w], rin[:, slot, 0:1], None, ALU.mult)\
                        .then_inc(pn_done, 1)

            def out_prompt(i, j):
                dve.wait_ge(pv_mm, job("p", i, j) + 1)
                v.tensor_copy(z[:, 2 * i + j // 2, P * (j % 2):P * (j % 2) + P], bank[6][:, 0:P]).then_inc(o_done, 1)

            def out_token(i, j):
                dve.wait_ge(pv_mm, job("s", i, j) + 1)
                v.tensor_copy(om[:, j % 2, :], bank[6][:, 0:P]).then_inc(om_done, 1)

            def out_stream(i, j):
                dve.wait_ge(o_mm, 4 * i + j + 1)
                for hh in range(2):
                    rows = slice(HD * hh, HD * hh + HD)
                    src = bank[4 + (j + 1) % 2][rows, 384:512].rearrange("p (k c) -> p k c", k=4)
                    op = v.tensor_copy(z[rows, 4 * (j % 2):4 * (j % 2) + 4, bass.ds(SEQ + DS * (2 * i + j // 2), DS)],
                                       src[:, :, DS * hh:DS * hh + DS])
                op.then_inc(o_done, 1)

            def body(kind, i, scores=True):
                for j in range(4):
                    if scores:
                        row_max(kind, i, j)
                    jn, jv, jo = (earlier(kind, i, j - n) for n in (1, 3, 4))
                    if jn and (scores or j < 1):
                        norm(*jn)
                    if jv and (scores or j < 3):
                        (out_prompt if jv[0] == "p" else out_token)(*jv[1:])
                    if jo and jo[0] == "s":
                        out_stream(*jo[1:])

            dve.wait_ge(xa_done, 5 * KT)
            body("p", 0)
            with dve.Fori(1, 4) as i:
                body("p", i)
            body("s", 0)
            with dve.Fori(1, 4) as i:
                body("s", i)
            body("s", 4, scores=False)
            rest_h(M_O, z, hH, hL)
            gate(4)
            with dve.Fori(0, 2) as i:
                for j in range(RING):
                    n = U_O + RING * i + j
                    refill(n + RING, j)
                    dve.wait_ge(w_used, n + 1)
                    add_residual(4, RING * i + j, bank[j], j % 2)
            normalise(5, [6])
            modulate(6)
            rest_h(M_S5, h32, hH, hL)
            ffn(3)
            for k in range(KT):
                c = 6 * KT + k
                dve.wait_ge(zn_done, 4 * 6 + k // 2 + 1)
                op = v.tensor_scalar(z[:, k, :], z[:, k, :], pcol("ln_g", c), pcol("ln_b", c), ALU.mult, ALU.add)
                if k % 2:
                    op.then_inc(y_done, 1)

        @block.tensor
        def _(pe):
            mm = nc.tensor.matmul

            def tile_w(ring, slot, k):
                return ring[:, slot, k * P:(k + 1) * P]

            def unit(n, slot, out, movH, movL, k0=0, nk=8, start=True, stop=True, ready=None):
                pe.wait_ge(w_lo, n + 1)
                for k in range(nk):
                    if ready is not None and k % 2 == 0:
                        pe.wait_ge(hl_done, 4 * ready + k // 2 + 1)
                    for q, (w, m) in enumerate(((wH, movH), (wH, movL), (wL, movH))):
                        op = mm(out, tile_w(w, slot, k), m[:, k0 + k, :],
                                start=start and k == 0 and q == 0, stop=stop and k == nk - 1 and q == 2)
                op.then_inc(w_used, 1)

            def ada_mm(c, tile, waits):
                if not isinstance(c, int) or c > 0:
                    pe.wait_ge(a_mod, c)
                for half in range(2):
                    waits(half)
                    for j in range(4):
                        op = mm(ADB[32 * j:32 * j + 32, 0:256], cact[:, 4 * half + j, :], tile[:, half, j, :],
                                start=half == 0, stop=half == 1)
                op.then_inc(a_mm, 1)

            def ada_tr(c):
                pe.wait_ge(a_ev, c + 1)
                for j in range(2):
                    op = mm(ADB[:, 256 + 16 * j:256 + 16 * j + NG], adaS[:, P * j:P * j + P],
                            con[:, C_SEL9:C_SEL9 + NG], start=True, stop=True)
                op.then_inc(a_tr, 1)

            def ring_waits(c):
                return lambda half: pe.wait_ge(a_in[half], 16 * (c - FIRST_CHUNKS) + 16)

            def ada(c):
                ada_mm(c, araw, ring_waits(c))
                ada_tr(c)

            def stats(n):
                pe.wait_ge(zs_done, KT * (n + 1))
                mm(MEAN[:, 0:T], ones, zs[:], start=True, stop=True).then_inc(mean_ok, 1)
                for q in range(4):
                    pe.wait_ge(sq_done, 4 * n + q + 1)
                    for k in (2 * q, 2 * q + 1):
                        op = mm(VAR[:, 0:T], ones, sq[:, k, :], start=k == 0, stop=k == KT - 1)
                op.then_inc(var_ok, 1)

            def ffn(fi):
                u, (c, na, nd) = FFN_U[fi], FFN_ADA[fi]
                m = FFN_M[fi]

                def gate_up(i, with_ada):
                    for j in range(2):
                        f, n = 2 * i + j, u + 4 * i + 2 * j
                        pe.wait_ge(prod[fi], f + 1)
                        unit(n, 2 * j, bank[2 * j][:, 0:T], hH, hL, ready=m)
                        unit(n + 1, 2 * j + 1, bank[2 * j + 1][:, 0:T], hH, hL)
                        if with_ada:
                            if j == 0:
                                ada_mm(c + i, araw, ring_waits(c + i))
                            else:
                                ada_tr(c + i)

                with pe.Fori(0, na) as i:
                    gate_up(i, True)
                if na < 11:
                    with pe.Fori(na, 11) as i:
                        gate_up(i, False)
                with pe.Fori(0, 2) as i:
                    for dd in range(4):
                        pe.wait_ge(z_ready, KT * FFN_LN[fi] + 4 * i + dd + 1)
                        for j, (k0, nk) in enumerate(DOWN_K):
                            n = u + 2 * FT + 12 * i + 3 * dd + j
                            pe.wait_ge(hidl[fi], k0 + nk)
                            unit(n, (3 * dd + j) % RING, bank[4 + dd % 2][:, 0:T], hidH, hidL, k0, nk,
                                 start=j == 0, stop=j == 2)
                            if nd and j == 0:
                                ada_mm(c + na + 4 * i + dd, araw, ring_waits(c + na + 4 * i + dd))
                        if nd:
                            ada_tr(c + na + 4 * i + dd)
                stats(FFN_LN[fi])

            pe.wait_ge(con_in, 16)
            pe.wait_ge(cact_ok, 1)
            for c in range(FIRST_CHUNKS):
                ada_mm(c, land[:, c], lambda half, c=c: pe.wait_ge(land_in[c], 32))
                ada_tr(c)
            ffn(0)
            with pe.Fori(0, 4) as i:
                for j in range(2):
                    n = U_PW1 + 4 * i + 2 * j
                    pe.wait_ge(u_done, 2 * i + j + 1)
                    unit(n, 2 * j, bank[2 * j][:, 0:T], hH, hL, ready=M_S1)
                    unit(n + 1, 2 * j + 1, bank[2 * j + 1][:, 0:T], hH, hL)
                    ada(CH_S1 + 2 * i + j)
            stats(1)
            pe.wait_ge(u_done, 2 + KT)
            with pe.Fori(0, 2) as i:
                for j in range(RING):
                    pe.wait_ge(z_ready, 2 + KT * 2 - 4 + 4 * i + j + 1)
                    unit(U_PW2 + RING * i + j, j, bank[j][:, 0:T], hH, hL, ready=M_PW2)
            stats(2)
            ffn(1)
            pe.wait_ge(wf_in, 16)
            for k in range(KT):
                if k % 2 == 0:
                    pe.wait_ge(hl_done, 4 * M_KV + k // 2 + 1)
                op = mm(bank[6][0:H, 0:T], wf[:, k, :], kv32[:, k, :], start=k == 0, stop=k == KT - 1)
            op.then_inc(f_mm, 1)
            for i in range(2):
                for j in range(RING):
                    if i:
                        pe.wait_ge(kf_done, j + 1)
                    unit(U_K + RING * i + j, j, bank[j][:, 0:T], kvH, kvL, ready=M_KV)
            for half in range(2):
                if half == 0:
                    pe.wait_ge(kf_done, KT)
                for j in range(RING):
                    n = U_V + RING * half + j
                    pe.wait_ge(w_lo, n + 1)
                    for t in range(3):
                        tok = slice(P * t, P * t + P)
                        for kk in range(2):
                            k = 2 * j + kk
                            for q, (h, w) in enumerate(((kvH, wH), (kvH, wL), (kvL, wH))):
                                op = mm(bank[3 * half + t][:, :], h[:, k, tok],
                                        w[:, j, 512 * kk:512 * kk + 512],
                                        start=k == 0 and q == 0, stop=k == KT - 1 and q == 2)
                    op.then_inc(w_used, 1)
            pe.wait_ge(vs_done, 6)
            ffn(2)
            for i in range(2):
                for j in range(RING):
                    if i:
                        pe.wait_ge(q_done, j + 1)
                    unit(U_Q + RING * i + j, j, bank[j][:, 0:T], hH, hL, ready=M_S4)
            pe.wait_ge(q_done, KT)

            def scores(kind, i, j):
                J, S, w = job(kind, i, j), bank[j % 4], width(kind, j)
                s = j // 2
                if kind == "p":
                    if j % 2 == 0:
                        pe.wait_ge(kp_in[s], 32 * i + 32)
                        pe.wait_ge(qp_done, 4 * i + 2 * s + 2)
                    mm(S[:, 0:2 * w], con[0:1, C_ONE:C_ONE + P], ncP[0:1, s, :, 0:w], start=True, stop=False)
                    qt = j % 2
                    for hh in range(2):
                        c0 = hh * w
                        mm(S[:, c0 + w - P:c0 + w], ident, con[:, C_MP:C_MP + P], start=False, stop=False)
                        op = mm(S[:, c0:c0 + w], qP[:, s, hh, P * qt:P * qt + P], KP[:, s, 0:w],
                                start=False, stop=hh == 1)
                else:
                    hf = j % 2
                    if hf == 0:
                        pe.wait_ge(sk_in[s], 32 * i + 32)
                        pe.wait_ge(qbd_done, 6 * i + 3 * s + 3)
                    mm(S[:, 0:NK], con[0:H, C_SELH + P * hf:C_SELH + P * hf + P], ncS[:, s, :],
                       start=True, stop=False)
                    for kk in range(4):
                        mm(S[32 * kk:32 * kk + 32, 0:PAST], qbd[:, s, 4 * hf + kk, :], KTb[:, s, 4 * hf + kk, :],
                           start=False, stop=False)
                    for kk in range(4):
                        mm(S[32 * kk:32 * kk + 32, PAST:NK], qbd[:, s, 4 * hf + kk, :],
                           knS[:, s, 4 * hf + kk, :], start=False, stop=False)
                    op = mm(S[:, PAST:NK], ident, con[:, C_MS:C_MS + DS], start=False, stop=True)
                op.then_inc(s_mm, 1)

            def transposes(kind, i, j):
                J = job(kind, i, j)
                pe.wait_ge(pn_done, J + 1)
                if kind == "s" and (not isinstance(i, int) or J >= JP + 3):
                    pe.wait_ge(o_done, J - 2)
                w = 2 * width("p", j) if kind == "p" else NK
                for c0 in range(0, w, P):
                    n = min(P, w - c0)
                    op = nc.tensor.transpose(bank[4 + j % 2][0:n, c0:c0 + P], prS[:, j % 4, c0:c0 + n], ident)
                op.then_inc(t_mm, 1)

            def values(kind, i, j):
                J = job(kind, i, j)
                pe.wait_ge(pt_done, J + 1)
                if kind == "p" or (isinstance(i, int) and J == JP):
                    if not isinstance(i, int) or J > 0:
                        pe.wait_ge(o_done, J)
                else:
                    pe.wait_ge(om_done, J - JP)
                s = j // 2
                if kind == "p":
                    qt = j % 2
                    if qt == 0:
                        pe.wait_ge(vp_in[s], 16 * i + 16)
                    for hh in range(2):
                        rows = slice(HD * hh, HD * hh + HD)
                        for t in range(1 + qt):
                            c0 = (hh * (1 + qt) + t) * P
                            op = mm(bank[6][rows, 0:P], VP[:, s, t, rows], PT[:, j % 2, c0:c0 + P],
                                    start=t == 0, stop=t == qt)
                else:
                    hf = j % 2
                    if hf == 0:
                        pe.wait_ge(sv_in[s], 32 * i + 32)
                    for t in range(3):
                        rr = P if t < 2 else DS
                        for kk in range(4):
                            pair = slice(P * (4 * hf + kk), P * (4 * hf + kk) + P)
                            V = Vb[:, s, t, pair] if t < 2 else Vn[:, s, pair]
                            c0 = t * P + 32 * kk
                            op = mm(bank[6][32 * kk:32 * kk + 32, 0:P], PT[0:rr, j % 2, c0:c0 + 32], V,
                                    start=t == 0, stop=t == 2)
                op.then_inc(pv_mm, 1)

            def turn(kind, i, j):
                pe.wait_ge(om_done, 4 * i + j + 1)
                nc.tensor.transpose(bank[4 + (j + 1) % 2][:, 384:512], om[:, j % 2, :], ident).then_inc(o_mm, 1)

            def body(kind, i, with_ada=False, new=True):
                for j in range(4):
                    if new:
                        scores(kind, i, j)
                    jt, jv, jo = (earlier(kind, i, j - n) for n in (2, 3, 4))
                    if jt and (new or j < 2):
                        transposes(*jt)
                    if jv and (new or j < 3):
                        values(*jv)
                    if jo and jo[0] == "s":
                        turn(*jo)
                    if with_ada and j == 2:
                        ada_mm(CH_S4 + i, araw, ring_waits(CH_S4 + i))
                    if with_ada and j == 3:
                        ada_tr(CH_S4 + i)

            body("p", 0, True)
            with pe.Fori(1, 4) as i:
                body("p", i, True)
            body("s", 0)
            with pe.Fori(1, 4) as i:
                body("s", i)
            body("s", 4, new=False)
            for i in range(2):
                for j in range(RING):
                    if i:
                        pe.wait_ge(z_ready, 2 + KT * 5 + j + 1)
                    unit(U_O + RING * i + j, j, bank[j][:, 0:T], hH, hL, ready=M_O)
            stats(5)
            ffn(3)


def _tiles(w):
    k, n = w.shape[0] // P, w.shape[1] // P
    return w.reshape(k, P, n, P).transpose(2, 1, 0, 3)


def _cols(a):
    return np.ascontiguousarray(a.reshape(-1, P).T)


def _weight_stream(i):
    W = np.zeros((N_UNITS, P, UNIT), np.float32)

    def ffn(u, l, j):
        gu = W[u:u + 2 * FT].reshape(FT, 2, P, KT, P)
        gu[:, 0] = _tiles(i["ffn_w_gate"][l, j])
        gu[:, 1] = _tiles(i["ffn_w_up"][l, j])
        down = _tiles(i["ffn_w_down"][l, j])
        for q, (k0, nk) in enumerate(DOWN_K):
            W[u + 2 * FT + q:u + FFN_UNITS:3, :, 0:nk * P] = down[:, :, k0:k0 + nk].reshape(KT, P, nk * P)

    def square(u, w):
        W[u:u + KT] = _tiles(w).reshape(KT, P, UNIT)

    ffn(U_FFN0, 0, 0)
    pw1 = _tiles(i["pw1_w"][0]).reshape(2, KT, P, UNIT)
    W[U_PW1:U_PW2:2], W[U_PW1 + 1:U_PW2:2] = pw1[0], pw1[1]
    square(U_PW2, i["pw2_w"][0])
    ffn(U_FFN1, 0, 1)
    square(U_K, i["w_k"])
    W[U_V:U_V + KT] = i["w_v"].reshape(4, 2, P, 2, 512).transpose(3, 0, 2, 1, 4).reshape(KT, P, UNIT)
    ffn(U_FFN2, 1, 0)
    square(U_Q, i["w_q"][0])
    square(U_O, i["w_o"][0])
    ffn(U_FFN3, 1, 1)
    return W


def _constants():
    con = np.zeros((P, N_CONST), np.float32)
    r = np.arange(P)
    con[:, C_ID:C_ID + P] = np.eye(P)
    con[:, C_ONES:C_ONES + P] = 1.0 / D
    for g in range(NG):
        con[32 * np.arange(4) + g, C_SEL9 + g] = 1.0
    con[:, C_ONE:C_ONE + P] = 1.0
    for hf in range(2):
        con[8 * hf + r // DS, C_SELH + P * hf + r] = 1.0
    con[:, C_MP:C_MP + P] = np.where(r[None, :] <= r[:, None], 0.0, NEG)
    con[:, C_MS:C_MS + DS] = np.where(np.arange(DS)[None, :] <= (r % DS)[:, None], 0.0, NEG)
    return con


def kernel(**inputs):
    import concourse.bacc as bacc
    from concourse.bass_utils import run_bass_kernel_spmd as run

    i = {k: np.asarray(v) for k, v in inputs.items()}
    par = np.zeros((P, N_PAR), np.float32)

    def put(name, a):
        a0, n = PAR[name]
        par[:, a0:a0 + n] = a

    one = np.ones((P, KT), np.float32)
    put("ln_g", np.concatenate([one, _cols(i["ln_g"])], 1))
    put("ln_b", np.concatenate([0 * one, _cols(i["ln_b"])], 1))
    put("cln_g", _cols(i["conv_ln_g"]))
    put("cln_b", _cols(i["conv_ln_b"]))
    put("b_ada", np.concatenate([_cols(i["b_ada"][0]), _cols(i["b_ada_kv"]), _cols(i["b_ada"][1])], 1))
    put("pw1_b", _cols(i["pw1_b"]))
    put("pw2_b", _cols(i["pw2_b"]))
    put("dw_b", _cols(i["dw_b"]))
    put("dw_w", i["dw_w"][0].reshape(CK, KT, P).transpose(2, 1, 0).reshape(P, KT * CK))
    par[0:H, PAR["b_f"][0]] = i["b_f"]

    ada = np.concatenate([i["w_ada"][0], i["w_ada_kv"], i["w_ada"][1]], 1)
    ada = ada.reshape(2, 4, P, CHUNKS, 256).transpose(3, 0, 2, 1, 4).reshape(2 * CHUNKS, P, 4, 256)
    x = np.concatenate([i["x_prompt"].reshape(SEQ, D), i["x_sample"].reshape(DB * DS, D)], 0)
    c = np.zeros((32, D), np.float32)
    c[0:1], c[1:NG] = i["c_prompt"], i["c_sample"]

    def fm(a):
        return np.ascontiguousarray(a.reshape(-1, KT, P).transpose(2, 1, 0))

    arrays = {
        "W": _weight_stream(i), "ADA": np.ascontiguousarray(ada), "par_d": par, "con_d": _constants(),
        "x_d": fm(x), "c_d": fm(c),
        "conv_d": fm(i["cache_conv"][0].reshape(DB * HIST, D)).reshape(P, KT, DB, HIST),
        "kt_d": np.ascontiguousarray(
            i["cache_k"].reshape(DB, PAST, KT, P).transpose(0, 3, 2, 1)),
        "v_d": i["cache_v"].reshape(DB, PAST, D),
        "lf_d": np.ascontiguousarray(i["cache_logf"].transpose(2, 0, 1)),
        "wf_d": np.ascontiguousarray(i["w_f"].reshape(KT, P, H).transpose(1, 0, 2)),
    }
    outs = {"y_o": (P, KT, T), "kT_o": (P, KT, T), "v_o": (T, D), "lf_o": (H, T), "conv_o": (P, KT, HIST * NG)}
    nc = bacc.Bacc("TRN2", target_bir_lowering=False, num_devices=1)
    args = [nc.dram_tensor(n, a.shape, F32, kind="ExternalInput").ap() for n, a in arrays.items()]
    args += [nc.dram_tensor(n, s, F32, kind="ExternalOutput").ap() for n, s in outs.items()]
    args.append(nc.dram_tensor("ncp_d", (H, SEQ), F32, kind="Internal").ap())
    args.append(nc.dram_tensor("ncs_d", (H, DB, NK), F32, kind="Internal").ap())
    build_program(nc, *args)
    r = run(nc, [arrays], core_ids=[0]).results[0]

    def rows(a):
        return np.asarray(a).transpose(2, 1, 0).reshape(-1, D)

    y, k, v, lf, cv = rows(r["y_o"]), rows(r["kT_o"]), r["v_o"], r["lf_o"].T, rows(r["conv_o"])
    return (y[:SEQ].reshape(1, SEQ, D), y[SEQ:].reshape(DB, DS, D),
            cv[:HIST].reshape(1, 1, HIST, D),
            k[:SEQ].reshape(1, SEQ, H, HD), v[:SEQ].reshape(1, SEQ, H, HD), lf[:SEQ].reshape(1, SEQ, H),
            cv[HIST:].reshape(1, DB, HIST, D),
            k[SEQ:].reshape(DB, DS, H, HD), v[SEQ:].reshape(DB, DS, H, HD), lf[SEQ:].reshape(DB, DS, H))
```

```python
from contextlib import ExitStack

import numpy as np
import concourse.bass as bass
from concourse import mybir

F32 = mybir.dt.float32
F32R = mybir.dt.float32r
ALU = mybir.AluOpType
ACT = mybir.ActivationFunctionType
AX = mybir.AxisListType

P = 128
D = 1024
KT = D // P
SEQ = 256
DB, DS = 8, 16
T = SEQ + DB * DS
FF = 2816
FT = FF // P
PAST = 256
H, HD = 16, 64
CK = 31
HIST = CK - 1
TAPS_PE, TAPS_POOL = 6, 12
TAPS_DVE = CK - TAPS_PE - TAPS_POOL
PRODS = 4
NG = 1 + DB
ALPHA = float(4 ** 0.25)
EPS = 1e-5
UNIT = 1024
RING = 4
DOWN_K = ((0, 8), (8, 7), (15, 7))
FFN_UNITS = 2 * FT + 3 * KT
NK = PAST + DS
NEG = -1e30

U_FFN0 = 0
U_PW1 = U_FFN0 + FFN_UNITS
U_PW2 = U_PW1 + 2 * KT
U_FFN1 = U_PW2 + KT
U_K = U_FFN1 + FFN_UNITS
U_V = U_K + KT
U_FFN2 = U_V + KT
U_Q = U_FFN2 + FFN_UNITS
U_O = U_Q + KT
U_FFN3 = U_O + KT
N_UNITS = U_FFN3 + FFN_UNITS

V_L0, V_KV, V_L1, N_VEC = 0, 9, 11, 20
CHUNKS = 4 * N_VEC
FIRST_CHUNKS = 8

PAR = {}


def _par(name, n):
    PAR[name] = (PAR["_end"][1], n)
    PAR["_end"] = (0, PAR["_end"][1] + n)


PAR["_end"] = (0, 0)
_par("ln_g", 7 * KT)
_par("ln_b", 7 * KT)
_par("cln_g", KT)
_par("cln_b", KT)
_par("b_ada", 2 * CHUNKS)
_par("pw1_b", 2 * KT)
_par("pw2_b", KT)
_par("dw_b", KT)
_par("dw_w", KT * CK)
_par("b_f", 1)
N_PAR = PAR["_end"][1]

C_ID, C_ONES, C_SEL9, C_SELH, C_MP, C_MS, C_ONE = 0, 128, 256, 265, 521, 649, 665
N_CONST = 793


def build_program(nc, W, ADA, par_d, con_d, x_d, c_d, conv_d, kt_d, v_d, lf_d, wf_d,
                  y_o, kT_o, v_o, lf_o, conv_o, ncp_d, ncs_d):
    with ExitStack() as ctx:
        place = [(nc.sbuf_base + 31) // 32 * 32]

        def at(name, shape, offset, dt=F32):
            return nc.alloc_sbuf_tensor_at(name, shape, dt, offset=offset)

        def sb(name, shape, dt=F32):
            n = int(np.prod(shape[1:])) * 4
            o = place[0]
            place[0] += (n + 31) // 32 * 32
            return at(name, shape, o, dt)

        def sem(name):
            return ctx.enter_context(nc.semaphore(name))

        xa = sb("xa", [P, KT, T])
        z = sb("z", [P, KT, T])
        hH = sb("hH", [P, KT, T], F32R)
        hL = sb("hL", [P, KT, T], F32R)
        raw = sb("raw", [P, RING, UNIT])
        wH = sb("wH", [P, RING, UNIT], F32R)
        wL = sb("wL", [P, RING, UNIT], F32R)
        araw = sb("araw", [P, 2, 4, 256])
        hid = place[0]
        hidH = sb("hidH", [P, FT, T], F32R)
        hidL = sb("hidL", [P, FT, T], F32R)
        BLK = KT * T * 4
        land = at("land", [P, FIRST_CHUNKS, 2, 4, 256], hid)
        sq = at("sq", [P, KT, T], hid + 3 * BLK)
        h32 = at("h32", [P, KT, T], hid + 3 * BLK)
        uP = at("uP", [P, KT, HIST + SEQ], hid)
        uS = at("uS", [P, KT, DB, HIST + DS], hid + KT * (HIST + SEQ) * 4)
        conv_st = at("conv_st", [P, KT, HIST * NG], hid + 2 * BLK)
        conv_in = at("conv_in", [P, KT, DB, HIST], hid + 4 * BLK)
        diag = at("diag", [P, 2, TAPS_PE, P], hid + 3 * BLK)
        pacc = at("pacc", [P, 2, T], hid + 3 * BLK + 8192)
        assert 8 * TAPS_PE * P <= 8192 and 2 * TAPS_POOL % PRODS == 0
        tprod = at("tprod", [P, PRODS, T], hid + 5 * BLK)
        kvH = at("kvH", [P, KT, T], hid, F32R)
        kvL = at("kvL", [P, KT, T], hid + BLK, F32R)
        kv32 = at("kv32", [P, KT, T], hid + 2 * BLK)
        kF = at("kF", [P, KT, T], hid + 3 * BLK)
        vS = at("vS", [P, 3, D], hid + 4 * BLK)
        hH_off = hH.manual_sbuf_range[0]
        lfS = at("lfS", [H, DB, NK], hH_off)
        lfP = at("lfP", [H, SEQ], hH_off + DB * NK * 4)
        hL_off = hL.manual_sbuf_range[0]
        lf_l = at("lf_l", [H, T], hL_off)
        lf_m = at("lf_m", [H, T], hL_off + 4 * T)
        lf_e = at("lf_e", [H, T], hL_off + 8 * T)
        lf_g = at("lf_g", [H, T], hL_off + 12 * T)
        lf_n = at("lf_n", [H, T], hL_off + 16 * T)
        q32 = at("q32", [P, KT, T], hid)
        o = hid + BLK
        qP = at("qP", [P, 2, 2, SEQ], o)
        VP = at("VP", [P, 2, 2, P], o + 4096)
        KP = at("KP", [P, 2, SEQ], o + 6144)
        knS = at("knS", [P, 2, KT, DS], o + 8192)
        Kn = at("Kn", [P, KT, DB * DS], o + 12288)
        KTb = at("KTb", [P, 2, KT, PAST], o + 16384)
        Vb = at("Vb", [P, 2, 2, D], o + 32768)
        o += 49152
        prS = at("prS", [P, 4, 512], hH_off)
        PT = at("PT", [P, 2, 512], hH_off + 8192)
        Vn = at("Vn", [DS, 2, D], hL_off)
        assert o <= hid + 2 * FT * T * 4
        par = sb("par", [P, N_PAR])
        con = sb("con", [P, N_CONST])
        mods = sb("mods", [P, KT * N_VEC, NG])
        craw = sb("craw", [P, KT, 32])
        cact = sb("cact", [P, KT, 32])
        wf = sb("wf", [P, KT, H])
        Am = sb("Am", [P, 2, KT, NG])
        Bm = sb("Bm", [P, 2, KT, NG])
        Gm = sb("Gm", [P, 2, KT, NG])
        gA = sb("gA", [P, 7 * KT])
        bA = sb("bA", [P, 7 * KT])
        sg = sb("sg", [P, 2, T])
        tmp = sb("tmp", [P, 2, T])
        epS = sb("epS", [P, 2, DB * DS])
        zs = sb("zs", [P, T])
        rstd = sb("rstd", [P, T])
        sd = sb("sd", [P, T])
        eps = sb("eps", [P, 1])
        adaS = sb("adaS", [P, 256])
        qbd = sb("qbd", [P, 2, KT, 2 * DS])
        nmx = sb("nmx", [P, 4, 2])
        rsm = sb("rsm", [P, 4, 2])
        rin = sb("rin", [P, 4, 2])
        ncS = at("ncS", [H, 2, NK], sg.manual_sbuf_range[0])
        om = at("om", [P, 2, P], tmp.manual_sbuf_range[0])
        ncP = at("ncP", [1, 2, 2, SEQ], zs.manual_sbuf_range[0])
        assert place[0] <= nc.sbuf_usable_end, place[0] - nc.sbuf_usable_end
        ident = con[:, C_ID:C_ID + P]
        ones = con[:, C_ONES:C_ONES + P]

        bank = [ctx.enter_context(nc.psum_tensor(f"bank{i}", [P, 512], F32)) for i in range(8)]
        MEAN, VAR, ADB = bank[6], bank[5], bank[7]

        def pcol(name, c=0, n=1):
            a = PAR[name][0]
            return par[:, bass.ds(a + c, n)]

        par_in, wf_in, con_in, x_in, c_in, convc_in, lf_in, conv_out = (sem(n) for n in (
            "par_in", "wf_in", "con_in", "x_in", "c_in", "convc_in", "lf_in", "conv_out"))
        land_in = [sem(f"land_in{i}") for i in range(FIRST_CHUNKS)]
        w_in = [sem(f"w_in{i}") for i in range(RING)]
        w_hi = sem("w_hi")
        w_lo = sem("w_lo")
        w_used = sem("w_used")
        a_in = [sem(f"a_in{i}") for i in range(2)]
        a_mm, a_ev, a_tr, a_mod = (sem(n) for n in ("a_mm", "a_ev", "a_tr", "a_mod"))
        cact_ok, init_dve, init_pool = sem("cact_ok"), sem("init_dve"), sem("init_pool")
        z_ready = sem("z_ready")
        zs_done, mean_ok, zc_done, sq_done, sp_done, var_ok, sd_done, rs_done, zn_done = (sem(n) for n in (
            "zs_done", "mean_ok", "zc_done", "sq_done", "sp_done", "var_ok", "sd_done", "rs_done", "zn_done"))
        ab_done, hp_done, hs1_done, hs_done, hh_done, hl_done, xa_done = (sem(n) for n in (
            "ab_done", "hp_done", "hs1_done", "hs_done", "hh_done", "hl_done", "xa_done"))
        sm_done = sem("sm_done")
        gm_done = sem("gm_done")
        ep1_done = sem("ep1_done")
        sg_done = [sem(f"sg_done{i}") for i in range(4)]
        prod = [sem(f"prod{i}") for i in range(4)]
        hidh = [sem(f"hidh{i}") for i in range(4)]
        hidl = [sem(f"hidl{i}") for i in range(4)]
        hist_ok, sig_done, u_done, tapP, tapS, convst_ok = (sem(n) for n in (
            "hist_ok", "sig_done", "u_done", "tapP", "tapS", "convst_ok"))
        diag_done, cv_mm, prod_done, pacc_done, fin1_done, zs_clear = (sem(n) for n in (
            "diag_done", "cv_mm", "prod_done", "pacc_done", "fin1_done", "zs_clear"))
        silu_done = sem("silu_done")
        kf_done, vs_done, f_mm, lf_chain, lfe_done, lfg_done, ncum_done, lfo_done = (sem(n) for n in (
            "kf_done", "vs_done", "f_mm", "lf_chain", "lfe_done", "lfg_done", "ncum_done", "lfo_done"))
        kv_out, nc_out, fin_out = sem("kv_out"), sem("nc_out"), sem("fin_out")
        q_done, qp_done, qbd_done = sem("q_done"), sem("qp_done"), sem("qbd_done")
        kn_in = sem("kn_in")
        kp_in, vp_in, sk_in, sv_in = ([sem(f"{n}{i}") for i in range(2)] for n in ("kp_in", "vp_in", "sk_in", "sv_in"))
        om_done, o_mm = sem("om_done"), sem("o_mm")
        s_mm, nm_done, p_done, ri_done, pn_done, t_mm, pt_done, pv_mm, o_done = (sem(n) for n in (
            "s_mm", "nm_done", "p_done", "ri_done", "pn_done", "t_mm", "pt_done", "pv_mm", "o_done"))
        y_done = sem("y_done")

        GATE_VEC = [V_L0 + 2, V_L0 + 5, V_L0 + 8, V_L1 + 2, V_L1 + 5, V_L1 + 8]
        MODS = [(-1, 0, V_L0, False), (0, 1, V_L0 + 3, False), (2, 2, V_L0 + 6, False),
                (3, 3, V_KV, True), (3, 3, V_L1, False), (4, 4, V_L1 + 3, False), (5, 5, V_L1 + 6, False)]
        M_S0, M_S1, M_PW2, M_S2, M_KV, M_S3, M_S4, M_O, M_S5 = range(9)
        FFN_M = [M_S0, M_S2, M_S3, M_S5]
        FFN_U = [U_FFN0, U_FFN1, U_FFN2, U_FFN3]
        FFN_LN = [0, 3, 4, 6]
        FFN_SUB = [0, 2, 3, 5]
        FFN_ADA = [(8, 11, 8), (35, 11, 8), (54, 11, 8), (77, 3, 0)]
        CH_S1, CH_S4 = 27, 73
        JP, JS = 16, 16

        def streams(ap):
            return ap.rearrange("p k (b t) -> p k b t", b=DB)

        def job(kind, i, j):
            return 4 * i + j + (JP if kind == "s" else 0)

        def earlier(kind, i, j):
            if j >= 0:
                return kind, i, j
            if isinstance(i, int) and i == 0:
                return None if kind == "p" else ("p", JP // 4 - 1, j + 4)
            return kind, i - 1, j + 4

        def width(kind, j):
            return P * (1 + j % 2) if kind == "p" else NK

        def over_tokens(ap, k):
            return ap.unsqueeze(3).to_broadcast([P, k, DB, DS])

        block = ctx.enter_context(nc.Block())

        @block.sync
        def _(sp):
            def w_unit(n, slot, wait=True):
                if wait:
                    sp.wait_ge(w_lo, n - (RING - 1))
                sp.dma_start(raw[:, slot, :], W[n]).then_inc(w_in[slot], 16)

            def w_units(n, count, wait=True):
                for j in range(count):
                    w_unit(n + j, j % RING, wait)

            def ada_chunk(c):
                sp.wait_ge(a_mm, c)
                for j in range(2):
                    sp.dma_start(araw[:, j], ADA[2 * c + j]).then_inc(a_in[j], 16)

            def ffn(fi):
                u, (c, na, nd) = FFN_U[fi], FFN_ADA[fi]
                if fi != 2:
                    w_units(u, RING, wait=fi > 0)
                with sp.Fori(0, na) as i:
                    ada_chunk(c + i)
                    w_units(u + RING + RING * i, RING)
                if na < 11:
                    with sp.Fori(na, 11) as i:
                        w_units(u + RING + RING * i, RING)
                if nd:
                    with sp.Fori(0, 2) as i:
                        for dd in range(4):
                            ada_chunk(c + na + 4 * i + dd)
                            for j in range(3):
                                w_unit(u + 48 + 12 * i + 3 * dd + j, (3 * dd + j) % RING)
                else:
                    with sp.Fori(0, 5) as i:
                        w_units(u + 48 + RING * i, RING)

            sp.dma_start(craw[:], c_d).then_inc(c_in, 16)
            sp.dma_start(par[:], par_d).then_inc(par_in, 16)
            sp.dma_start(con[:], con_d).then_inc(con_in, 16)
            for c in range(FIRST_CHUNKS):
                sp.dma_start(land[:, c, 0], ADA[2 * c]).then_inc(land_in[c], 16)
                sp.dma_start(land[:, c, 1], ADA[2 * c + 1]).then_inc(land_in[c], 16)
            sp.dma_start(z[:], x_d).then_inc(x_in, 16)
            ffn(0)
            sp.dma_start(wf[:], wf_d).then_inc(wf_in, 16)
            sp.wait_ge(mean_ok, 1)
            sp.dma_start(conv_in[:], conv_d).then_inc(convc_in, 16)
            with sp.Fori(0, 4) as i:
                ada_chunk(CH_S1 + 2 * i)
                ada_chunk(CH_S1 + 2 * i + 1)
                w_units(U_PW1 + RING + RING * i, RING)
            w_units(U_PW2 + RING, RING)
            sp.wait_ge(convst_ok, 1)
            sp.dma_start(conv_o, conv_st[:]).then_inc(conv_out, 16)
            ffn(1)
            sp.dma_start(lfS[:, :, 0:PAST], lf_d).then_inc(lf_in, 16)
            w_units(U_K + RING, RING)
            sp.wait_ge(ncum_done, NG)
            sp.dma_start(ncs_d, lfS[:]).then_inc(nc_out, 16)
            sp.dma_start(ncp_d, lfP[:]).then_inc(nc_out, 16)
            sp.dma_start(lf_o, lf_n[:]).then_inc(nc_out, 16)
            w_units(U_V, 3 * RING)
            sp.wait_ge(kf_done, KT)
            sp.dma_start(kT_o, kF[:]).then_inc(kv_out, 16)
            sp.wait_ge(vs_done, 6)
            sp.dma_start(v_o.rearrange("(t p) n -> p t n", p=P), vS[:]).then_inc(kv_out, 16)
            ffn(2)
            w_units(U_Q + RING, RING)
            sp.wait_ge(kv_out, 32)
            sp.wait_ge(nc_out, 48)
            sp.wait_ge(hl_done, 4 * M_S4 + 4)
            sp.wait_ge(xa_done, 5 * KT)

            def prompt_k(pr, s):
                sp.dma_start(KP[:, s], kT_o[:, pr, 0:SEQ]).then_inc(kp_in[s], 16)
                sp.dma_start(ncP[:, s], ncp_d[bass.ds(2 * pr, 2), :].rearrange("(a h) s -> a h s", a=1))\
                    .then_inc(kp_in[s], 16)

            def prompt_v(pr, s):
                sp.dma_start(VP[:, s], v_o[0:SEQ, bass.ds(P * pr, P)].rearrange("(t p) n -> p t n", p=P))\
                    .then_inc(vp_in[s], 16)

            def stream_k(b, s):
                sp.dma_start(KTb[:, s], kt_d[b]).then_inc(sk_in[s], 16)
                sp.dma_start(ncS[:, s], ncs_d[:, b, :]).then_inc(sk_in[s], 16)

            def stream_v(b, s):
                sp.dma_start(Vb[:, s], v_d[b].rearrange("(t p) n -> p t n", p=P)).then_inc(sv_in[s], 16)
                sp.dma_start(Vn[:, s], v_o[bass.ds(SEQ + DS * b, DS), :]).then_inc(sv_in[s], 16)

            def next_k(b, s):
                sp.wait_ge(s_mm, JP + 2 * b - 2)
                stream_k(b, s)

            def next_v(b, s):
                sp.wait_ge(pv_mm, JP + 2 * b - 2)
                stream_v(b, s)

            for s in range(2):
                prompt_k(s, s)
                prompt_v(s, s)
            sp.dma_start(Kn[:], kT_o[:, :, SEQ:T]).then_inc(kn_in, 16)
            w_units(U_O, RING)
            stream_k(0, 0)
            stream_k(1, 1)
            sp.wait_ge(q_done, KT)
            stream_v(0, 0)
            stream_v(1, 1)
            ada_chunk(CH_S4)
            with sp.Fori(0, 3) as i:
                for s in range(2):
                    sp.wait_ge(s_mm, 4 * i + 2 * s + 2)
                    prompt_k(2 * i + 2 + s, s)
                ada_chunk(CH_S4 + 1 + i)
                for s in range(2):
                    sp.wait_ge(pv_mm, 4 * i + 2 * s + 2)
                    prompt_v(2 * i + 2 + s, s)
            next_k(2, 0)
            next_k(3, 1)
            next_v(2, 0)
            with sp.Fori(1, 3) as i:
                next_k(2 * i + 2, 0)
                next_v(2 * i + 1, 1)
                next_k(2 * i + 3, 1)
                next_v(2 * i + 2, 0)
            next_v(7, 1)
            w_units(U_O + RING, RING)
            ffn(3)
            for g in range(4):
                sp.wait_ge(y_done, g + 1)
                sp.dma_start(y_o[:, 2 * g:2 * g + 2], z[:, 2 * g:2 * g + 2]).then_inc(fin_out, 16)
            sp.wait_ge(fin_out, 64)
            sp.wait_ge(conv_out, 16)

        @block.gpsimd
        def _(pool):
            g = nc.gpsimd
            g.memset(qbd[:], 0.0).then_inc(init_pool, 1)

            def sums(n):
                for k in range(KT - 1):
                    pool.wait_ge(z_ready, 2 + KT * n + k + 1)
                    if k == 0:
                        op = g.tensor_copy(zs[:], z[:, 0, :])
                    else:
                        pool.wait_ge(zs_done, (KT - 1) * n + k)
                        op = g.tensor_tensor(zs[:], zs[:], z[:, k, :], ALU.add)
                    op.then_inc(zs_done, 1)

            def modulate(mi):
                n, _, _, kv = MODS[mi]
                dst = kv32 if mi in (3, 4) else h32
                pool.wait_ge(ab_done, mi + 1)
                for q in range(4):
                    ks = slice(2 * q, 2 * q + 2)
                    if n >= 0:
                        pool.wait_ge(zn_done, 4 * n + q + 1)
                    else:
                        pool.wait_ge(x_in, 16)
                    dd = streams(dst[:, ks, SEQ:T])
                    g.tensor_tensor(dd, streams(z[:, ks, SEQ:T]),
                                    over_tokens(Am[:, mi % 2, ks, 1:NG], 2), ALU.mult).then_inc(hs1_done, 1)
                    pool.wait_ge(hs1_done, 4 * mi + q + 1)
                    g.tensor_tensor(dd, dd, over_tokens(Bm[:, mi % 2, ks, 1:NG], 2), ALU.add)\
                        .then_inc(hs_done, 1)

            def residual(e):
                for k in range(KT):
                    c = e * KT + k
                    g.tensor_scalar(xa[:, k, :], z[:, k, :], gA[:, c:c + 1], bA[:, c:c + 1],
                                    ALU.mult, ALU.add).then_inc(xa_done, 1)

            modulate(0)
            pool.wait_ge(init_dve, 1)
            residual(0)
            sums(0)
            pool.wait_ge(convc_in, 16)
            g.memset(uP[:, :, 0:HIST], 0.0).then_inc(hist_ok, 1)
            for k in range(KT):
                op = g.tensor_copy(uS[:, k, :, 0:HIST], conv_in[:, k])
            op.then_inc(hist_ok, 1)
            modulate(1)
            residual(1)
            g.memset(zs[:], 0.0).then_inc(zs_clear, 1)
            pool.wait_ge(zs_clear, 1)

            def add_products(d, j):
                pool.wait_ge(z_ready, 2 + KT + d - 1)
                g0 = TAPS_POOL * d
                pool.wait_ge(prod_done, g0 + 2)
                s0 = TAPS_POOL * j
                g.tensor_tensor(pacc[:, j], tprod[:, s0 % PRODS], tprod[:, (s0 + 1) % PRODS], ALU.add)\
                    .then_inc(pacc_done, 2)
                for t in range(2, TAPS_POOL):
                    pool.wait_ge(prod_done, g0 + t + 1)
                    pool.wait_ge(pacc_done, PRODS + g0 + t)
                    g.tensor_tensor(pacc[:, j], pacc[:, j], tprod[:, (s0 + t) % PRODS], ALU.add)\
                        .then_inc(pacc_done, 1)

            def add_tile(d):
                pool.wait_ge(z_ready, 2 + KT + d + 1)
                pool.wait_ge(zs_done, KT - 1 + d)
                g.tensor_tensor(zs[:], zs[:], z[:, d, :], ALU.add).then_inc(zs_done, 1)

            for j in range(2):
                add_products(j, j)
            with pool.Fori(1, 4) as i:
                for j in range(2):
                    add_products(2 * i + j, j)
                    add_tile(2 * i + j - 2)
            add_tile(KT - 2)
            for k in range(KT):
                g.tensor_copy(conv_st[:, k, 0:HIST], uP[:, k, SEQ:SEQ + HIST])
                op = g.tensor_copy(conv_st[:, k, HIST:].rearrange("p (b t) -> p b t", b=DB),
                                   uS[:, k, :, DS:DS + HIST])
            op.then_inc(convst_ok, 1)
            sums(2)
            modulate(2)
            residual(2)
            sums(3)
            modulate(3)
            pool.wait_ge(f_mm, 1)
            pool.wait_ge(hl_done, 4 * M_KV + 4)
            modulate(4)
            residual(3)
            sums(4)
            modulate(5)
            residual(4)

            def pair_q(pr, s):
                for hh in range(2):
                    rows = slice(HD * hh, HD * hh + HD)
                    g.tensor_copy(qP[rows, s, hh, :], q32[rows, pr, 0:SEQ]).then_inc(qp_done, 1)
                    pool.wait_ge(qp_done, 2 * pr + hh + 1)

            def block_q(b, s):
                g.tensor_copy(knS[:, s], Kn[:, :, bass.ds(DS * b, DS)]).then_inc(qbd_done, 1)
                pool.wait_ge(qbd_done, 3 * b + 1)
                for hh in range(2):
                    rows = slice(HD * hh, HD * hh + HD)
                    g.tensor_copy(qbd[rows, s, :, DS * hh:DS * hh + DS], q32[rows, :, bass.ds(SEQ + DS * b, DS)])\
                        .then_inc(qbd_done, 1)
                    pool.wait_ge(qbd_done, 3 * b + hh + 2)

            g.memset(qP[:], 0.0).then_inc(init_pool, 1)
            pool.wait_ge(init_pool, 2)
            for s in range(2):
                pool.wait_ge(q_done, s + 1)
                pair_q(s, s)
            pool.wait_ge(q_done, KT)
            pool.wait_ge(kn_in, 16)
            for s in range(2):
                block_q(s, s)
            with pool.Fori(0, 3) as i:
                for s in range(2):
                    pool.wait_ge(s_mm, 4 * i + 2 * s + 2)
                    pair_q(2 * i + 2 + s, s)
            with pool.Fori(0, 3) as i:
                for s in range(2):
                    pool.wait_ge(s_mm, JP + 4 * i + 2 * s + 2)
                    block_q(2 * i + 2 + s, s)
            sums(5)
            modulate(6)
            residual(5)
            sums(6)

        @block.scalar
        def _(act):
            a = nc.scalar

            def refill(n, slot, wait_used=True):
                if wait_used:
                    act.wait_ge(w_used, n - (RING - 1))
                act.wait_ge(w_in[slot], landed(n, slot))
                a.activation(wH[:, slot, :], raw[:, slot, :], ACT.Copy).then_inc(w_hi, 1)

            def landed(n, slot):
                return 4 * n - 4 * slot + 16

            def ada_evac(c, bank=ADB):
                act.wait_ge(a_mm, c + 1)
                a.activation(adaS[:], bank[:, 0:256], ACT.Copy).then_inc(a_ev, 1)

            def ada_mods(c, bank=ADB):
                act.wait_ge(a_tr, c + 1)
                for j in range(2):
                    op = a.activation(mods[:, 2 * c + j, :], bank[:, 256 + 16 * j:256 + 16 * j + NG], ACT.Identity,
                                      bias=pcol("b_ada", 2 * c + j))
                op.then_inc(a_mod, 1)

            def squares(n, following=None):
                a.preload_act_table(ACT.Sqrt)
                for q in range(4):
                    act.wait_ge(zc_done, 4 * n + q + 1)
                    a.activation(sq[:, 2 * q:2 * q + 2, :], z[:, 2 * q:2 * q + 2, :], ACT.Square)\
                        .then_inc(sq_done, 1)
                act.wait_ge(var_ok, n + 1)
                a.activation(sd[:], VAR[:, 0:T], ACT.Sqrt, bias=eps[:, 0:1]).then_inc(sd_done, 1)
                if following is not None:
                    a.preload_act_table(following)

            def split_h(m, mi, src, dst):
                if mi is not None:
                    act.wait_ge(ab_done, mi + 1)
                for q in range(4):
                    if mi is not None:
                        if mi == 0:
                            act.wait_ge(x_in, 16)
                        elif mi != 4:
                            act.wait_ge(zn_done, 4 * MODS[mi][0] + q + 1)
                        if mi != 4:
                            for k in (2 * q, 2 * q + 1):
                                op = a.activation(src[:, k, 0:SEQ], z[:, k, 0:SEQ], ACT.Identity,
                                                  bias=Bm[:, mi % 2, k, 0:1], scale=Am[:, mi % 2, k, 0:1])
                            op.then_inc(hp_done, 1)
                        act.wait_ge(hp_done, 4 * mi + q + 1)
                        act.wait_ge(hs_done, 4 * mi + q + 1)
                    a.activation(dst[:, 2 * q:2 * q + 2, :], src[:, 2 * q:2 * q + 2, :], ACT.Copy)\
                        .then_inc(hh_done, 1)

            def ffn(fi):
                u, (c, na, nd) = FFN_U[fi], FFN_ADA[fi]

                def gate_up(i, with_ada):
                    for j in range(2):
                        f, n = 2 * i + j, u + 4 * i + 2 * j
                        act.wait_ge(w_used, n + 1)
                        act.wait_ge(prod[fi], f + 1)
                        a.activation(sg[:, j, :], bank[2 * j][:, 0:T], ACT.Silu).then_inc(sg_done[fi], 1)
                        refill(n + RING, 2 * j)
                        refill(n + RING + 1, 2 * j + 1)
                        act.wait_ge(prod[fi], f + 3)
                        a.activation(hidH[:, f, :], tmp[:, j, :], ACT.Copy).then_inc(hidh[fi], 1)
                        if with_ada:
                            if j == 0:
                                ada_evac(c + i)
                            else:
                                ada_mods(c + i)

                with act.Fori(0, na) as i:
                    gate_up(i, True)
                if na < 11:
                    with act.Fori(na, 11) as i:
                        gate_up(i, False)
                if nd:
                    with act.Fori(0, 2) as i:
                        for dd in range(4):
                            for j in range(3):
                                refill(u + 48 + 12 * i + 3 * dd + j, (3 * dd + j) % RING)
                                if j == 0:
                                    ada_evac(c + na + 4 * i + dd)
                            ada_mods(c + na + 4 * i + dd)
                else:
                    with act.Fori(0, 5) as i:
                        for j in range(RING):
                            refill(u + 48 + RING * i + j, j)
                squares(FFN_LN[fi], (ACT.Sigmoid, None, None, None)[fi])

            act.wait_ge(c_in, 16)
            a.activation(cact[:], craw[:], ACT.Silu).then_inc(cact_ok, 1)
            act.wait_ge(par_in, 16)
            act.wait_ge(con_in, 16)
            for c in range(FIRST_CHUNKS):
                ada_evac(c, (ADB, MEAN)[c % 2])
                ada_mods(c, (ADB, MEAN)[c % 2])
            for n in range(2):
                refill(n, n, wait_used=False)
            split_h(M_S0, 0, h32, hH)
            for n in range(2, RING):
                refill(n, n, wait_used=False)
            ffn(0)
            split_h(M_S1, 1, h32, hH)
            act.wait_ge(hl_done, 4 * M_S1 + 4)
            with act.Fori(0, 4) as i:
                for j in range(2):
                    d, n = 2 * i + j, U_PW1 + 4 * i + 2 * j
                    act.wait_ge(cv_mm, d + 1)
                    for t in range(TAPS_PE):
                        op = a.activation(diag[:, j, t, :], ident, ACT.Identity, scale=pcol("dw_w", CK * d + t))
                    op.then_inc(diag_done, 1)
                    ada_evac(CH_S1 + d)
                    act.wait_ge(w_used, n + 2)
                    act.wait_ge(u_done, d + 1)
                    a.activation(sg[:, j, :], bank[2 * j + 1][:, 0:T], ACT.Sigmoid,
                                 bias=pcol("pw1_b", KT + d)).then_inc(sig_done, 1)
                    refill(n + RING, 2 * j)
                    refill(n + RING + 1, 2 * j + 1)
                    act.wait_ge(u_done, 2 + d + 1)
                    for t in range(TAPS_POOL):
                        k, slot = TAPS_PE + t, (TAPS_POOL * j + t) % PRODS
                        act.wait_ge(pacc_done, TAPS_POOL * d + t + 1)
                        w = pcol("dw_w", CK * d + k)
                        a.activation(tprod[:, slot, 0:SEQ], uP[:, d, k:k + SEQ], ACT.Identity, scale=w)
                        a.activation(tprod[:, slot, SEQ:T].rearrange("p (b t) -> p b t", b=DB),
                                     uS[:, d, :, k:k + DS], ACT.Identity, scale=w).then_inc(prod_done, 1)
                        if t == PRODS:
                            ada_mods(CH_S1 + d)
            squares(1, ACT.Silu)
            for q in range(4):
                act.wait_ge(zn_done, 4 * 1 + q + 1)
                for k in (2 * q, 2 * q + 1):
                    a.activation(h32[:, k, :], z[:, k, :], ACT.Silu, bias=pcol("cln_b", k),
                                 scale=pcol("cln_g", k)).then_inc(silu_done, 1)
                act.wait_ge(silu_done, 2 * q + 2)
                a.activation(hH[:, 2 * q:2 * q + 2, :], h32[:, 2 * q:2 * q + 2, :], ACT.Copy).then_inc(hh_done, 1)
            with act.Fori(0, 2) as i:
                for j in range(RING):
                    refill(U_PW2 + RING + RING * i + j, j)
            squares(2, ACT.Silu)
            split_h(M_S2, 2, h32, hH)
            act.wait_ge(conv_out, 16)
            ffn(1)
            split_h(M_KV, 3, kv32, kvH)
            act.wait_ge(lf_chain, 1)
            a.activation(lf_e[:], lf_e[:], ACT.Exp, scale=-1.0).then_inc(lfe_done, 1)
            act.wait_ge(lfe_done, 1)
            a.activation(lf_g[:], lf_e[:], ACT.Ln, bias=1.0).then_inc(lfg_done, 1)
            with act.Fori(0, 2) as i:
                for j in range(RING):
                    n = U_K + RING * i + j
                    act.wait_ge(w_used, n + 1)
                    a.activation(kF[:, RING * i + j, :], bank[j][:, 0:T], ACT.Copy).then_inc(kf_done, 1)
                    refill(n + RING, j)
            act.wait_ge(nc_out, 48)
            split_h(M_S3, 4, kv32, hH)
            for half in range(2):
                for j in range(RING):
                    n = U_V + RING * half + j
                    refill(n + RING, j)
                for t in range(3):
                    a.activation(vS[:, t, half * 512:(half + 1) * 512], bank[3 * half + t][:, :], ACT.Copy)\
                        .then_inc(vs_done, 1)
            act.wait_ge(kv_out, 32)
            ffn(2)
            split_h(M_S4, 5, h32, hH)
            act.wait_ge(xa_done, 5 * KT)
            with act.Fori(0, 2) as i:
                for j in range(RING):
                    n = U_Q + RING * i + j
                    act.wait_ge(w_used, n + 1)
                    a.activation(q32[:, RING * i + j, :], bank[j][:, 0:T], ACT.Copy, scale=HD ** -0.5)\
                        .then_inc(q_done, 1)
                    refill(n + RING, j)

            def soft(kind, i, j):
                J, slot = job(kind, i, j), j % 4
                act.wait_ge(nm_done, J + 1)
                if not isinstance(J, int) or J >= 4:
                    act.wait_ge(t_mm, J - 3)
                parts = 2 if kind == "p" else 1
                w = width(kind, j)
                for hh in range(parts):
                    op = a.activation(prS[:, slot, hh * w:hh * w + w], bank[slot][:, hh * w:hh * w + w], ACT.Exp,
                                      bias=nmx[:, slot, hh:hh + 1], accum_out=rsm[:, slot, hh:hh + 1])
                op.then_inc(p_done, 1)

            def evac_t(kind, i, j):
                J, w = job(kind, i, j), 2 * width("p", j) if kind == "p" else 3 * P
                act.wait_ge(t_mm, J + 1)
                a.activation(PT[:, j % 2, 0:w], bank[4 + j % 2][:, 0:w], ACT.Copy).then_inc(pt_done, 1)

            def body(kind, i, with_ada=False, scores=True):
                for j in range(4):
                    if scores:
                        soft(kind, i, j)
                    before = earlier(kind, i, j - 2)
                    if before and (scores or j < 2):
                        evac_t(*before)
                    if with_ada and j == 2:
                        ada_evac(CH_S4 + i)
                    if with_ada and j == 3:
                        ada_mods(CH_S4 + i)

            act.wait_ge(q_done, KT)
            body("p", 0, True)
            with act.Fori(1, 4) as i:
                body("p", i, True)
            body("s", 0)
            with act.Fori(1, 4) as i:
                body("s", i)
            body("s", 4, scores=False)
            act.wait_ge(o_done, JP + JS)
            split_h(M_O, None, z, hH)
            with act.Fori(0, 2) as i:
                for j in range(RING):
                    refill(U_O + RING + RING * i + j, j)
            squares(5, ACT.Silu)
            split_h(M_S5, 6, h32, hH)
            ffn(3)
            for k in range(KT):
                c = 6 * KT + k
                act.wait_ge(zn_done, 4 * 6 + k // 2 + 1)
                op = a.activation(z[:, k, :], z[:, k, :], ACT.Identity, bias=pcol("ln_b", c), scale=pcol("ln_g", c))
                if k % 2:
                    op.then_inc(y_done, 1)

        @block.vector
        def _(dve):
            v = nc.vector
            small = [0]

            def step(op):
                small[0] += 1
                op.then_inc(sm_done, 1)
                dve.wait_ge(sm_done, small[0])

            def refill(n, slot):
                dve.wait_ge(w_hi, n + 1)
                v.tensor_tensor(wL[:, slot, :], raw[:, slot, :], wH[:, slot, :].bitcast(F32), ALU.subtract)\
                    .then_inc(w_lo, 1)

            def normalise(n, meanwhile, h=None):
                dve.wait_ge(mean_ok, n + 1)
                for q in range(4):
                    ks = slice(2 * q, 2 * q + 2)
                    v.tensor_tensor(z[:, ks, :], z[:, ks, :],
                                    MEAN[:, 0:T].unsqueeze(1).to_broadcast([P, 2, T]), ALU.subtract)\
                        .then_inc(zc_done, 1)
                for half in range(2):
                    for q in (2 * half, 2 * half + 1):
                        dve.wait_ge(sq_done, 4 * n + q + 1)
                        v.tensor_tensor(sq[:, 2 * q, :], sq[:, 2 * q, :], sq[:, 2 * q + 1, :], ALU.add)\
                            .then_inc(sp_done, 1)
                    dve.wait_ge(sp_done, 6 * n + 3 * half + 2)
                    v.tensor_tensor(sq[:, 4 * half, :], sq[:, 4 * half, :], sq[:, 4 * half + 2, :], ALU.add)\
                        .then_inc(sp_done, 1)
                for mi in meanwhile:
                    prepare(mi)
                dve.wait_ge(sd_done, n + 1)
                v.reciprocal(rstd[:], sd[:]).then_inc(rs_done, 1)
                dve.wait_ge(rs_done, n + 1)
                for q in range(4):
                    ks = slice(2 * q, 2 * q + 2)
                    v.tensor_tensor(z[:, ks, :], z[:, ks, :],
                                    rstd[:].unsqueeze(1).to_broadcast([P, 2, T]), ALU.mult).then_inc(zn_done, 1)
                if h:
                    rest_h(*h)

            def prepare(mi):
                _, e, vec, _ = MODS[mi]
                dve.wait_ge(a_mod, 4 * (vec + 2))
                shift, scale = mods[:, KT * vec:KT * vec + KT, :], mods[:, KT * vec + KT:KT * vec + 2 * KT, :]
                gg = pcol("ln_g", e * KT, KT).unsqueeze(2).to_broadcast([P, KT, NG])
                bb = pcol("ln_b", e * KT, KT).unsqueeze(2).to_broadcast([P, KT, NG])
                step(v.scalar_tensor_tensor(Am[:, mi % 2], scale, 1.0, gg, ALU.add, ALU.mult))
                step(v.scalar_tensor_tensor(Bm[:, mi % 2], scale, 1.0, bb, ALU.add, ALU.mult))
                v.tensor_tensor(Bm[:, mi % 2], Bm[:, mi % 2], shift, ALU.add).then_inc(ab_done, 1)

            def modulate(mi):
                dve.wait_ge(ab_done, mi + 1)
                for k in range(KT):
                    op = v.tensor_scalar(kv32[:, k, 0:SEQ], z[:, k, 0:SEQ], Am[:, mi % 2, k, 0:1],
                                         Bm[:, mi % 2, k, 0:1], ALU.mult, ALU.add)
                    if k % 2:
                        op.then_inc(hp_done, 1)

            def rest(m, src, hi, lo, q):
                ks = slice(2 * q, 2 * q + 2)
                dve.wait_ge(hh_done, 4 * m + q + 1)
                v.tensor_tensor(lo[:, ks, :], src[:, ks, :], hi[:, ks, :].bitcast(F32), ALU.subtract)\
                    .then_inc(hl_done, 1)

            def rest_h(m, src, hi, lo):
                for q in range(4):
                    rest(m, src, hi, lo, q)

            def gate(r):
                vec = GATE_VEC[r]
                dve.wait_ge(a_mod, 4 * (vec + 1))
                v.tensor_scalar(Gm[:, r % 2], mods[:, KT * vec:KT * vec + KT, :], 1.0,
                                1.0 if r in (1, 4) else 0.5, ALU.add, ALU.mult).then_inc(gm_done, 1)
                dve.wait_ge(gm_done, r + 1)

            def add_residual(r, d, src, par2, bias=None):
                G = Gm[:, r % 2]
                if bias is None:
                    v.scalar_tensor_tensor(z[:, d, 0:SEQ], src[:, 0:SEQ], G[:, d, 0:1], xa[:, d, 0:SEQ],
                                           ALU.mult, ALU.add)
                    v.tensor_tensor(epS[:, par2].rearrange("p (b t) -> p b t", b=DB),
                                    src[:, SEQ:T].rearrange("p (b t) -> p b t", b=DB),
                                    G[:, d, 1:NG].unsqueeze(2).to_broadcast([P, DB, DS]), ALU.mult)\
                        .then_inc(ep1_done, 1)
                else:
                    v.tensor_scalar(z[:, d, 0:SEQ], src[:, 0:SEQ], bias, G[:, d, 0:1], ALU.add, ALU.mult)
                    v.scalar_tensor_tensor(epS[:, par2].rearrange("p (b t) -> p b t", b=DB),
                                           src[:, SEQ:T].rearrange("p (b t) -> p b t", b=DB), bias,
                                           G[:, d, 1:NG].unsqueeze(2).to_broadcast([P, DB, DS]),
                                           ALU.add, ALU.mult).then_inc(ep1_done, 1)
                dve.wait_ge(ep1_done, KT * r + d + 1)
                if bias is not None:
                    v.tensor_tensor(z[:, d, 0:SEQ], z[:, d, 0:SEQ], xa[:, d, 0:SEQ], ALU.add)
                v.tensor_tensor(z[:, d, SEQ:T], epS[:, par2], xa[:, d, SEQ:T], ALU.add).then_inc(z_ready, 1)

            def ffn(fi):
                u, (c, na, nd) = FFN_U[fi], FFN_ADA[fi]
                r, n_ln = FFN_SUB[fi], FFN_LN[fi]
                with dve.Fori(0, 11) as i:
                    for j in range(2):
                        f, n = 2 * i + j, u + 4 * i + 2 * j
                        dve.wait_ge(w_used, n + 2)
                        dve.wait_ge(sg_done[fi], f + 1)
                        v.tensor_tensor(tmp[:, j, :], sg[:, j, :], bank[2 * j + 1][:, 0:T], ALU.mult)\
                            .then_inc(prod[fi], 1)
                        refill(n + RING, 2 * j)
                        refill(n + RING + 1, 2 * j + 1)
                        dve.wait_ge(hidh[fi], f + 1)
                        v.tensor_tensor(hidL[:, f, :], tmp[:, j, :], hidH[:, f, :].bitcast(F32), ALU.subtract)\
                            .then_inc(hidl[fi], 1)
                gate(r)
                dve.wait_ge(xa_done, KT * (r + 1))

                def down(i, dd):
                    n = u + 2 * FT + 12 * i + 3 * dd
                    dve.wait_ge(w_used, n + 3)
                    add_residual(r, 4 * i + dd, bank[4 + dd % 2], dd % 2)

                last = fi == 3
                if not last:
                    with dve.Fori(0, 2) as i:
                        for dd in range(4):
                            for j in range(3):
                                refill(u + 48 + 12 * i + 3 * dd + j, (3 * dd + j) % RING)
                            down(i, dd)
                else:
                    for i in range(2):
                        for dd in range(4):
                            for j in range(3):
                                if 12 * i + 3 * dd + j < 20:
                                    refill(u + 48 + 12 * i + 3 * dd + j, (3 * dd + j) % RING)
                            down(i, dd)
                normalise(n_ln, PREP[r], NEXT_H[r])

            PREP = {0: [1], 2: [3, 4], 3: [5], 5: []}
            NEXT_H = {0: (M_S1, h32, hH, hL), 2: (M_KV, kv32, kvH, kvL), 3: (M_S4, h32, hH, hL), 5: None}

            dve.sem_inc(z_ready, 2)
            dve.sem_inc(u_done, 2)
            for fi in range(4):
                dve.sem_inc(prod[fi], 2)
            dve.wait_ge(par_in, 16)
            v.memset(eps[:], EPS)
            g0, b0 = PAR["ln_g"][0], PAR["ln_b"][0]
            v.tensor_scalar(gA[:], par[:, g0:g0 + 7 * KT], ALPHA, None, ALU.mult)
            v.tensor_scalar(bA[:], par[:, b0:b0 + 7 * KT], ALPHA, None, ALU.mult).then_inc(init_dve, 1)
            prepare(0)
            for n in range(2):
                refill(n, n)
            rest_h(M_S0, h32, hH, hL)
            for n in range(2, RING):
                refill(n, n)
            ffn(0)
            dve.wait_ge(hist_ok, 2)
            dve.sem_inc(cv_mm, 2)
            dve.sem_inc(pacc_done, PRODS)

            def join(d, j):
                dve.wait_ge(cv_mm, 2 + d + 1)
                dve.wait_ge(tapP, TAPS_DVE * (d + 1))
                dve.wait_ge(tapS, TAPS_DVE * (d + 1))
                v.tensor_tensor(z[:, d, :], z[:, d, :], bank[4 + j][:, 0:T], ALU.add).then_inc(fin1_done, 1)
                dve.wait_ge(pacc_done, PRODS + TAPS_POOL * (d + 1))
                dve.wait_ge(fin1_done, d + 1)
                v.tensor_tensor(z[:, d, :], z[:, d, :], pacc[:, j], ALU.add).then_inc(z_ready, 1)

            def conv_body(i):
                for j in range(2):
                    d, n = 2 * i + j, U_PW1 + 4 * i + 2 * j
                    dve.wait_ge(sig_done, d + 1)
                    A = bank[2 * j]
                    v.scalar_tensor_tensor(uP[:, d, HIST:], A[:, 0:SEQ], pcol("pw1_b", d), sg[:, j, 0:SEQ],
                                           ALU.add, ALU.mult)
                    v.scalar_tensor_tensor(uS[:, d, :, HIST:], A[:, SEQ:T].rearrange("p (b t) -> p b t", b=DB),
                                           pcol("pw1_b", d), sg[:, j, SEQ:T].rearrange("p (b t) -> p b t", b=DB),
                                           ALU.add, ALU.mult).then_inc(u_done, 1)
                    refill(n + RING, 2 * j)
                    refill(n + RING + 1, 2 * j + 1)
                    dve.wait_ge(u_done, 2 + d + 1)
                    dve.wait_ge(xa_done, KT + d + 1)
                    zP = z[:, d, 0:SEQ]
                    zS = z[:, d, SEQ:T].rearrange("p (b t) -> p b t", b=DB)
                    for t in range(TAPS_DVE):
                        k = TAPS_PE + TAPS_POOL + t
                        w = pcol("dw_w", CK * d + k)
                        sP, sS = uP[:, d, k:k + SEQ], uS[:, d, :, k:k + DS]
                        if t == 0:
                            v.tensor_scalar(zP, sP, w, pcol("dw_b", d), ALU.mult, ALU.add).then_inc(tapP, 1)
                            v.tensor_scalar(zS, sS, w, pcol("dw_b", d), ALU.mult, ALU.add).then_inc(tapS, 1)
                        else:
                            dve.wait_ge(tapP, TAPS_DVE * d + t)
                            v.scalar_tensor_tensor(zP, sP, w, zP, ALU.mult, ALU.add).then_inc(tapP, 1)
                            dve.wait_ge(tapS, TAPS_DVE * d + t)
                            v.scalar_tensor_tensor(zS, sS, w, zS, ALU.mult, ALU.add).then_inc(tapS, 1)
                    if not isinstance(d, int) or d > 0:
                        join(d - 1, 1 - j)

            conv_body(0)
            with dve.Fori(1, 4) as i:
                conv_body(i)
            join(KT - 1, 1)
            normalise(1, [], (M_PW2, h32, hH, hL))
            gate(1)
            dve.wait_ge(xa_done, 2 * KT)
            with dve.Fori(0, 2) as i:
                for j in range(RING):
                    n = U_PW2 + RING * i + j
                    refill(n + RING, j)
                    dve.wait_ge(w_used, n + 1)
                    add_residual(1, RING * i + j, bank[j], j % 2, bias=pcol("pw2_b", RING * i + j))
            normalise(2, [2], (M_S2, h32, hH, hL))
            ffn(1)
            dve.wait_ge(f_mm, 1)
            step(v.tensor_scalar(lf_l[:], bank[6][0:H, 0:T], par[0:H, PAR["b_f"][0]:PAR["b_f"][0] + 1], None,
                                 ALU.add))
            step(v.tensor_scalar(lf_m[:], lf_l[:], 0.0, None, ALU.min))
            v.scalar_tensor_tensor(lf_e[:], lf_m[:], -2.0, lf_l[:], ALU.mult, ALU.add).then_inc(lf_chain, 1)
            dve.wait_ge(lfg_done, 1)
            step(v.tensor_tensor(lf_n[:], lf_m[:], lf_g[:], ALU.subtract))
            dve.wait_ge(lf_in, 16)
            step(v.tensor_copy(lfS[:, :, PAST:NK], lf_n[:, SEQ:T].rearrange("h (b t) -> h b t", b=DB)))
            one_row = pcol("ln_g", 0)[0:H, :]
            for b in range(DB):
                v.tensor_tensor_scan(lfS[:, b, :], one_row.to_broadcast([H, NK]), lfS[:, b, :], 0.0,
                                     ALU.mult, ALU.subtract).then_inc(ncum_done, 1)
            v.tensor_tensor_scan(lfP[:], one_row.to_broadcast([H, SEQ]), lf_n[:, 0:SEQ], 0.0,
                                 ALU.mult, ALU.subtract).then_inc(ncum_done, 1)
            modulate(4)
            for n in range(U_K + RING, U_V + RING):
                refill(n, n % RING)
            rest_h(M_S3, kv32, hH, hL)
            for n in range(U_V + RING, U_FFN2 + RING):
                refill(n, n % RING)
            ffn(2)
            for n in range(U_Q + RING, U_O + RING):
                refill(n, n % RING)

            def row_max(kind, i, j):
                slot, w = j % 4, width(kind, j)
                dve.wait_ge(s_mm, job(kind, i, j) + 1)
                if kind == "p":
                    v.tensor_reduce(nmx[:, slot, :], bank[slot][:, 0:2 * w].rearrange("p (h w) -> p h w", h=2),
                                    AX.X, ALU.max, negate=True).then_inc(nm_done, 1)
                else:
                    v.tensor_reduce(nmx[:, slot, 0:1], bank[slot][:, 0:w], AX.X, ALU.max, negate=True)\
                        .then_inc(nm_done, 1)

            def norm(kind, i, j):
                J, slot, w = job(kind, i, j), j % 4, width(kind, j)
                n = 2 if kind == "p" else 1
                dve.wait_ge(p_done, J + 1)
                v.reciprocal(rin[:, slot, 0:n], rsm[:, slot, 0:n]).then_inc(ri_done, 1)
                dve.wait_ge(ri_done, J + 1)
                if kind == "p":
                    pr = prS[:, slot, 0:2 * w].rearrange("p (h w) -> p h w", h=2)
                    v.tensor_tensor(pr, pr, rin[:, slot, :].unsqueeze(2).to_broadcast([P, 2, w]), ALU.mult)\
                        .then_inc(pn_done, 1)
                else:
                    v.tensor_scalar(prS[:, slot, 0:w], prS[:, slot, 0:w], rin[:, slot, 0:1], None, ALU.mult)\
                        .then_inc(pn_done, 1)

            def out_prompt(i, j):
                dve.wait_ge(pv_mm, job("p", i, j) + 1)
                v.tensor_copy(z[:, 2 * i + j // 2, P * (j % 2):P * (j % 2) + P], bank[6][:, 0:P]).then_inc(o_done, 1)

            def out_token(i, j):
                dve.wait_ge(pv_mm, job("s", i, j) + 1)
                v.tensor_copy(om[:, j % 2, :], bank[6][:, 0:P]).then_inc(om_done, 1)

            def out_stream(i, j):
                dve.wait_ge(o_mm, 4 * i + j + 1)
                for hh in range(2):
                    rows = slice(HD * hh, HD * hh + HD)
                    src = bank[4 + (j + 1) % 2][rows, 384:512].rearrange("p (k c) -> p k c", k=4)
                    op = v.tensor_copy(z[rows, 4 * (j % 2):4 * (j % 2) + 4, bass.ds(SEQ + DS * (2 * i + j // 2), DS)],
                                       src[:, :, DS * hh:DS * hh + DS])
                op.then_inc(o_done, 1)

            def body(kind, i, scores=True):
                for j in range(4):
                    if scores:
                        row_max(kind, i, j)
                    jn, jv, jo = (earlier(kind, i, j - n) for n in (1, 3, 4))
                    if jn and (scores or j < 1):
                        norm(*jn)
                    if jv and (scores or j < 3):
                        (out_prompt if jv[0] == "p" else out_token)(*jv[1:])
                    if jo and jo[0] == "s":
                        out_stream(*jo[1:])

            dve.wait_ge(xa_done, 5 * KT)
            body("p", 0)
            with dve.Fori(1, 4) as i:
                body("p", i)
            body("s", 0)
            with dve.Fori(1, 4) as i:
                body("s", i)
            body("s", 4, scores=False)
            rest_h(M_O, z, hH, hL)
            gate(4)
            with dve.Fori(0, 2) as i:
                for j in range(RING):
                    n = U_O + RING * i + j
                    refill(n + RING, j)
                    dve.wait_ge(w_used, n + 1)
                    add_residual(4, RING * i + j, bank[j], j % 2)
            normalise(5, [6], (M_S5, h32, hH, hL))
            ffn(3)

        @block.tensor
        def _(pe):
            mm = nc.tensor.matmul

            def tile_w(ring, slot, k):
                return ring[:, slot, k * P:(k + 1) * P]

            def unit(n, slot, out, movH, movL, k0=0, nk=8, start=True, stop=True, ready=None):
                pe.wait_ge(w_lo, n + 1)
                for k in range(nk):
                    if ready is not None and k % 2 == 0:
                        pe.wait_ge(hl_done, 4 * ready + k // 2 + 1)
                    for q, (w, m) in enumerate(((wH, movH), (wH, movL), (wL, movH))):
                        op = mm(out, tile_w(w, slot, k), m[:, k0 + k, :],
                                start=start and k == 0 and q == 0, stop=stop and k == nk - 1 and q == 2)
                op.then_inc(w_used, 1)

            def ada_mm(c, tile, waits, bank=ADB, read=None):
                read = c if read is None else read
                if not isinstance(read, int) or read > 0:
                    pe.wait_ge(a_mod, read)
                for half in range(2):
                    waits(half)
                    for j in range(4):
                        op = mm(bank[32 * j:32 * j + 32, 0:256], cact[:, 4 * half + j, :], tile[:, half, j, :],
                                start=half == 0, stop=half == 1)
                op.then_inc(a_mm, 1)

            def ada_tr(c, bank=ADB):
                pe.wait_ge(a_ev, c + 1)
                for j in range(2):
                    op = mm(bank[:, 256 + 16 * j:256 + 16 * j + NG], adaS[:, P * j:P * j + P],
                            con[:, C_SEL9:C_SEL9 + NG], start=True, stop=True)
                op.then_inc(a_tr, 1)

            def ring_waits(c):
                return lambda half: pe.wait_ge(a_in[half], 16 * (c - FIRST_CHUNKS) + 16)

            def ada(c):
                ada_mm(c, araw, ring_waits(c))
                ada_tr(c)

            def stats(n):
                pe.wait_ge(zs_done, (KT - 1) * (n + 1))
                mm(MEAN[:, 0:T], ones, zs[:], start=True, stop=False)
                pe.wait_ge(z_ready, 2 + KT * (n + 1))
                mm(MEAN[:, 0:T], ones, z[:, KT - 1, :], start=False, stop=True).then_inc(mean_ok, 1)
                for half in range(2):
                    pe.wait_ge(sp_done, 6 * n + 3 * half + 3)
                    op = mm(VAR[:, 0:T], ones, sq[:, 4 * half, :], start=half == 0, stop=half == 1)
                op.then_inc(var_ok, 1)

            def ffn(fi):
                u, (c, na, nd) = FFN_U[fi], FFN_ADA[fi]
                m = FFN_M[fi]

                def gate_up(i, with_ada):
                    for j in range(2):
                        f, n = 2 * i + j, u + 4 * i + 2 * j
                        pe.wait_ge(prod[fi], f + 1)
                        unit(n, 2 * j, bank[2 * j][:, 0:T], hH, hL, ready=m)
                        unit(n + 1, 2 * j + 1, bank[2 * j + 1][:, 0:T], hH, hL)
                        if with_ada:
                            if j == 0:
                                ada_mm(c + i, araw, ring_waits(c + i))
                            else:
                                ada_tr(c + i)

                with pe.Fori(0, na) as i:
                    gate_up(i, True)
                if na < 11:
                    with pe.Fori(na, 11) as i:
                        gate_up(i, False)
                with pe.Fori(0, 2) as i:
                    for dd in range(4):
                        pe.wait_ge(z_ready, KT * FFN_LN[fi] + 4 * i + dd + 1)
                        for j, (k0, nk) in enumerate(DOWN_K):
                            n = u + 2 * FT + 12 * i + 3 * dd + j
                            pe.wait_ge(hidl[fi], k0 + nk)
                            unit(n, (3 * dd + j) % RING, bank[4 + dd % 2][:, 0:T], hidH, hidL, k0, nk,
                                 start=j == 0, stop=j == 2)
                            if nd and j == 0:
                                ada_mm(c + na + 4 * i + dd, araw, ring_waits(c + na + 4 * i + dd))
                        if nd:
                            ada_tr(c + na + 4 * i + dd)
                stats(FFN_LN[fi])

            pe.wait_ge(con_in, 16)
            pe.wait_ge(cact_ok, 1)
            for c in range(FIRST_CHUNKS + 1):
                if c < FIRST_CHUNKS:
                    ada_mm(c, land[:, c], lambda half, c=c: pe.wait_ge(land_in[c], 32), (ADB, MEAN)[c % 2], c - 1)
                if c > 0:
                    ada_tr(c - 1, (ADB, MEAN)[(c - 1) % 2])
            ffn(0)
            def taps(d, j):
                pe.wait_ge(u_done, 2 + d + 1)
                pe.wait_ge(diag_done, d + 1)
                pe.wait_ge(z_ready, 2 + KT + d - 1)
                for t in range(TAPS_PE):
                    first, last = t == 0, t == TAPS_PE - 1
                    mm(bank[4 + j][:, 0:SEQ], diag[:, j, t, :], uP[:, d, t:t + SEQ], start=first, stop=last)
                for t in range(TAPS_PE):
                    first, last = t == 0, t == TAPS_PE - 1
                    op = mm(bank[4 + j][:, SEQ:T].rearrange("p (b t) -> p b t", b=DB), diag[:, j, t, :],
                            uS[:, d, :, t:t + DS], start=first, stop=last)
                op.then_inc(cv_mm, 1)

            def conv_body(i):
                for j in range(2):
                    d, n = 2 * i + j, U_PW1 + 4 * i + 2 * j
                    pe.wait_ge(u_done, d + 1)
                    unit(n, 2 * j, bank[2 * j][:, 0:T], hH, hL, ready=M_S1)
                    ada_mm(CH_S1 + d, araw, ring_waits(CH_S1 + d))
                    unit(n + 1, 2 * j + 1, bank[2 * j + 1][:, 0:T], hH, hL)
                    if not isinstance(d, int) or d > 0:
                        taps(d - 1, 1 - j)
                    ada_tr(CH_S1 + d)

            conv_body(0)
            with pe.Fori(1, 4) as i:
                conv_body(i)
            taps(KT - 1, 1)
            stats(1)
            pe.wait_ge(u_done, 2 + KT)
            with pe.Fori(0, 2) as i:
                for j in range(RING):
                    pe.wait_ge(z_ready, 2 + KT * 2 - 4 + 4 * i + j + 1)
                    unit(U_PW2 + RING * i + j, j, bank[j][:, 0:T], hH, hL, ready=M_PW2)
            stats(2)
            ffn(1)
            pe.wait_ge(wf_in, 16)
            for k in range(KT):
                if k % 2 == 0:
                    pe.wait_ge(hl_done, 4 * M_KV + k // 2 + 1)
                op = mm(bank[6][0:H, 0:T], wf[:, k, :], kv32[:, k, :], start=k == 0, stop=k == KT - 1)
            op.then_inc(f_mm, 1)
            for i in range(2):
                for j in range(RING):
                    if i:
                        pe.wait_ge(kf_done, j + 1)
                    unit(U_K + RING * i + j, j, bank[j][:, 0:T], kvH, kvL, ready=M_KV)
            for half in range(2):
                if half == 0:
                    pe.wait_ge(kf_done, KT)
                for j in range(RING):
                    n = U_V + RING * half + j
                    pe.wait_ge(w_lo, n + 1)
                    for t in range(3):
                        tok = slice(P * t, P * t + P)
                        for kk in range(2):
                            k = 2 * j + kk
                            for q, (h, w) in enumerate(((kvH, wH), (kvH, wL), (kvL, wH))):
                                op = mm(bank[3 * half + t][:, :], h[:, k, tok],
                                        w[:, j, 512 * kk:512 * kk + 512],
                                        start=k == 0 and q == 0, stop=k == KT - 1 and q == 2)
                    op.then_inc(w_used, 1)
            pe.wait_ge(vs_done, 4)
            ffn(2)
            for i in range(2):
                for j in range(RING):
                    if i:
                        pe.wait_ge(q_done, j + 1)
                    unit(U_Q + RING * i + j, j, bank[j][:, 0:T], hH, hL, ready=M_S4)
            pe.wait_ge(q_done, KT)

            def scores(kind, i, j):
                J, S, w = job(kind, i, j), bank[j % 4], width(kind, j)
                s = j // 2
                if kind == "p":
                    if j % 2 == 0:
                        pe.wait_ge(kp_in[s], 32 * i + 32)
                        pe.wait_ge(qp_done, 4 * i + 2 * s + 2)
                    mm(S[:, 0:2 * w], con[0:1, C_ONE:C_ONE + P], ncP[0:1, s, :, 0:w], start=True, stop=False)
                    qt = j % 2
                    for hh in range(2):
                        c0 = hh * w
                        mm(S[:, c0 + w - P:c0 + w], ident, con[:, C_MP:C_MP + P], start=False, stop=False)
                        op = mm(S[:, c0:c0 + w], qP[:, s, hh, P * qt:P * qt + P], KP[:, s, 0:w],
                                start=False, stop=hh == 1)
                else:
                    hf = j % 2
                    if hf == 0:
                        pe.wait_ge(sk_in[s], 32 * i + 32)
                        pe.wait_ge(qbd_done, 6 * i + 3 * s + 3)
                    mm(S[:, 0:NK], con[0:H, C_SELH + P * hf:C_SELH + P * hf + P], ncS[:, s, :],
                       start=True, stop=False)
                    for kk in range(4):
                        mm(S[32 * kk:32 * kk + 32, 0:PAST], qbd[:, s, 4 * hf + kk, :], KTb[:, s, 4 * hf + kk, :],
                           start=False, stop=False)
                    for kk in range(4):
                        mm(S[32 * kk:32 * kk + 32, PAST:NK], qbd[:, s, 4 * hf + kk, :],
                           knS[:, s, 4 * hf + kk, :], start=False, stop=False)
                    op = mm(S[:, PAST:NK], ident, con[:, C_MS:C_MS + DS], start=False, stop=True)
                op.then_inc(s_mm, 1)

            def transposes(kind, i, j):
                J = job(kind, i, j)
                pe.wait_ge(pn_done, J + 1)
                if kind == "s" and (not isinstance(i, int) or J >= JP + 3):
                    pe.wait_ge(o_done, J - 2)
                w = 2 * width("p", j) if kind == "p" else NK
                for c0 in range(0, w, P):
                    n = min(P, w - c0)
                    op = nc.tensor.transpose(bank[4 + j % 2][0:n, c0:c0 + P], prS[:, j % 4, c0:c0 + n], ident)
                op.then_inc(t_mm, 1)

            def values(kind, i, j):
                J = job(kind, i, j)
                pe.wait_ge(pt_done, J + 1)
                if kind == "p" or (isinstance(i, int) and J == JP):
                    if not isinstance(i, int) or J > 0:
                        pe.wait_ge(o_done, J)
                else:
                    pe.wait_ge(om_done, J - JP)
                s = j // 2
                if kind == "p":
                    qt = j % 2
                    if qt == 0:
                        pe.wait_ge(vp_in[s], 16 * i + 16)
                    for hh in range(2):
                        rows = slice(HD * hh, HD * hh + HD)
                        for t in range(1 + qt):
                            c0 = (hh * (1 + qt) + t) * P
                            op = mm(bank[6][rows, 0:P], VP[:, s, t, rows], PT[:, j % 2, c0:c0 + P],
                                    start=t == 0, stop=t == qt)
                else:
                    hf = j % 2
                    if hf == 0:
                        pe.wait_ge(sv_in[s], 32 * i + 32)
                    for t in range(3):
                        rr = P if t < 2 else DS
                        for kk in range(4):
                            pair = slice(P * (4 * hf + kk), P * (4 * hf + kk) + P)
                            V = Vb[:, s, t, pair] if t < 2 else Vn[:, s, pair]
                            c0 = t * P + 32 * kk
                            op = mm(bank[6][32 * kk:32 * kk + 32, 0:P], PT[0:rr, j % 2, c0:c0 + 32], V,
                                    start=t == 0, stop=t == 2)
                op.then_inc(pv_mm, 1)

            def turn(kind, i, j):
                pe.wait_ge(om_done, 4 * i + j + 1)
                nc.tensor.transpose(bank[4 + (j + 1) % 2][:, 384:512], om[:, j % 2, :], ident).then_inc(o_mm, 1)

            def body(kind, i, with_ada=False, new=True):
                for j in range(4):
                    if new:
                        scores(kind, i, j)
                    jt, jv, jo = (earlier(kind, i, j - n) for n in (2, 3, 4))
                    if jt and (new or j < 2):
                        transposes(*jt)
                    if jv and (new or j < 3):
                        values(*jv)
                    if jo and jo[0] == "s":
                        turn(*jo)
                    if with_ada and j == 2:
                        ada_mm(CH_S4 + i, araw, ring_waits(CH_S4 + i))
                    if with_ada and j == 3:
                        ada_tr(CH_S4 + i)

            body("p", 0, True)
            with pe.Fori(1, 4) as i:
                body("p", i, True)
            body("s", 0)
            with pe.Fori(1, 4) as i:
                body("s", i)
            body("s", 4, new=False)
            for i in range(2):
                for j in range(RING):
                    if i:
                        pe.wait_ge(z_ready, 2 + KT * 5 + j + 1)
                    unit(U_O + RING * i + j, j, bank[j][:, 0:T], hH, hL, ready=M_O)
            stats(5)
            ffn(3)


def _tiles(w):
    k, n = w.shape[0] // P, w.shape[1] // P
    return w.reshape(k, P, n, P).transpose(2, 1, 0, 3)


def _cols(a):
    return np.ascontiguousarray(a.reshape(-1, P).T)


def _weight_stream(i):
    W = np.zeros((N_UNITS, P, UNIT), np.float32)

    def ffn(u, l, j):
        gu = W[u:u + 2 * FT].reshape(FT, 2, P, KT, P)
        gu[:, 0] = _tiles(i["ffn_w_gate"][l, j])
        gu[:, 1] = _tiles(i["ffn_w_up"][l, j])
        down = _tiles(i["ffn_w_down"][l, j])
        for q, (k0, nk) in enumerate(DOWN_K):
            W[u + 2 * FT + q:u + FFN_UNITS:3, :, 0:nk * P] = down[:, :, k0:k0 + nk].reshape(KT, P, nk * P)

    def square(u, w):
        W[u:u + KT] = _tiles(w).reshape(KT, P, UNIT)

    ffn(U_FFN0, 0, 0)
    pw1 = _tiles(i["pw1_w"][0]).reshape(2, KT, P, UNIT)
    W[U_PW1:U_PW2:2], W[U_PW1 + 1:U_PW2:2] = pw1[0], pw1[1]
    square(U_PW2, i["pw2_w"][0])
    ffn(U_FFN1, 0, 1)
    square(U_K, i["w_k"])
    W[U_V:U_V + KT] = i["w_v"].reshape(4, 2, P, 2, 512).transpose(3, 0, 2, 1, 4).reshape(KT, P, UNIT)
    ffn(U_FFN2, 1, 0)
    square(U_Q, i["w_q"][0])
    square(U_O, i["w_o"][0])
    ffn(U_FFN3, 1, 1)
    return W


def _constants():
    con = np.zeros((P, N_CONST), np.float32)
    r = np.arange(P)
    con[:, C_ID:C_ID + P] = np.eye(P)
    con[:, C_ONES:C_ONES + P] = 1.0 / D
    for g in range(NG):
        con[32 * np.arange(4) + g, C_SEL9 + g] = 1.0
    con[:, C_ONE:C_ONE + P] = 1.0
    for hf in range(2):
        con[8 * hf + r // DS, C_SELH + P * hf + r] = 1.0
    con[:, C_MP:C_MP + P] = np.where(r[None, :] <= r[:, None], 0.0, NEG)
    con[:, C_MS:C_MS + DS] = np.where(np.arange(DS)[None, :] <= (r % DS)[:, None], 0.0, NEG)
    return con


def kernel(**inputs):
    import concourse.bacc as bacc
    from concourse.bass_utils import run_bass_kernel_spmd as run

    i = {k: np.asarray(v) for k, v in inputs.items()}
    par = np.zeros((P, N_PAR), np.float32)

    def put(name, a):
        a0, n = PAR[name]
        par[:, a0:a0 + n] = a

    one = np.ones((P, KT), np.float32)
    put("ln_g", np.concatenate([one, _cols(i["ln_g"])], 1))
    put("ln_b", np.concatenate([0 * one, _cols(i["ln_b"])], 1))
    put("cln_g", _cols(i["conv_ln_g"]))
    put("cln_b", _cols(i["conv_ln_b"]))
    put("b_ada", np.concatenate([_cols(i["b_ada"][0]), _cols(i["b_ada_kv"]), _cols(i["b_ada"][1])], 1))
    put("pw1_b", _cols(i["pw1_b"]))
    put("pw2_b", _cols(i["pw2_b"]))
    put("dw_b", _cols(i["dw_b"]))
    put("dw_w", i["dw_w"][0].reshape(CK, KT, P).transpose(2, 1, 0).reshape(P, KT * CK))
    par[0:H, PAR["b_f"][0]] = i["b_f"]

    ada = np.concatenate([i["w_ada"][0], i["w_ada_kv"], i["w_ada"][1]], 1)
    ada = ada.reshape(2, 4, P, CHUNKS, 256).transpose(3, 0, 2, 1, 4).reshape(2 * CHUNKS, P, 4, 256)
    x = np.concatenate([i["x_prompt"].reshape(SEQ, D), i["x_sample"].reshape(DB * DS, D)], 0)
    c = np.zeros((32, D), np.float32)
    c[0:1], c[1:NG] = i["c_prompt"], i["c_sample"]

    def fm(a):
        return np.ascontiguousarray(a.reshape(-1, KT, P).transpose(2, 1, 0))

    arrays = {
        "W": _weight_stream(i), "ADA": np.ascontiguousarray(ada), "par_d": par, "con_d": _constants(),
        "x_d": fm(x), "c_d": fm(c),
        "conv_d": fm(i["cache_conv"][0].reshape(DB * HIST, D)).reshape(P, KT, DB, HIST),
        "kt_d": np.ascontiguousarray(
            i["cache_k"].reshape(DB, PAST, KT, P).transpose(0, 3, 2, 1)),
        "v_d": i["cache_v"].reshape(DB, PAST, D),
        "lf_d": np.ascontiguousarray(i["cache_logf"].transpose(2, 0, 1)),
        "wf_d": np.ascontiguousarray(i["w_f"].reshape(KT, P, H).transpose(1, 0, 2)),
    }
    outs = {"y_o": (P, KT, T), "kT_o": (P, KT, T), "v_o": (T, D), "lf_o": (H, T), "conv_o": (P, KT, HIST * NG)}
    nc = bacc.Bacc("TRN2", target_bir_lowering=False, num_devices=1)
    args = [nc.dram_tensor(n, a.shape, F32, kind="ExternalInput").ap() for n, a in arrays.items()]
    args += [nc.dram_tensor(n, s, F32, kind="ExternalOutput").ap() for n, s in outs.items()]
    args.append(nc.dram_tensor("ncp_d", (H, SEQ), F32, kind="Internal").ap())
    args.append(nc.dram_tensor("ncs_d", (H, DB, NK), F32, kind="Internal").ap())
    build_program(nc, *args)
    r = run(nc, [arrays], core_ids=[0]).results[0]

    def rows(a):
        return np.asarray(a).transpose(2, 1, 0).reshape(-1, D)

    y, k, v, lf, cv = rows(r["y_o"]), rows(r["kT_o"]), r["v_o"], r["lf_o"].T, rows(r["conv_o"])
    return (y[:SEQ].reshape(1, SEQ, D), y[SEQ:].reshape(DB, DS, D),
            cv[:HIST].reshape(1, 1, HIST, D),
            k[:SEQ].reshape(1, SEQ, H, HD), v[:SEQ].reshape(1, SEQ, H, HD), lf[:SEQ].reshape(1, SEQ, H),
            cv[HIST:].reshape(1, DB, HIST, D),
            k[SEQ:].reshape(DB, DS, H, HD), v[SEQ:].reshape(DB, DS, H, HD), lf[SEQ:].reshape(DB, DS, H))
```
